# Optimizing a Trainium2 kernel written in Bass

```python
import math
import jax, jax.numpy as jnp
from jax import lax
import numpy as np

D_MODEL = 1024
BATCH = 1
SEQ = 256
DEPTH = 2

PLE_DIM = 256
MIX_WIDTH = D_MODEL
HEAD_DIM = 64
LRU_WIDTH = D_MODEL // 4
LRU_HEADS = LRU_WIDTH // HEAD_DIM
LRU_BLOCK = LRU_WIDTH // LRU_HEADS
LRU_C = 8.0
CONV_K = 4
ATT_WIDTH = D_MODEL // 4
ATT_HEADS = ATT_WIDTH // HEAD_DIM
ATT_BLOCK = 128
SSD_WIDTH = D_MODEL // 2
SSD_HEADS = SSD_WIDTH // HEAD_DIM
SSD_GROUPS = 2
SSD_HEADS_PER_GROUP = SSD_HEADS // SSD_GROUPS
SSD_STATE = 128
SSD_CHUNK = 128
SSD_CONV_DIM = SSD_WIDTH + 2 * SSD_GROUPS * SSD_STATE
FFN_DIM = 128 * ((8 * D_MODEL // 3 + 127) // 128)
ALPHA = (2.0 * DEPTH) ** 0.25
BETA = (8.0 * DEPTH) ** -0.25
LN_EPS = 1e-5
RMS_EPS = 1e-5
IN_SIZES = (LRU_WIDTH, LRU_WIDTH,
            ATT_WIDTH, ATT_WIDTH, ATT_WIDTH,
            ATT_HEADS,
            SSD_WIDTH, SSD_CONV_DIM, SSD_HEADS)
IN_WIDTH = sum(IN_SIZES)

kernel_name = "hymba_style_lru_fox_ssd_macaron_deepnorm"

def _split_points(sizes):
    pts, acc = [], 0
    for s in sizes[:-1]:
        acc += s
        pts.append(acc)
    return pts

def layer_norm(x, g, b):
    xf = x.astype(jnp.float32)
    mu = jnp.mean(xf, axis=-1, keepdims=True)
    var = jnp.mean(jnp.square(xf - mu), axis=-1, keepdims=True)
    y = (xf - mu) * lax.rsqrt(var + LN_EPS) * g.astype(jnp.float32) + b.astype(jnp.float32)
    return y.astype(x.dtype)

def swiglu(x, wg, wu, wd):
    return (jax.nn.silu(x @ wg) * (x @ wu)) @ wd

def causal_dwconv(u, w, b):
    c = u.shape[-1]
    y = lax.conv_general_dilated(u, w[:, None, :].astype(u.dtype), window_strides=(1,),
                                 padding=[(CONV_K - 1, 0)],
                                 dimension_numbers=("NWC", "WIO", "NWC"),
                                 feature_group_count=c)
    return y + b

def _lin_combine(e1, e2):
    a1, b1 = e1
    a2, b2 = e2
    return a1 * a2, a2 * b1 + b2

def rglru_block(u_raw, gate_raw, conv_w, conv_b, wa, ba, wx, bx, lam):
    bsz, s, _ = u_raw.shape
    u = causal_dwconv(u_raw, conv_w, conv_b)
    ub = u.reshape(bsz, s, LRU_HEADS, LRU_BLOCK)
    r = jax.nn.sigmoid(jnp.einsum("bshi,hij->bshj", ub, wa).reshape(bsz, s, LRU_WIDTH) + ba)
    ig = jax.nn.sigmoid(jnp.einsum("bshi,hij->bshj", ub, wx).reshape(bsz, s, LRU_WIDTH) + bx)
    log_a = -LRU_C * r.astype(jnp.float32) * jax.nn.softplus(-lam.astype(jnp.float32))
    a = jnp.exp(log_a)
    b = jnp.sqrt(-jnp.expm1(2.0 * log_a)) * (ig * u).astype(jnp.float32)
    _, h = lax.associative_scan(_lin_combine, (a, b), axis=1)
    return (h * jax.nn.gelu(gate_raw.astype(jnp.float32))).astype(u_raw.dtype)

def forgetting_attention(q, k, v, f_logit, b_f):
    bsz, s, _ = q.shape
    nblk = s // ATT_BLOCK
    log_f = jax.nn.log_sigmoid((f_logit + b_f).astype(jnp.float32))
    F = jnp.cumsum(log_f, axis=1).transpose(0, 2, 1)
    qh = q.astype(jnp.float32).reshape(bsz, s, ATT_HEADS, HEAD_DIM).transpose(0, 2, 1, 3) * (HEAD_DIM ** -0.5)
    kh = k.astype(jnp.float32).reshape(bsz, s, ATT_HEADS, HEAD_DIM).transpose(0, 2, 1, 3)
    vh = v.astype(jnp.float32).reshape(bsz, s, ATT_HEADS, HEAD_DIM).transpose(0, 2, 1, 3)
    q_blocks = qh.reshape(bsz, ATT_HEADS, nblk, ATT_BLOCK, HEAD_DIM).transpose(2, 0, 1, 3, 4)
    f_blocks = F.reshape(bsz, ATT_HEADS, nblk, ATT_BLOCK).transpose(2, 0, 1, 3)
    key_pos = jnp.arange(s)

    def one_block(args):
        qb, fb, bi = args
        logits = jnp.einsum("bhqd,bhkd->bhqk", qb, kh) + fb[..., :, None] - F[:, :, None, :]
        q_pos = bi * ATT_BLOCK + jnp.arange(ATT_BLOCK)
        logits = jnp.where(key_pos[None, :] <= q_pos[:, None], logits, -jnp.inf)
        w = jax.nn.softmax(logits, axis=-1)
        return jnp.einsum("bhqk,bhkd->bhqd", w, vh)

    out = lax.map(one_block, (q_blocks, f_blocks, jnp.arange(nblk)))
    out = out.transpose(1, 0, 3, 2, 4).reshape(bsz, s, ATT_WIDTH)
    return out.astype(q.dtype)

def segsum(x):
    t = x.shape[-1]
    xc = jnp.cumsum(x, axis=-1)
    seg = xc[..., :, None] - xc[..., None, :]
    mask = jnp.tril(jnp.ones((t, t), dtype=bool))
    return jnp.where(mask, seg, -jnp.inf)

def ssd_chunked(xs, a, bm, cm):
    bsz, s, h, p = xs.shape
    n = bm.shape[-1]
    c = s // SSD_CHUNK
    xs = xs.reshape(bsz, c, SSD_CHUNK, h, p)
    bm = bm.reshape(bsz, c, SSD_CHUNK, h, n)
    cm = cm.reshape(bsz, c, SSD_CHUNK, h, n)
    a = a.reshape(bsz, c, SSD_CHUNK, h).transpose(0, 3, 1, 2)
    a_cum = jnp.cumsum(a, axis=-1)
    L = jnp.exp(segsum(a))
    y_diag = jnp.einsum("bclhn,bcshn,bhcls,bcshp->bclhp", cm, bm, L, xs)
    decay_states = jnp.exp(a_cum[..., -1:] - a_cum)
    states = jnp.einsum("bclhn,bhcl,bclhp->bchpn", bm, decay_states, xs)
    states = jnp.concatenate([jnp.zeros_like(states[:, :1]), states], axis=1)
    decay_chunk = jnp.exp(segsum(jnp.pad(a_cum[..., -1], ((0, 0), (0, 0), (1, 0)))))
    states = jnp.einsum("bhzc,bchpn->bzhpn", decay_chunk, states)[:, :-1]
    y_off = jnp.einsum("bclhn,bchpn,bhcl->bclhp", cm, states, jnp.exp(a_cum))
    return (y_diag + y_off).reshape(bsz, s, h, p)

def ssd_mixer(z, xbc_raw, dt_raw, conv_w, conv_b, dt_bias, a_log, d_skip, norm_g):
    bsz, s, _ = z.shape
    xbc = jax.nn.silu(causal_dwconv(xbc_raw, conv_w, conv_b)).astype(jnp.float32)
    xs, bm, cm = jnp.split(xbc, [SSD_WIDTH, SSD_WIDTH + SSD_GROUPS * SSD_STATE], axis=-1)
    dt = jax.nn.softplus((dt_raw + dt_bias).astype(jnp.float32))
    A = -jnp.exp(a_log.astype(jnp.float32))
    xs_h = xs.reshape(bsz, s, SSD_HEADS, HEAD_DIM)
    bm_h = jnp.repeat(bm.reshape(bsz, s, SSD_GROUPS, SSD_STATE), SSD_HEADS_PER_GROUP, axis=2)
    cm_h = jnp.repeat(cm.reshape(bsz, s, SSD_GROUPS, SSD_STATE), SSD_HEADS_PER_GROUP, axis=2)
    y = ssd_chunked(xs_h * dt[..., None], A * dt, bm_h, cm_h)
    y = y + d_skip.astype(jnp.float32)[:, None] * xs_h
    y = y.reshape(bsz, s, SSD_WIDTH) * jax.nn.silu(z.astype(jnp.float32))
    yg = y.reshape(bsz, s, SSD_GROUPS, SSD_WIDTH // SSD_GROUPS)
    yg = yg * lax.rsqrt(jnp.mean(jnp.square(yg), axis=-1, keepdims=True) + RMS_EPS)
    y = yg.reshape(bsz, s, SSD_WIDTH) * norm_g.astype(jnp.float32)
    return y.astype(z.dtype)

def setup_inputs(seed: int = 0) -> dict:
    key = jax.random.key(seed)
    ks = iter(jax.random.split(key, 33))
    f32 = jnp.float32

    def nrm(shape, scale):
        return scale * jax.random.normal(next(ks), shape, f32)

    def gain(shape):
        return 1.0 + nrm(shape, 0.02)

    d = DEPTH
    out = {}
    out["x"] = nrm((BATCH, SEQ, D_MODEL), 1.0)
    out["p"] = nrm((DEPTH, BATCH, SEQ, PLE_DIM), 1.0)
    out["ln1_g"] = gain((d, D_MODEL))
    out["ln1_b"] = nrm((d, D_MODEL), 0.02)
    out["ffn1_wg"] = nrm((d, D_MODEL, FFN_DIM), BETA * D_MODEL ** -0.5)
    out["ffn1_wu"] = nrm((d, D_MODEL, FFN_DIM), BETA * D_MODEL ** -0.5)
    out["ffn1_wd"] = nrm((d, FFN_DIM, D_MODEL), BETA * FFN_DIM ** -0.5)
    out["w_in"] = nrm((d, D_MODEL, IN_WIDTH), D_MODEL ** -0.5)
    out["lru_conv_w"] = nrm((d, CONV_K, LRU_WIDTH), CONV_K ** -0.5)
    out["lru_conv_b"] = nrm((d, LRU_WIDTH), 0.02)
    out["lru_wa"] = nrm((d, LRU_HEADS, LRU_BLOCK, LRU_BLOCK), LRU_BLOCK ** -0.5)
    out["lru_ba"] = nrm((d, LRU_WIDTH), 0.02)
    out["lru_wx"] = nrm((d, LRU_HEADS, LRU_BLOCK, LRU_BLOCK), LRU_BLOCK ** -0.5)
    out["lru_bx"] = nrm((d, LRU_WIDTH), 0.02)
    a_c = jax.random.uniform(next(ks), (d, LRU_WIDTH), f32, 0.9, 0.999)
    a0 = a_c ** (1.0 / LRU_C)
    out["lru_lambda"] = jnp.log(a0) - jnp.log1p(-a0)
    out["fox_bf"] = 3.0 + nrm((d, ATT_HEADS), 0.1)
    out["ssd_conv_w"] = nrm((d, CONV_K, SSD_CONV_DIM), CONV_K ** -0.5)
    out["ssd_conv_b"] = nrm((d, SSD_CONV_DIM), 0.02)
    dt0 = jnp.exp(jax.random.uniform(next(ks), (d, SSD_HEADS), f32, math.log(1e-3), math.log(1e-1)))
    out["ssd_dt_bias"] = dt0 + jnp.log(-jnp.expm1(-dt0))
    out["ssd_a_log"] = jnp.log(jax.random.uniform(next(ks), (d, SSD_HEADS), f32, 1.0, 16.0))
    out["ssd_d"] = gain((d, SSD_HEADS))
    out["ssd_norm_g"] = gain((d, SSD_WIDTH))
    out["w_out"] = nrm((d, MIX_WIDTH, D_MODEL), BETA * MIX_WIDTH ** -0.5)
    out["ln2_g"] = gain((d, D_MODEL))
    out["ln2_b"] = nrm((d, D_MODEL), 0.02)
    out["ffn2_wg"] = nrm((d, D_MODEL, FFN_DIM), BETA * D_MODEL ** -0.5)
    out["ffn2_wu"] = nrm((d, D_MODEL, FFN_DIM), BETA * D_MODEL ** -0.5)
    out["ffn2_wd"] = nrm((d, FFN_DIM, D_MODEL), BETA * FFN_DIM ** -0.5)
    out["ln3_g"] = gain((d, D_MODEL))
    out["ln3_b"] = nrm((d, D_MODEL), 0.02)
    out["pe_proj"] = nrm((d, PLE_DIM, D_MODEL), BETA * PLE_DIM ** -0.5)
    out["pe_gate_w"] = nrm((d, D_MODEL, D_MODEL), D_MODEL ** -0.5)
    out["pe_gate_b"] = nrm((d, D_MODEL), 0.02)
    return out

def reference(x, p, ln1_g, ln1_b, ffn1_wg, ffn1_wu, ffn1_wd, w_in,
              lru_conv_w, lru_conv_b, lru_wa, lru_ba, lru_wx, lru_bx, lru_lambda,
              fox_bf, ssd_conv_w, ssd_conv_b, ssd_dt_bias, ssd_a_log, ssd_d, ssd_norm_g,
              w_out, ln2_g, ln2_b, ffn2_wg, ffn2_wu, ffn2_wd, ln3_g, ln3_b,
              pe_proj, pe_gate_w, pe_gate_b):
    pts = _split_points(IN_SIZES)
    for i in range(DEPTH):
        x = layer_norm(ALPHA * x + 0.5 * swiglu(x, ffn1_wg[i], ffn1_wu[i], ffn1_wd[i]), ln1_g[i], ln1_b[i])
        h = x @ w_in[i]
        u_lru, g_lru, q, k, v, f_logit, z, xbc, dt_raw = jnp.split(h, pts, axis=-1)
        y_a = rglru_block(u_lru, g_lru, lru_conv_w[i], lru_conv_b[i], lru_wa[i], lru_ba[i],
                          lru_wx[i], lru_bx[i], lru_lambda[i])
        y_b = forgetting_attention(q, k, v, f_logit, fox_bf[i])
        y_c = ssd_mixer(z, xbc, dt_raw, ssd_conv_w[i], ssd_conv_b[i], ssd_dt_bias[i],
                        ssd_a_log[i], ssd_d[i], ssd_norm_g[i])
        mix = jnp.concatenate([y_a, y_b, y_c], axis=-1) @ w_out[i]
        x = layer_norm(ALPHA * x + mix, ln2_g[i], ln2_b[i])
        x = layer_norm(ALPHA * x + 0.5 * swiglu(x, ffn2_wg[i], ffn2_wu[i], ffn2_wd[i]), ln3_g[i], ln3_b[i])
        x = x + jax.nn.sigmoid(x @ pe_gate_w[i] + pe_gate_b[i]) * (p[i] @ pe_proj[i])
    return x


_drawn_inputs = setup_inputs


def setup_inputs(seed=0):
    import zlib

    import numpy as np

    out = dict(_drawn_inputs(seed))
    spreads = {}
    factors = {'lru_conv_b': 39.016,
     'lru_ba': 200.0,
     'lru_bx': 200.0,
     'fox_bf': 64.0,
     'ssd_conv_b': 6.24,
     'ssd_d': 21.661,
     'ssd_norm_g': 8.0,
     'pe_gate_b': 8.0,
     'lru_wa': 32.152,
     'lru_lambda': 28.12,
     'lru_conv_w': 8.0,
     'lru_wx': 8.0}
    for name, (base, spread) in spreads.items():
        noise = np.random.default_rng([zlib.crc32(name.encode()), seed]).standard_normal(out[name].shape)
        drawn = base * np.exp(spread * noise) if base else spread * noise
        out[name] = __import__('jax').numpy.asarray(drawn.astype(out[name].dtype))
    for name, factor in factors.items():
        out[name] = (out[name] * factor).astype(out[name].dtype)
    return out
```

```python
import concourse.bass as bass
from concourse import mybir
from contextlib import ExitStack

P = 128
DEPTH, SEQ, D = 2, 256, 1024
TT = SEQ // P
KT = D // P
F = 2816
FC = 256
CHUNKS = F // FC
HD = 64
AH, SH = 4, 8
NG = 2
ROWS = AH + SH
PLE = 256
ALPHA = (2.0 * DEPTH) ** 0.25
EPS = 1e-5
BIG = 1e30

W = 2048
SLOTS = 3
FFN_UNITS = 3 * CHUNKS
U_FFN1 = 0
U_XS, U_B, U_C = FFN_UNITS, FFN_UNITS + 2, FFN_UNITS + 3
U_Q, U_K, U_V = FFN_UNITS + 4, FFN_UNITS + 5, FFN_UNITS + 6
U_Z, U_U, U_G = FFN_UNITS + 7, FFN_UNITS + 9, FFN_UNITS + 10
U_OUT = FFN_UNITS + 11
U_FFN2 = U_OUT + 4
U_GATE = U_FFN2 + FFN_UNITS
U_PE = U_GATE + 4
UNITS = U_PE + 1
SLOT_UNITS = [(UNITS - s + SLOTS - 1) // SLOTS for s in range(SLOTS)]
assert U_FFN1 % SLOTS == 0 and U_FFN2 % SLOTS == 0 and FFN_UNITS % SLOTS == 0 and UNITS % SLOTS == 2

E_CW, E_CB = 0, 32
E_UW, E_UB = 40, 48
E_BA, E_BX, E_LAM = 50, 52, 54
E_BIAS, E_SIGN, E_ALOG = 56, 57, 58
E_WA, E_WX = 60, 316
E_SPLIT = 572
E_FD = E_SPLIT
E_PT = E_FD + KT * ROWS
E_ALL = E_PT + (PLE // P) * SEQ
NSPLIT = E_ALL - E_SPLIT

C_ID, C_SSD, C_ATT, C_SEL, C_RESET = 0, 128, 640, 768, 768 + ROWS * P
C_ALL = C_RESET + SEQ

DVE_STEPS, ACT_STEPS = 79, 2


def free_count(n):
    return {0: 2, 1: 3, 2: 1}.get(n, n + 1) if isinstance(n, int) else n + 1


def trunk(nc, w_stream, extras, norms, mix_rows, consts, x_in_dram, out):
    f32, f32r = mybir.dt.float32, mybir.dt.float32r
    ALU, ACT, AX = mybir.AluOpType, mybir.ActivationFunctionType, mybir.AxisListType

    with ExitStack() as ctx:
        def sb(name, shape, dt=f32):
            return ctx.enter_context(nc.sbuf_tensor(name, shape, dt))

        def sem(name):
            return ctx.enter_context(nc.semaphore(name))

        w_raw = sb("w_raw", [P, SLOTS, W])
        w_hi = sb("w_hi", [P, SLOTS, W], f32r)
        w_lo = sb("w_lo", [P, SLOTS, W], f32r)
        xt_hi = sb("xt_hi", [P, TT, KT, P], f32r)
        xt_lo = sb("xt_lo", [P, TT, KT, P], f32r)
        x_tok = sb("x_tok", [P, TT, D])
        gain = sb("gain", [P, 2, D])
        mix = sb("mix", [P, 520])
        ex = sb("ex", [P, E_ALL])
        ex_hi = sb("ex_hi", [P, NSPLIT], f32r)
        ex_lo = sb("ex_lo", [P, NSPLIT], f32r)
        cst = sb("cst", [P, C_ALL])
        id_r = sb("id_r", [P, P], f32r)
        ssd_mask = sb("ssd_mask", [P, 512], f32r)
        att_mask = sb("att_mask", [P, P], f32r)
        big = sb("big", [P, 8, 260])
        xbc = sb("xbc", [P, 8, SEQ])
        u_raw = sb("u_raw", [P, 2, 260])
        uc = sb("uc", [P, 2, SEQ])
        gate_g = sb("gate_g", [P, 2, SEQ])
        qt = sb("qt", [P, 2, SEQ])
        kt_ = sb("kt_", [P, 2, SEQ])
        v_tok = sb("v_tok", [P, TT, 256])
        z_tok = sb("z_tok", [P, TT, 512])
        sp = sb("sp", [P, 6, 258])
        cum = sb("cum", [ROWS, 2, SEQ])
        expa = sb("expa", [ROWS, 1])
        c8 = sb("c8", [P, 2, 2])
        cum_tok = sb("cum_tok", [P, TT, 2, ROWS])
        ncum_tok = sb("ncum_tok", [P, TT, ROWS])
        ecum = sb("ecum", [P, SH])
        lru = sb("lru", [P, 4, 2, SEQ])
        xdt = sb("xdt", [P, TT, SH, HD])
        xdd = sb("xdd", [P, SH, HD])
        b_tok = sb("b_tok", [P, NG, P])
        cb = sb("cb", [P, NG, TT, P])
        state = sb("state", [P, SH * HD])
        y_tok = sb("y_tok", [P, TT, 512])
        probs = sb("probs", [P, AH, 384])
        nmax = sb("nmax", [P, 2, AH])
        rsum = sb("rsum", [P, 2, AH])
        stats = sb("stats", [P, TT, 2, 6])
        mv = sb("mv", [P, TT, 2])
        rstd = sb("rstd", [P, TT])
        warm = sb("warm", [P, 2])
        spare = sb("spare", [P, 2])
        msq = sb("msq", [P, TT * NG])
        silu_g = sb("silu_g", [P, TT, FC])
        h_tok = sb("h_tok", [P, TT, FC])
        ht_hi = sb("ht_hi", [P, 2, TT, P], f32r)
        ht_lo = sb("ht_lo", [P, 2, TT, P], f32r)
        ps = ctx.enter_context(nc.psum_tensor("ps", [P, 8, 512], f32))

        ident = cst[:, C_ID:C_ID + P]
        decay = big[:, :, :].rearrange("p a b -> p (a b)")[:, 0:SH * TT * P].rearrange(
            "p (h c l) -> p h c l", h=SH, c=TT)
        sig = big[:, :, :].rearrange("p a b -> p (a b)")[:, 0:TT * D].rearrange("p (t d) -> p t d", t=TT)
        probs_t = xbc[:, 0:6, :].rearrange("p a b -> p (a b)").rearrange("p (h k) -> p h k", h=AH)
        y_off = xdd
        GU, HT = 4, 6

        x_loaded, cst_loaded = sem("x_loaded"), sem("cst_loaded")
        raw_in = [sem(f"raw_in{s}") for s in range(SLOTS)]
        hi_ready, lo_ready = sem("hi_ready"), sem("lo_ready")
        unit_done = sem("unit_done")
        ex_in, gain_in, mix_in = sem("ex_in"), sem("gain_in"), sem("mix_in")
        gain_used, mix_used = sem("gain_used"), sem("mix_used")
        exhi_ready, exlo_ready = sem("exhi_ready"), sem("exlo_ready")
        masks_ready, pads_ready = sem("masks_ready"), sem("pads_ready")
        x_ready = sem("x_ready")
        xt_turned, xthi_ready, xt_ready = sem("xt_turned"), sem("xthi_ready"), sem("xt_ready")
        gu_half, silu_ready, h_ready = sem("gu_half"), sem("silu_ready"), sem("h_ready")
        ht_turned, hthi_ready, ht_ready = sem("ht_turned"), sem("hthi_ready"), sem("ht_ready")
        acc_half = sem("acc_half")
        fd_done, abs_ready, exp_ready, cum_ready, ncum_ready = (sem(n) for n in (
            "fd_done", "abs_ready", "exp_ready", "cum_ready", "ncum_ready"))
        conv_first, conv_ready, xbc_ready = sem("conv_first"), sem("conv_ready"), sem("xbc_ready")
        evac = sem("evac")
        cum_turned, cumtok_ready = sem("cum_turned"), sem("cumtok_ready")
        xs_turned, b_turned, cb_done, bcb_ready = sem("xs_turned"), sem("b_turned"), sem("cb_done"), sem("bcb_ready")
        gates_done, gates_ready, aa_ready = sem("gates_done"), sem("gates_ready"), sem("aa_ready")
        one_a2_ready, root_ready, ya_ready, yahi_ready, yalo_ready = (sem(n) for n in (
            "one_a2_ready", "root_ready", "ya_ready", "yahi_ready", "yalo_ready"))
        bc_done, decay_ready = sem("bc_done"), sem("decay_ready")
        xs_used, xdd_ready, m_ready = sem("xs_used"), sem("xdd_ready"), sem("m_ready")
        logits_done, nmax_ready, probs_raw, probs_ready = (sem(n) for n in (
            "logits_done", "nmax_ready", "probs_raw", "probs_ready"))
        ydiag_done, state_done, state_ready, yoff_done = (sem(n) for n in (
            "ydiag_done", "state_done", "state_ready", "yoff_done"))
        probs_turned, probst_ready, pv_done, ybhi_ready, yblo_ready = (sem(n) for n in (
            "probs_turned", "probst_ready", "pv_done", "ybhi_ready", "yblo_ready"))
        yz_ready, msq_ready, yn_ready, yc_turned, ychi_ready, yclo_ready = (sem(n) for n in (
            "yz_ready", "msq_ready", "yn_ready", "yc_turned", "ychi_ready", "yclo_ready"))
        var_ready, std_ready, ms_ready, rms_ready = sem("var_ready"), sem("std_ready"), sem("ms_ready"), sem("rms_ready")
        biased_ready, sig_ready = sem("biased_ready"), sem("sig_ready")
        dve_step, act_step, stored = sem("dve_step"), sem("act_step"), sem("stored")

        block = ctx.enter_context(nc.Block())

        @block.sync
        def _(sp_):
            def load(layer, n, slot):
                sp_.wait_ge(lo_ready, layer * UNITS + free_count(n))
                sp_.dma_start(w_raw[:, slot, :], w_stream[layer, n]).then_inc(raw_in[slot], 16)

            sp_.dma_start(x_tok[:, :, :], x_in_dram).then_inc(x_loaded, 16)
            with sp_.Fori(0, DEPTH) as layer:
                for n in range(SLOTS):
                    load(layer, n, n)
                with sp_.Fori(1, UNITS // SLOTS) as g:
                    for s in range(SLOTS):
                        load(layer, g * SLOTS + s, s)
                for n in range(UNITS // SLOTS * SLOTS, UNITS):
                    load(layer, n, n % SLOTS)
            sp_.wait_ge(x_ready, 8 * DEPTH + 2)
            sp_.dma_start(out, x_tok[:, :, :]).then_inc(stored, 16)
            sp_.wait_ge(stored, 16)

        @block.gpsimd
        def _(pool):
            pool.dma_start(cst[:, :], consts).then_inc(cst_loaded, 16)
            with pool.Fori(0, DEPTH) as layer:
                pool.wait_ge(x_ready, layer * 8 + 2)
                pool.dma_start(ex[:, :], extras[layer]).then_inc(ex_in, 16)
                pool.dma_start(mix[:, :], mix_rows[layer].partition_broadcast(P)).then_inc(mix_in, 16)
                for i in range(4):
                    pool.wait_ge(gain_used, layer * 4 + i + 1)
                    pool.dma_start(gain[:, :, :], norms[layer, i].partition_broadcast(P)).then_inc(gain_in, 16)

        @block.tensor
        def _(pe):
            mm = nc.tensor.matmul

            def unit_ready(layer, n):
                pe.wait_ge(lo_ready, layer * UNITS + n + 1 + SLOTS)

            def three(out_, a_hi, a_lo, b_hi, b_lo, start, stop):
                mm(out_, a_hi, b_hi, start=start, stop=False)
                mm(out_, a_hi, b_lo, start=False, stop=False)
                return mm(out_, a_lo, b_hi, start=False, stop=stop)

            def turn_x(layer, j, bank):
                for t in range(TT):
                    pe.wait_ge(x_ready, (layer * 4 + j) * 2 + t + 1)
                    for k in range(KT):
                        last = nc.tensor.transpose(ps[:, bank + 2 * t + k // 4, k % 4 * P:(k % 4 + 1) * P],
                                                   x_tok[:, t, k * P:(k + 1) * P], ident)
                    last.then_inc(xt_turned, 1)

            def token_unit(layer, n, slot, half, banks, signal=None):
                unit_ready(layer, n)
                hi = w_hi[:, slot, :].rearrange("p (k c) -> p k c", k=4)
                lo = w_lo[:, slot, :].rearrange("p (k c) -> p k c", k=4)
                for t in range(TT):
                    for k in range(4):
                        kt = 4 * half + k
                        last = three(ps[:, banks[t], :], xt_hi[:, t, kt, :], xt_lo[:, t, kt, :], hi[:, k], lo[:, k],
                                     kt == 0, kt == KT - 1)
                    if signal is not None and t == 0:
                        last.then_inc(signal, 1)
                last.then_inc(unit_done, 1)

            def row_unit(layer, n, slot, lhs, bank, first, last_unit):
                unit_ready(layer, n)
                hi = w_hi[:, slot, :].rearrange("p (k h c) -> p k h c", k=2, h=2)
                lo = w_lo[:, slot, :].rearrange("p (k h c) -> p k h c", k=2, h=2)
                for t in range(TT):
                    for k in range(2):
                        a_hi, a_lo = lhs(k, t)
                        start, stop = first and k == 0, last_unit and k == 1
                        for h in range(2):
                            mm(ps[:, bank + 2 * t + h, :], a_hi, hi[:, k, h], start=start, stop=False)
                        for h in range(2):
                            mm(ps[:, bank + 2 * t + h, :], a_hi, lo[:, k, h], start=False, stop=False)
                        for h in range(2):
                            last = mm(ps[:, bank + 2 * t + h, :], a_lo, hi[:, k, h], start=False, stop=stop)
                    if last_unit and t == 0:
                        last.then_inc(acc_half, 1)
                last.then_inc(unit_done, 1)

            def channel_unit(layer, n, bank):
                unit_ready(layer, n)
                hi = w_hi[:, n % SLOTS, :].rearrange("p (k c) -> p k c", k=KT)
                lo = w_lo[:, n % SLOTS, :].rearrange("p (k c) -> p k c", k=KT)
                for m in range(2):
                    for k in range(KT):
                        c = slice(m * P, (m + 1) * P)
                        last = three(ps[:, bank, m * SEQ:(m + 1) * SEQ], hi[:, k, c], lo[:, k, c],
                                     xt_hi[:, :, k, :], xt_lo[:, :, k, :], k == 0, k == KT - 1)
                last.then_inc(unit_done, 1)

            def turn_h(chunk):
                pe.wait_ge(h_ready, chunk * 2 + 2)
                for k in range(2):
                    for t in range(TT):
                        last = nc.tensor.transpose(ps[:, HT, (k * TT + t) * P:(k * TT + t + 1) * P],
                                                   h_tok[:, t, k * P:(k + 1) * P], ident)
                last.then_inc(ht_turned, 1)

            def ht(k, t):
                return ht_hi[:, k, t, :], ht_lo[:, k, t, :]

            def ffn(layer, f, base):
                chunk0 = (layer * 2 + f) * CHUNKS
                token_unit(layer, base, 0, 0, (GU, GU + 1))
                token_unit(layer, base + 1, 1, 1, (GU, GU + 1), gu_half)
                turn_h(chunk0)
                for c in range(1, 2):
                    token_unit(layer, base + 2, 2, 0, (GU, GU + 1))
                    token_unit(layer, base + 3, 0, 1, (GU, GU + 1), gu_half)
                    pe.wait_ge(ht_ready, chunk0 + 1)
                    row_unit(layer, base + 4, 1, ht, 0, True, False)
                    turn_h(chunk0 + 1)
                with pe.Fori(2, CHUNKS) as c:
                    token_unit(layer, c * 3 + (base - 1), 2, 0, (GU, GU + 1))
                    token_unit(layer, c * 3 + base, 0, 1, (GU, GU + 1), gu_half)
                    pe.wait_ge(ht_ready, chunk0 + c)
                    row_unit(layer, c * 3 + (base + 1), 1, ht, 0, False, False)
                    turn_h(chunk0 + c)
                pe.wait_ge(ht_ready, chunk0 + CHUNKS)
                row_unit(layer, base + FFN_UNITS - 1, 2, ht, 0, False, True)

            def xt_whole(layer, j):
                pe.wait_ge(xt_ready, (layer * 4 + j) * 2 + 2)

            def xt(kt0):
                return lambda k, t: (xt_hi[:, t, kt0 + k, :], xt_lo[:, t, kt0 + k, :])

            pe.wait_ge(cst_loaded, 16)
            with pe.Fori(0, DEPTH) as layer:
                turn_x(layer, 0, 0)
                xt_whole(layer, 0)
                ffn(layer, 0, U_FFN1)
                turn_x(layer, 1, 0)
                xt_whole(layer, 1)

                pe.wait_ge(exlo_ready, layer + 1)
                for k in range(KT):
                    c = slice(k * ROWS, (k + 1) * ROWS)
                    last = three(ps[0:ROWS, 0, 0:SEQ], ex_hi[:, c], ex_lo[:, c], xt_hi[:, :, k, :], xt_lo[:, :, k, :],
                                 k == 0, k == KT - 1)
                last.then_inc(fd_done, 1)
                channel_unit(layer, U_XS, 1)
                channel_unit(layer, U_XS + 1, 2)
                channel_unit(layer, U_B, 3)
                channel_unit(layer, U_C, 4)
                channel_unit(layer, U_Q, 5)
                channel_unit(layer, U_K, 6)
                unit_ready(layer, U_V)
                vh = w_hi[:, U_V % SLOTS, :].rearrange("p (k c) -> p k c", k=KT)
                vl = w_lo[:, U_V % SLOTS, :].rearrange("p (k c) -> p k c", k=KT)
                for t in range(TT):
                    for k in range(KT):
                        last = three(ps[:, 7, t * 256:(t + 1) * 256], xt_hi[:, t, k, :], xt_lo[:, t, k, :],
                                     vh[:, k], vl[:, k], k == 0, k == KT - 1)
                last.then_inc(unit_done, 1)
                pe.wait_ge(conv_first, layer * 5 + 2)
                pe.wait_ge(conv_first, layer * 5 + 3)
                token_unit(layer, U_Z, U_Z % SLOTS, 0, (2, 3))
                token_unit(layer, U_Z + 1, (U_Z + 1) % SLOTS, 1, (2, 3))
                pe.wait_ge(abs_ready, layer + 1)
                channel_unit(layer, U_U, 0)
                channel_unit(layer, U_G, 1)

                pe.wait_ge(evac, layer * 5 + 4)
                pe.wait_ge(cum_ready, layer + 1)
                pe.wait_ge(xbc_ready, layer * 4 + 4)
                for g in range(NG):
                    for c in range(TT):
                        s = slice(c * P, (c + 1) * P)
                        last = mm(ps[:, 7, (g * TT + c) * P:(g * TT + c + 1) * P], xbc[:, 4 + g, s], xbc[:, 6 + g, s],
                                  start=True, stop=True)
                last.then_inc(cb_done, 1)
                for t in range(TT):
                    for i, rows in enumerate((cum[:, 0, :], sp[0:ROWS, 5, 0:SEQ])):
                        c = (t * 2 + i) * ROWS
                        last = nc.tensor.transpose(ps[:, 2, c:c + ROWS], rows[:, t * P:(t + 1) * P],
                                                   cst[0:ROWS, C_ID:C_ID + ROWS])
                last.then_inc(cum_turned, 1)
                for g in range(NG):
                    last = nc.tensor.transpose(ps[:, 6, g * P:(g + 1) * P], xbc[:, 4 + g, 0:P], ident)
                last.then_inc(b_turned, 1)
                for t in range(TT):
                    for m in range(4):
                        last = nc.tensor.transpose(ps[:, 4 + t, m * P:(m + 1) * P], xbc[:, m, t * P:(t + 1) * P], ident)
                last.then_inc(xs_turned, 1)
                pe.wait_ge(conv_ready, layer * 5 + 5)
                pe.wait_ge(evac, layer * 5 + 5)
                for i, w in enumerate((E_WA, E_WX)):
                    for m in range(2):
                        last = mm(ps[:, i, m * SEQ:(m + 1) * SEQ], ex[:, w + m * P:w + (m + 1) * P], uc[:, m, :],
                                  start=True, stop=True)
                last.then_inc(gates_done, 1)
                pe.wait_ge(ncum_ready, layer + 1)
                pe.wait_ge(bcb_ready, layer * 2 + 2)
                pe.wait_ge(xs_used, layer + 1)
                for h in range(AH):
                    rows = slice(h % 2 * HD, h % 2 * HD + HD)
                    sel = cst[0:ROWS, C_SEL + h * P:C_SEL + (h + 1) * P]
                    for q, k, col in ((0, 0, 0), (1, 0, P), (1, 1, 2 * P)):
                        o = ps[:, 4 + h, col:col + P]
                        mm(o, qt[rows, h // 2, q * P:(q + 1) * P], kt_[rows, h // 2, k * P:(k + 1) * P],
                           start=True, stop=False)
                        mm(o, cum[:, 0, q * P:(q + 1) * P], sel, start=False, stop=False)
                        last = mm(o, sel, cum[:, 1, k * P:(k + 1) * P], start=False, stop=q != k)
                        if q == k:
                            last = mm(o, id_r[:, :], att_mask[:, :], start=False, stop=True)
                last.then_inc(logits_done, 1)
                pe.wait_ge(gates_ready, layer + 1)
                pe.wait_ge(cumtok_ready, layer + 1)
                for b in range(SH // 2):
                    for i in range(2):
                        h = AH + 2 * b + i
                        mm(ps[:, b, i * SEQ:(i + 1) * SEQ], cst[0:ROWS, C_SEL + h * P:C_SEL + (h + 1) * P], cum[:, 0, :],
                           start=i == 0, stop=False, skip_group_check=True)
                    last = mm(ps[:, b, :], id_r[:, :], ssd_mask[:, :], start=False, stop=True, skip_group_check=True)
                last.then_inc(bc_done, 1)
                pe.wait_ge(xdd_ready, layer + 1)
                for g in range(NG):
                    last = mm(ps[:, 2, g * 256:(g + 1) * 256], b_tok[:, g, :],
                              xdd[:, 4 * g:4 * g + 4, :].rearrange("p h d -> p (h d)"), start=True, stop=True)
                last.then_inc(state_done, 1)
                pe.wait_ge(m_ready, layer * 4 + 4)
                for c in range(TT):
                    for h in range(SH):
                        last = mm(ps[:, c, h * HD:(h + 1) * HD], decay[:, h, c, :], xdt[:, c, h, :],
                                  start=True, stop=True)
                last.then_inc(ydiag_done, 1)
                pe.wait_ge(state_ready, layer + 1)
                for g in range(NG):
                    last = mm(ps[:, 3, g * 256:(g + 1) * 256], xbc[:, 6 + g, P:2 * P], state[:, g * 256:(g + 1) * 256],
                              start=True, stop=True)
                last.then_inc(yoff_done, 1)
                pe.wait_ge(probs_ready, layer + 1)
                for h in range(AH):
                    for i in range(3):
                        last = nc.tensor.transpose(ps[:, 4 + h, i * P:(i + 1) * P], probs[:, h, i * P:(i + 1) * P], ident)
                last.then_inc(probs_turned, 1)
                pe.wait_ge(probst_ready, layer + 1)
                for h in range(AH):
                    rows = slice(h % 2 * HD, h % 2 * HD + HD)
                    v = [v_tok[:, t, h * HD:(h + 1) * HD] for t in range(TT)]
                    o = ps[rows, 2, h // 2 * SEQ:(h // 2 + 1) * SEQ]
                    mm(o[:, 0:P], v[0], probs_t[:, h, 0:P], start=True, stop=True)
                    mm(o[:, P:SEQ], v[0], probs_t[:, h, P:2 * P], start=True, stop=False)
                    last = mm(o[:, P:SEQ], v[1], probs_t[:, h, 2 * P:3 * P], start=False, stop=True)
                last.then_inc(pv_done, 1)
                pe.wait_ge(yalo_ready, layer + 1)
                row_unit(layer, U_OUT, U_OUT % SLOTS, xt(0), 4, True, False)
                pe.wait_ge(yblo_ready, layer + 1)
                row_unit(layer, U_OUT + 1, (U_OUT + 1) % SLOTS, xt(2), 4, False, False)
                for t in range(TT):
                    pe.wait_ge(yn_ready, layer * 2 + t + 1)
                    for m in range(4):
                        last = nc.tensor.transpose(ps[:, t, m * P:(m + 1) * P], y_tok[:, t, m * P:(m + 1) * P], ident)
                    last.then_inc(yc_turned, 1)
                pe.wait_ge(yclo_ready, layer * 2 + 2)
                row_unit(layer, U_OUT + 2, (U_OUT + 2) % SLOTS, xt(4), 4, False, False)
                row_unit(layer, U_OUT + 3, (U_OUT + 3) % SLOTS, xt(6), 4, False, True)

                turn_x(layer, 2, 4)
                xt_whole(layer, 2)
                ffn(layer, 1, U_FFN2)
                turn_x(layer, 3, 0)
                xt_whole(layer, 3)
                for i in range(4):
                    row_unit(layer, U_GATE + i, (U_GATE + i) % SLOTS, xt(2 * i), 0, i == 0, i == 3)
                row_unit(layer, U_PE, U_PE % SLOTS,
                         lambda k, t: tuple(e[:, E_PT - E_SPLIT + k * SEQ + t * P:E_PT - E_SPLIT + k * SEQ + (t + 1) * P]
                                            for e in (ex_hi, ex_lo)), 4, True, True)

        @block.scalar
        def _(act):
            fn = nc.scalar.activation

            def make_hi(layer, n, slot, nth):
                act.wait_ge(raw_in[slot], (layer * SLOT_UNITS[slot] + nth + 1) * 16)
                act.wait_ge(unit_done, layer * UNITS + free_count(n))
                fn(w_hi[:, slot, :], w_raw[:, slot, :], ACT.Copy).then_inc(hi_ready, 1)

            def hi_of(layer, n):
                make_hi(layer, n, n % SLOTS, n // SLOTS)

            def roots(layer, i):
                fn(warm[:, 0:1], warm[:, 1:2], ACT.Sqrt)
                for t in range(TT):
                    act.wait_ge(var_ready, (layer * 3 + i) * 2 + t + 1)
                    fn(rstd[:, t:t + 1], rstd[:, t:t + 1], ACT.Sqrt).then_inc(std_ready, 1)

            def xt_hi_of(layer, j, bank):
                for t in range(TT):
                    act.wait_ge(xt_turned, (layer * 4 + j) * 2 + t + 1)
                    fn(xt_hi[:, t, :, :].rearrange("p k c -> p (k c)"),
                       ps[:, bank + 2 * t:bank + 2 * t + 2, :].rearrange("p b c -> p (b c)"),
                       ACT.Copy).then_inc(xthi_ready, 1)

            def silu(chunk, done_first, done_second):
                act.wait_ge(gu_half, done_first)
                fn(silu_g[:, 0, :], ps[:, GU, 0:FC], ACT.Silu).then_inc(silu_ready, 1)
                act.wait_ge(unit_done, done_second)
                fn(silu_g[:, 1, :], ps[:, GU + 1, 0:FC], ACT.Silu).then_inc(silu_ready, 1)

            def ht_hi_of(chunk):
                act.wait_ge(ht_turned, chunk + 1)
                fn(ht_hi[:, :, :, :].rearrange("p k t c -> p (k t c)"), ps[:, HT, :], ACT.Copy).then_inc(hthi_ready, 1)

            def ffn(layer, f, base):
                chunk0 = (layer * 2 + f) * CHUNKS
                hi_of(layer, base + 3)
                silu(chunk0, chunk0 + 1, layer * UNITS + base + 2 + SLOTS)
                hi_of(layer, base + 4)
                ht_hi_of(chunk0)
                with act.Fori(1, CHUNKS) as c:
                    make_hi(layer, c * 3 + (base + 2), 2, c + base // 3)
                    silu(chunk0 + c, chunk0 + c + 1, layer * UNITS + c * 3 + base + 1 + SLOTS)
                    make_hi(layer, c * 3 + (base + 3), 0, c + (base // 3 + 1))
                    ht_hi_of(chunk0 + c)
                    make_hi(layer, c * 3 + (base + 4), 1, c + (base // 3 + 1))
                hi_of(layer, base + 3 * CHUNKS + 2)

            act.wait_ge(pads_ready, 3)
            with act.Fori(0, DEPTH) as layer:
                for n in range(SLOTS):
                    hi_of(layer, n)
                xt_hi_of(layer, 0, 0)
                act.wait_ge(ex_in, layer * 16 + 16)
                fn(ex_hi[:, :], ex[:, E_SPLIT:E_ALL], ACT.Copy).then_inc(exhi_ready, 1)
                ffn(layer, 0, U_FFN1)
                roots(layer, 0)
                xt_hi_of(layer, 1, 0)

                def done(n):
                    act.wait_ge(unit_done, layer * UNITS + n + 1 + SLOTS)

                act.wait_ge(abs_ready, layer + 1)
                fn(sp[:, 1, :], sp[:, 1, :], ACT.Exp, scale=-1.0).then_inc(act_step, 1)
                act.wait_ge(act_step, layer * ACT_STEPS + 1)
                fn(expa[:, :], ex[0:ROWS, E_ALOG:E_ALOG + 1], ACT.Exp).then_inc(exp_ready, 1)

                def conv_in(i, bank):
                    fn(big[:, 2 * i:2 * i + 2, 3:3 + SEQ], ps[:, bank, :].rearrange("p (m s) -> p m s", m=2),
                       ACT.Copy)
                    for m in range(2 * i, 2 * i + 2):
                        last = fn(xbc[:, m, :], ps[:, bank, m % 2 * SEQ:(m % 2 + 1) * SEQ], ACT.Identity,
                                  bias=ex[:, E_CB + m:E_CB + m + 1], scale=ex[:, E_CW + 24 + m:E_CW + 25 + m])
                    last.then_inc(conv_first, 1)

                def conv_out(i):
                    act.wait_ge(conv_ready, layer * 5 + i + 1)
                    fn(xbc[:, 2 * i:2 * i + 2, :], xbc[:, 2 * i:2 * i + 2, :], ACT.Silu).then_inc(xbc_ready, 1)

                done(U_XS)
                conv_in(0, 1)
                hi_of(layer, U_XS + 3)
                done(U_XS + 1)
                conv_in(1, 2)
                act.wait_ge(cum_ready, layer + 1)
                fn(cum[:, 1, :], cum[:, 0, :], ACT.Copy, scale=-1.0).then_inc(ncum_ready, 1)
                hi_of(layer, U_XS + 4)
                conv_out(0)
                done(U_B)
                conv_in(2, 3)
                hi_of(layer, U_B + 3)
                conv_out(1)
                done(U_C)
                conv_in(3, 4)
                hi_of(layer, U_C + 3)
                conv_out(2)
                done(U_Q)
                fn(qt[:, :, :].rearrange("p a b -> p (a b)"), ps[:, 5, :], ACT.Copy, scale=HD ** -0.5).then_inc(evac, 1)
                hi_of(layer, U_Q + 3)
                conv_out(3)
                done(U_K)
                fn(kt_[:, :, :].rearrange("p a b -> p (a b)"), ps[:, 6, :], ACT.Copy).then_inc(evac, 1)
                hi_of(layer, U_K + 3)
                done(U_V)
                fn(v_tok[:, :, :].rearrange("p a b -> p (a b)"), ps[:, 7, :], ACT.Copy).then_inc(evac, 1)
                hi_of(layer, U_V + 3)
                done(U_Z)
                hi_of(layer, U_Z + 3)
                done(U_Z + 1)
                fn(z_tok[:, :, :], ps[:, 2:4, :], ACT.Silu).then_inc(evac, 1)
                hi_of(layer, U_Z + 4)
                done(U_U)
                fn(u_raw[:, :, 3:3 + SEQ], ps[:, 0, :].rearrange("p (m s) -> p m s", m=2), ACT.Copy)
                for m in range(2):
                    last = fn(uc[:, m, :], ps[:, 0, m * SEQ:(m + 1) * SEQ], ACT.Identity,
                              bias=ex[:, E_UB + m:E_UB + m + 1], scale=ex[:, E_UW + 6 + m:E_UW + 7 + m])
                last.then_inc(conv_first, 1)
                hi_of(layer, U_U + 3)
                act.wait_ge(cum_turned, layer + 1)
                fn(cum_tok[:, :, :, :].rearrange("p a b c -> p (a b c)"), ps[:, 2, 0:TT * 2 * ROWS], ACT.Copy)
                fn(ncum_tok[:, :, :], ps[:, 2, 0:TT * 2 * ROWS].rearrange("p (a b c) -> p a b c", a=TT, b=2)[:, :, 0, :],
                   ACT.Copy, scale=-1.0).then_inc(act_step, 1)
                done(U_G)
                fn(gate_g[:, :, :].rearrange("p a b -> p (a b)"), ps[:, 1, :], ACT.Gelu_apprx_tanh).then_inc(evac, 1)
                hi_of(layer, U_G + 3)
                fn(ecum[:, :], ps[:, 2, 2 * ROWS + AH:3 * ROWS], ACT.Exp).then_inc(cumtok_ready, 1)
                act.wait_ge(cb_done, layer + 1)
                fn(cb[:, :, :, :].rearrange("p a b c -> p (a b c)"), ps[:, 7, :], ACT.Copy).then_inc(bcb_ready, 1)
                act.wait_ge(b_turned, layer + 1)
                fn(b_tok[:, :, :].rearrange("p a b -> p (a b)"), ps[:, 6, 0:256], ACT.Copy).then_inc(bcb_ready, 1)
                act.wait_ge(gates_done, layer + 1)
                for i, b in enumerate((E_BA, E_BX)):
                    for m in range(2):
                        last = fn(lru[:, i, m, :], ps[:, i, m * SEQ:(m + 1) * SEQ], ACT.Sigmoid,
                                  bias=ex[:, b + m:b + m + 1])
                last.then_inc(gates_ready, 1)
                act.wait_ge(bc_done, layer + 1)
                act.wait_ge(act_step, layer * ACT_STEPS + 2)
                for h in range(SH):
                    for c in range(TT):
                        fn(decay[:, h, c, :], ps[:, h // 2, (h % 2 * TT + c) * P:(h % 2 * TT + c + 1) * P], ACT.Exp,
                           bias=ncum_tok[:, c, AH + h:AH + h + 1]).then_inc(decay_ready, 1)
                act.wait_ge(gates_ready, layer + 1)
                for m in range(2):
                    fn(lru[:, 2, m, :], lru[:, 0, m, :], ACT.Exp, scale=c8[:, 0, m:m + 1])
                for m in range(2):
                    last = fn(lru[:, 3, m, :], lru[:, 0, m, :], ACT.Tanh, scale=c8[:, 1, m:m + 1])
                last.then_inc(aa_ready, 1)
                act.wait_ge(nmax_ready, layer + 1)
                for h in range(AH):
                    fn(probs[:, h, 0:P], ps[:, 4 + h, 0:P], ACT.Exp, bias=nmax[:, 0, h:h + 1],
                       accum_out=rsum[:, 0, h:h + 1])
                    last = fn(probs[:, h, P:3 * P], ps[:, 4 + h, P:3 * P], ACT.Exp, bias=nmax[:, 1, h:h + 1],
                              accum_out=rsum[:, 1, h:h + 1])
                last.then_inc(probs_raw, 1)
                act.wait_ge(state_done, layer + 1)
                fn(state[:, :], ps[:, 2, :], ACT.Copy).then_inc(state_ready, 1)
                act.wait_ge(one_a2_ready, layer + 1)
                fn(lru[:, 3, :, :], lru[:, 3, :, :], ACT.Sqrt).then_inc(root_ready, 1)

                def split_hi(kt0, n, src, signal):
                    return fn(xt_hi[:, :, kt0:kt0 + n, :], src, ACT.Copy).then_inc(signal, 1)

                act.wait_ge(probs_turned, layer + 1)
                fn(probs_t, ps[:, 4:8, 0:3 * P], ACT.Copy).then_inc(probst_ready, 1)
                act.wait_ge(ya_ready, layer + 1)
                split_hi(0, 2, lru[:, 1, :, :].rearrange("p m (t c) -> p t m c", t=TT), yahi_ready)
                act.wait_ge(pv_done, layer + 1)
                split_hi(2, 2, ps[:, 2, :].rearrange("p (m t c) -> p t m c", m=2, t=TT), ybhi_ready)
                act.wait_ge(yz_ready, layer + 1)
                for t in range(TT):
                    for g in range(NG):
                        i = t * NG + g
                        last = fn(big[:, 0, 0:256], y_tok[:, t, g * 256:(g + 1) * 256], ACT.Square,
                                  accum_out=msq[:, i:i + 1])
                        last.then_inc(msq_ready, 1)
                        act.wait_ge(msq_ready, layer * 4 + i + 1)
                act.wait_ge(ms_ready, layer + 1)
                fn(msq[:, :], msq[:, :], ACT.Sqrt).then_inc(rms_ready, 1)
                for t in range(TT):
                    act.wait_ge(yc_turned, layer * 2 + t + 1)
                    fn(xt_hi[:, t, 4:8, :].rearrange("p k c -> p (k c)"), ps[:, t, :], ACT.Copy).then_inc(ychi_ready, 1)
                for n in range(U_OUT, U_OUT + 4):
                    hi_of(layer, n + 3)
                roots(layer, 1)
                xt_hi_of(layer, 2, 4)
                ffn(layer, 1, U_FFN2)
                roots(layer, 2)
                xt_hi_of(layer, 3, 0)
                for n in range(U_GATE, U_GATE + 2):
                    hi_of(layer, n + 3)
                for t in range(TT):
                    act.wait_ge(biased_ready, layer * 2 + t + 1)
                    fn(sig[:, t, :], sig[:, t, :], ACT.Sigmoid).then_inc(sig_ready, 1)

        @block.vector
        def _(dve):
            v = nc.vector

            def make_lo(layer, n, slot):
                dve.wait_ge(hi_ready, layer * UNITS + n + 1)
                v.tensor_tensor(w_lo[:, slot, :], w_raw[:, slot, :], w_hi[:, slot, :].bitcast(f32),
                                ALU.subtract).then_inc(lo_ready, 1)

            def lo_of(layer, n):
                make_lo(layer, n, n % SLOTS)

            def xt_lo_of(layer, j, bank):
                for t in range(TT):
                    dve.wait_ge(xthi_ready, (layer * 4 + j) * 2 + t + 1)
                    v.tensor_tensor(xt_lo[:, t, :, :].rearrange("p k c -> p (k c)"),
                                    ps[:, bank + 2 * t:bank + 2 * t + 2, :].rearrange("p b c -> p (b c)"),
                                    xt_hi[:, t, :, :].rearrange("p k c -> p (k c)").bitcast(f32),
                                    ALU.subtract).then_inc(xt_ready, 1)

            def hidden(chunk):
                for t in range(TT):
                    dve.wait_ge(silu_ready, chunk * 2 + t + 1)
                    v.scalar_tensor_tensor(out=h_tok[:, t, :], in0=silu_g[:, t, :], scalar=0.5,
                                           in1=ps[:, GU + t, FC:2 * FC], op0=ALU.mult, op1=ALU.mult).then_inc(h_ready, 1)

            def ht_lo_of(chunk):
                dve.wait_ge(hthi_ready, chunk + 1)
                v.tensor_tensor(ht_lo[:, :, :, :].rearrange("p k t c -> p (k t c)"), ps[:, HT, :],
                                ht_hi[:, :, :, :].rearrange("p k t c -> p (k t c)").bitcast(f32),
                                ALU.subtract).then_inc(ht_ready, 1)

            def ffn(layer, f, base):
                chunk0 = (layer * 2 + f) * CHUNKS
                lo_of(layer, base + 3)
                hidden(chunk0)
                lo_of(layer, base + 4)
                ht_lo_of(chunk0)
                with dve.Fori(1, CHUNKS) as c:
                    make_lo(layer, c * 3 + (base + 2), 2)
                    hidden(chunk0 + c)
                    make_lo(layer, c * 3 + (base + 3), 0)
                    ht_lo_of(chunk0 + c)
                    make_lo(layer, c * 3 + (base + 4), 1)
                lo_of(layer, base + 3 * CHUNKS + 2)

            v.memset(big[:, :, 0:3], 0.0).then_inc(pads_ready, 1)
            v.memset(u_raw[:, :, 0:3], 0.0).then_inc(pads_ready, 1)
            v.memset(warm[:, :], 1.0).then_inc(pads_ready, 1)
            v.memset(sp[:, :, :], 0.0).then_inc(lo_ready, SLOTS)
            v.memset(msq[:, :], 0.0).then_inc(unit_done, SLOTS)
            v.memset(rstd[:, :], 0.0).then_inc(gain_used, 1)
            dve.wait_ge(cst_loaded, 16)
            v.tensor_copy(id_r[:, :], ident).then_inc(masks_ready, 1)
            v.tensor_copy(ssd_mask[:, :], cst[:, C_SSD:C_SSD + 512]).then_inc(masks_ready, 1)
            v.tensor_copy(att_mask[:, :], cst[:, C_ATT:C_ATT + P]).then_inc(masks_ready, 1)
            dve.wait_ge(x_loaded, 16)
            v.memset(mv[:, :, :], 0.0).then_inc(x_ready, 2)

            with dve.Fori(0, DEPTH) as layer:
                steps = [0]

                def step(ins):
                    steps[0] += 1
                    ins.then_inc(dve_step, 1)
                    dve.wait_ge(dve_step, layer * DVE_STEPS + steps[0])

                def done(n):
                    dve.wait_ge(unit_done, layer * UNITS + n + 1 + SLOTS)

                def layer_norm(i, bank, last_unit):
                    dve.wait_ge(gain_in, (layer * 4 + i + 1) * 16)
                    for t in range(TT):
                        if t == 0:
                            dve.wait_ge(acc_half, layer * 5 + (0, 1, 2)[i] + 1)
                        else:
                            done(last_unit)
                        step(v.scalar_tensor_tensor(out=x_tok[:, t, :], in0=x_tok[:, t, :], scalar=ALPHA,
                                                    in1=ps[:, bank + 2 * t:bank + 2 * t + 2, :].rearrange("p b c -> p (b c)"),
                                                    op0=ALU.mult, op1=ALU.add))
                        for s in range(2):
                            ins = v.bn_stats(stats[:, t, s, :], x_tok[:, t, s * 512:(s + 1) * 512])
                            if s == 1:
                                step(ins)
                        v.memset(spare[:, :], 0.0)
                        step(v.bn_aggr(mv[:, t, :], stats[:, t, :, :].rearrange("p a b -> p (a b)")))
                        v.tensor_scalar(rstd[:, t:t + 1], mv[:, t, 1:2], EPS, None, ALU.add).then_inc(var_ready, 1)
                        step(v.scalar_tensor_tensor(out=x_tok[:, t, :], in0=x_tok[:, t, :], scalar=mv[:, t, 0:1],
                                                    in1=gain[:, 0, :], op0=ALU.subtract, op1=ALU.mult))
                        dve.wait_ge(std_ready, (layer * 3 + i) * 2 + t + 1)
                        step(v.reciprocal(rstd[:, t:t + 1], rstd[:, t:t + 1]))
                        v.scalar_tensor_tensor(out=x_tok[:, t, :], in0=x_tok[:, t, :], scalar=rstd[:, t:t + 1],
                                               in1=gain[:, 1, :], op0=ALU.mult, op1=ALU.add).then_inc(x_ready, 1)
                    dve.wait_ge(x_ready, (layer * 4 + i) * 2 + 4)
                    v.memset(stats[:, 0, 0, 0:1], 0.0).then_inc(gain_used, 1)

                for n in range(SLOTS):
                    lo_of(layer, n)
                xt_lo_of(layer, 0, 0)
                dve.wait_ge(exhi_ready, layer + 1)
                v.tensor_tensor(ex_lo[:, :], ex[:, E_SPLIT:E_ALL], ex_hi[:, :].bitcast(f32),
                                ALU.subtract).then_inc(exlo_ready, 1)
                ffn(layer, 0, U_FFN1)
                layer_norm(0, 0, U_FFN1 + FFN_UNITS - 1)
                xt_lo_of(layer, 1, 0)

                v.tensor_scalar(sp[:, 0, SEQ:SEQ + 2], ex[:, E_LAM:E_LAM + 2], -1.0, None, ALU.mult)
                dve.wait_ge(fd_done, layer + 1)
                step(v.tensor_scalar(sp[0:ROWS, 0, 0:SEQ], ps[0:ROWS, 0, 0:SEQ], ex[0:ROWS, E_BIAS:E_BIAS + 1],
                                     ex[0:ROWS, E_SIGN:E_SIGN + 1], ALU.add, ALU.mult))
                v.scalar_tensor_tensor(out=sp[:, 1, :], in0=sp[:, 0, :], scalar=-1.0, in1=sp[:, 0, :],
                                       op0=ALU.mult, op1=ALU.max).then_inc(abs_ready, 1)
                dve.wait_ge(exp_ready, layer + 1)
                step(v.tensor_scalar(sp[:, 2, :], sp[:, 1, :], 2.0, None, ALU.add))
                step(v.reciprocal(sp[:, 2, :], sp[:, 2, :]))
                step(v.tensor_tensor(sp[:, 1, :], sp[:, 1, :], sp[:, 2, :], ALU.mult))
                step(v.tensor_tensor(sp[:, 3, :], sp[:, 1, :], sp[:, 1, :], ALU.mult))
                step(v.tensor_scalar(sp[:, 4, :], sp[:, 3, :], 1.0 / 17, None, ALU.mult))
                for k in (15, 13, 11, 9, 7, 5, 3):
                    step(v.scalar_tensor_tensor(out=sp[:, 4, :], in0=sp[:, 4, :], scalar=1.0 / k, in1=sp[:, 3, :],
                                                op0=ALU.add, op1=ALU.mult))
                step(v.scalar_tensor_tensor(out=sp[:, 4, :], in0=sp[:, 4, :], scalar=1.0, in1=sp[:, 1, :],
                                            op0=ALU.add, op1=ALU.mult))
                step(v.tensor_scalar(sp[:, 4, :], sp[:, 4, :], 2.0, None, ALU.mult))
                step(v.scalar_tensor_tensor(out=sp[:, 5, :], in0=sp[:, 0, :], scalar=0.0, in1=sp[:, 4, :],
                                            op0=ALU.max, op1=ALU.add))
                v.tensor_scalar(c8[:, 0, :], sp[:, 5, SEQ:SEQ + 2], -8.0, None, ALU.mult)
                v.tensor_scalar(c8[:, 1, :], sp[:, 5, SEQ:SEQ + 2], 8.0, None, ALU.mult)
                step(v.tensor_scalar(sp[0:ROWS, 2, 0:SEQ], sp[0:ROWS, 5, 0:SEQ], expa[:, 0:1], -1.0,
                                     ALU.mult, ALU.mult))
                v.tensor_tensor_scan(cum[:, 0, :], cst[0:ROWS, C_RESET:C_RESET + SEQ], sp[0:ROWS, 2, 0:SEQ], 0.0,
                                     ALU.mult, ALU.add).then_inc(cum_ready, 1)

                def conv(dst, src, m, taps, tiles):
                    for j in range(3):
                        ins = v.scalar_tensor_tensor(out=dst[:, m, :], in0=src[:, m, j:j + SEQ],
                                                     scalar=ex[:, taps + j * tiles + m:taps + j * tiles + m + 1],
                                                     in1=dst[:, m, :], op0=ALU.mult, op1=ALU.add)
                        if j < 2:
                            step(ins)
                    return ins

                for i in range(4):
                    dve.wait_ge(conv_first, layer * 5 + i + 1)
                    conv(xbc, big, 2 * i, E_CW, 8)
                    conv(xbc, big, 2 * i + 1, E_CW, 8).then_inc(conv_ready, 1)
                    lo_of(layer, U_XS + i + 3)
                for n in range(U_Q, U_U):
                    lo_of(layer, n + 3)
                dve.wait_ge(conv_first, layer * 5 + 5)
                conv(uc, u_raw, 0, E_UW, 2)
                conv(uc, u_raw, 1, E_UW, 2).then_inc(conv_ready, 1)
                for n in (U_U, U_G):
                    lo_of(layer, n + 3)

                dve.wait_ge(xs_turned, layer + 1)
                dve.wait_ge(cumtok_ready, layer + 1)
                dve.wait_ge(mix_in, layer * 16 + 16)
                for t in range(TT):
                    xs = ps[:, 4 + t, :].rearrange("p (h d) -> p h d", h=SH)
                    v.tensor_tensor(xdt[:, t, :, :], xs, cum_tok[:, t, 1, AH:ROWS].unsqueeze(2).to_broadcast([P, SH, HD]),
                                    ALU.mult)
                    ins = v.tensor_tensor(y_tok[:, t, :].rearrange("p (h d) -> p h d", h=SH), xs,
                                          mix[:, 512:520].unsqueeze(2).to_broadcast([P, SH, HD]), ALU.mult)
                ins.then_inc(xs_used, 1)
                dve.wait_ge(logits_done, layer + 1)
                v.tensor_reduce(nmax[:, 0, :], ps[:, 4:8, 0:P], AX.X, ALU.max)
                step(v.tensor_reduce(nmax[:, 1, :], ps[:, 4:8, P:3 * P], AX.X, ALU.max))
                v.tensor_scalar(nmax[:, :, :], nmax[:, :, :], -1.0, None, ALU.mult).then_inc(nmax_ready, 1)
                dve.wait_ge(decay_ready, (layer + 1) * 16)
                dve.wait_ge(xs_used, layer + 1)
                v.tensor_tensor(xdd[:, :, :], xdt[:, 0, :, :], decay[:, :, 0, P - 1:P].to_broadcast([P, SH, HD]),
                                ALU.mult).then_inc(xdd_ready, 1)
                dve.wait_ge(xdd_ready, layer + 1)
                for g in range(NG):
                    for c in range(TT):
                        d = decay[:, 4 * g:4 * g + 4, c, :]
                        v.tensor_tensor(d, d, cb[:, g, c, :].unsqueeze(1).to_broadcast([P, 4, P]),
                                        ALU.mult).then_inc(m_ready, 1)
                dve.wait_ge(aa_ready, layer + 1)
                r, ig, a, th = (lru[:, i, :, :] for i in range(4))
                step(v.tensor_tensor(r, a, a, ALU.mult))
                v.scalar_tensor_tensor(out=th, in0=r, scalar=1.0, in1=th, op0=ALU.add, op1=ALU.mult)\
                    .then_inc(one_a2_ready, 1)
                dve.wait_ge(probs_raw, layer + 1)
                step(v.reciprocal(rsum[:, :, :], rsum[:, :, :]))
                v.tensor_tensor(probs[:, :, 0:P], probs[:, :, 0:P],
                                rsum[:, 0, :].unsqueeze(2).to_broadcast([P, AH, P]), ALU.mult)
                v.tensor_tensor(probs[:, :, P:3 * P], probs[:, :, P:3 * P],
                                rsum[:, 1, :].unsqueeze(2).to_broadcast([P, AH, 2 * P]), ALU.mult).then_inc(probs_ready, 1)
                step(v.tensor_tensor(ig, ig, uc[:, :, :], ALU.mult))
                dve.wait_ge(root_ready, layer + 1)
                step(v.tensor_tensor(ig, ig, th, ALU.mult))
                for m in range(2):
                    ins = v.tensor_tensor_scan(r[:, m, :], a[:, m, :], ig[:, m, :], 0.0, ALU.mult, ALU.add)
                step(ins)
                v.tensor_tensor(ig, r, gate_g[:, :, :], ALU.mult).then_inc(ya_ready, 1)
                dve.wait_ge(ydiag_done, layer + 1)
                step(v.tensor_tensor(y_tok[:, :, :], y_tok[:, :, :], ps[:, 0:2, :], ALU.add))
                dve.wait_ge(yoff_done, layer + 1)
                step(v.tensor_tensor(y_off[:, :, :], ps[:, 3, :].rearrange("p (h d) -> p h d", h=SH),
                                     ecum[:, :].unsqueeze(2).to_broadcast([P, SH, HD]), ALU.mult))
                step(v.tensor_tensor(y_tok[:, 1, :], y_tok[:, 1, :], y_off[:, :, :].rearrange("p h d -> p (h d)"), ALU.add))
                v.tensor_tensor(y_tok[:, :, :], y_tok[:, :, :], z_tok[:, :, :], ALU.mult).then_inc(yz_ready, 1)

                def split_lo(kt0, n, src, signal):
                    v.tensor_tensor(xt_lo[:, :, kt0:kt0 + n, :], src, xt_hi[:, :, kt0:kt0 + n, :].bitcast(f32),
                                    ALU.subtract).then_inc(signal, 1)

                dve.wait_ge(yahi_ready, layer + 1)
                split_lo(0, 2, ig.rearrange("p m (t c) -> p t m c", t=TT), yalo_ready)
                dve.wait_ge(ybhi_ready, layer + 1)
                split_lo(2, 2, ps[:, 2, :].rearrange("p (m t c) -> p t m c", m=2, t=TT), yblo_ready)
                dve.wait_ge(msq_ready, layer * 4 + 4)
                v.tensor_scalar(msq[:, :], msq[:, :], 1.0 / 256, EPS, ALU.mult, ALU.add).then_inc(ms_ready, 1)
                dve.wait_ge(rms_ready, layer + 1)
                step(v.reciprocal(msq[:, :], msq[:, :]))
                for t in range(TT):
                    for g in range(NG):
                        i, c = t * NG + g, slice(g * 256, (g + 1) * 256)
                        ins = v.scalar_tensor_tensor(out=y_tok[:, t, c], in0=y_tok[:, t, c], scalar=msq[:, i:i + 1],
                                                     in1=mix[:, c], op0=ALU.mult, op1=ALU.mult)
                    ins.then_inc(yn_ready, 1)
                for t in range(TT):
                    dve.wait_ge(ychi_ready, layer * 2 + t + 1)
                    v.tensor_tensor(xt_lo[:, t, 4:8, :].rearrange("p k c -> p (k c)"), ps[:, t, :],
                                    xt_hi[:, t, 4:8, :].rearrange("p k c -> p (k c)").bitcast(f32),
                                    ALU.subtract).then_inc(yclo_ready, 1)
                for n in range(U_OUT, U_OUT + 4):
                    lo_of(layer, n + 3)
                layer_norm(1, 4, U_OUT + 3)
                xt_lo_of(layer, 2, 4)
                ffn(layer, 1, U_FFN2)
                layer_norm(2, 0, U_FFN2 + FFN_UNITS - 1)
                xt_lo_of(layer, 3, 0)
                for n in range(U_GATE, U_GATE + 2):
                    lo_of(layer, n + 3)
                dve.wait_ge(gain_in, (layer * 4 + 4) * 16)
                for t in range(TT):
                    if t == 0:
                        dve.wait_ge(acc_half, layer * 5 + 4)
                    else:
                        done(U_PE - 1)
                    ins = v.tensor_tensor(sig[:, t, :], ps[:, 2 * t:2 * t + 2, :].rearrange("p b c -> p (b c)"),
                                          gain[:, 0, :], ALU.add)
                    ins.then_inc(biased_ready, 1)
                for t in range(TT):
                    if t == 0:
                        dve.wait_ge(acc_half, layer * 5 + 5)
                    else:
                        done(U_PE)
                    dve.wait_ge(sig_ready, layer * 2 + t + 1)
                    ins = v.tensor_tensor(sig[:, t, :], sig[:, t, :],
                                          ps[:, 4 + 2 * t:6 + 2 * t, :].rearrange("p b c -> p (b c)"), ALU.mult)
                    if t == 0:
                        step(ins)
                    else:
                        step(ins)
                    v.tensor_tensor(x_tok[:, t, :], x_tok[:, t, :], sig[:, t, :], ALU.add).then_inc(x_ready, 1)
                dve.wait_ge(x_ready, layer * 8 + 10)
                v.memset(big[:, :, 0:3], 0.0).then_inc(gain_used, 1)
                assert steps[0] == DVE_STEPS, steps[0]


def lay_out(i):
    import numpy as np
    f = np.float32
    ws = np.zeros((DEPTH, UNITS, P, W), f)

    def tiles(w):
        return w.reshape(w.shape[0] // P, P, w.shape[1]).transpose(1, 0, 2)

    def flat(a):
        return a.reshape(P, -1)

    for l in range(DEPTH):
        for base, name in ((U_FFN1, "ffn1"), (U_FFN2, "ffn2")):
            wg, wu = tiles(i[f"{name}_wg"][l]), tiles(i[f"{name}_wu"][l])
            wd = tiles(i[f"{name}_wd"][l])
            n = base
            for c in range(CHUNKS + 1):
                if c < CHUNKS:
                    cols = slice(c * FC, (c + 1) * FC)
                    for half in range(2):
                        k = slice(4 * half, 4 * half + 4)
                        ws[l, n] = flat(np.stack([wg[:, k, cols], wu[:, k, cols]], axis=2))
                        n += 1
                if c > 0:
                    ws[l, n] = flat(wd[:, 2 * (c - 1):2 * c, :])
                    n += 1
        wi = tiles(i["w_in"][l])
        for n, col in ((U_XS, 1796), (U_XS + 1, 2052), (U_B, 2308), (U_C, 2564), (U_Q, 512), (U_K, 768), (U_V, 1024),
                       (U_U, 0), (U_G, 256)):
            ws[l, n] = flat(wi[:, :, col:col + 256])
        for half in range(2):
            ws[l, U_Z + half] = flat(wi[:, 4 * half:4 * half + 4, 1284:1796])
        for base, name, count in ((U_OUT, "w_out", 4), (U_GATE, "pe_gate_w", 4), (U_PE, "pe_proj", 1)):
            w = tiles(i[name][l])
            for j in range(count):
                ws[l, base + j] = flat(w[:, 2 * j:2 * j + 2, :])

    ex = np.zeros((DEPTH, P, E_ALL), f)
    for l in range(DEPTH):
        ex[l, :, E_CW:E_CW + 32] = i["ssd_conv_w"][l].reshape(32, P).T
        ex[l, :, E_CB:E_CB + 8] = i["ssd_conv_b"][l].reshape(8, P).T
        ex[l, :, E_UW:E_UW + 8] = i["lru_conv_w"][l].reshape(8, P).T
        for at, name in ((E_UB, "lru_conv_b"), (E_BA, "lru_ba"), (E_BX, "lru_bx"), (E_LAM, "lru_lambda")):
            ex[l, :, at:at + 2] = i[name][l].reshape(2, P).T
        ex[l, 0:AH, E_BIAS] = i["fox_bf"][l]
        ex[l, AH:ROWS, E_BIAS] = i["ssd_dt_bias"][l]
        ex[l, 0:AH, E_SIGN] = -1.0
        ex[l, AH:ROWS, E_SIGN] = 1.0
        ex[l, AH:ROWS, E_ALOG] = i["ssd_a_log"][l]
        for at, name in ((E_WA, "lru_wa"), (E_WX, "lru_wx")):
            for h in range(4):
                r, m = h % 2 * HD, h // 2
                ex[l, r:r + HD, at + m * P + r:at + m * P + r + HD] = i[name][l, h]
        wi = tiles(i["w_in"][l])
        fd = ex[l, :, E_FD:E_PT].reshape(P, KT, ROWS)
        ex[l, :, E_FD:E_PT] = flat(np.concatenate([wi[:, :, 1280:1284], wi[:, :, 2820:2828]], axis=2))
        ex[l, :, E_PT:E_ALL] = flat(i["p"][l, 0].T.reshape(PLE // P, P, SEQ).transpose(1, 0, 2))

    norms = np.zeros((DEPTH, 4, 2, D), f)
    for j in range(3):
        norms[:, j, 0] = i[f"ln{j + 1}_g"]
        norms[:, j, 1] = i[f"ln{j + 1}_b"]
    norms[:, 3, 0] = i["pe_gate_b"]
    mix_rows = np.concatenate([i["ssd_norm_g"], i["ssd_d"]], axis=1)

    cst = np.zeros((P, C_ALL), f)
    cst[:, C_ID:C_ID + P] = np.eye(P, dtype=f)
    cst[:, C_SSD:C_SSD + 512] = np.tile(-BIG * np.tril(np.ones((P, P), f), -1), (1, 4))
    cst[:, C_ATT:C_ATT + P] = -BIG * np.triu(np.ones((P, P), f), 1)
    for h in range(ROWS):
        cst[h, C_SEL + h * P:C_SEL + (h + 1) * P] = 1.0
    cst[0:ROWS, C_RESET:C_RESET + SEQ] = 1.0
    cst[AH:ROWS, C_RESET + P] = 0.0
    x = i["x"][0].reshape(TT, P, D).transpose(1, 0, 2)
    return {"w_stream": ws, "extras": ex, "norms": norms, "mix_rows": mix_rows, "consts": cst, "x": x}


def kernel(**inputs):
    import numpy as _np
    import concourse.bacc as _bacc
    from concourse import mybir as _mybir
    from concourse.bass_utils import run_bass_kernel_spmd as _run

    nc = _bacc.Bacc("TRN2", target_bir_lowering=False, num_devices=1)
    arrays, args = {}, []
    for name, a in lay_out({k: _np.asarray(v) for k, v in inputs.items()}).items():
        a = _np.ascontiguousarray(a)
        arrays[f"in_{name}_dram"] = a
        args.append(nc.dram_tensor(f"in_{name}_dram", a.shape, _mybir.dt.from_np(a.dtype), kind="ExternalInput").ap())
    args.append(nc.dram_tensor("out_0_dram", (P, TT, D), _mybir.dt.float32, kind="ExternalOutput").ap())
    trunk(nc, *args)
    r = _run(nc, [arrays], core_ids=[0])
    got = r.results[0]["out_0_dram"]
    return got.transpose(1, 0, 2).reshape(1, SEQ, D)
```

```python
import concourse.bass as bass
from concourse import mybir
from contextlib import ExitStack

P = 128
DEPTH, SEQ, D = 2, 256, 1024
TT = SEQ // P
KT = D // P
F = 2816
FC = 256
CHUNKS = F // FC
HD = 64
AH, SH = 4, 8
NG = 2
ROWS = AH + SH
PLE = 256
ALPHA = (2.0 * DEPTH) ** 0.25
EPS = 1e-5
BIG = 1e30

W = 2048
SLOTS = 3
FFN_UNITS = 3 * CHUNKS
U_FFN1 = 0
U_V, U_Z = FFN_UNITS, FFN_UNITS + 1
U_XS, U_B, U_C = U_Z + 2, U_Z + 4, U_Z + 5
U_U, U_G, U_Q, U_K = U_C + 1, U_C + 2, U_C + 3, U_C + 4
U_YA, U_YC, U_YB = U_K + 1, U_K + 2, U_K + 4
U_FFN2 = U_YB + 1
U_PE = U_FFN2 + FFN_UNITS
U_GATE = U_PE + 1
UNITS = U_GATE + 4
SLOT_UNITS = [(UNITS - s + SLOTS - 1) // SLOTS for s in range(SLOTS)]
assert U_FFN1 % SLOTS == 0 and U_FFN2 % SLOTS == 0 and FFN_UNITS % SLOTS == 0 and UNITS % SLOTS == 2

E_CW, E_CB = 0, 32
E_UW, E_UB = 40, 48
E_BA, E_BX, E_LAM = 50, 52, 54
E_BIAS, E_SIGN, E_ALOG = 56, 57, 58
E_WA, E_WX = 60, 316
E_SPLIT = 572
E_FD = E_SPLIT
E_PT = E_FD + KT * ROWS
E_ALL = E_PT + (PLE // P) * SEQ
NSPLIT = E_ALL - E_SPLIT

C_ID, C_SSD, C_ATT, C_RESET = 0, P, 2 * P, 3 * P
C_ALL = C_RESET + SEQ

DVE_STEPS, ACT_STEPS = 51, 2


def free_count(n):
    return {0: 2, 1: 3, 2: 1}.get(n, n + 1) if isinstance(n, int) else n + 1


def trunk(nc, w_stream, extras, norms, mix_rows, consts, x_in_dram, out):
    f32, f32r = mybir.dt.float32, mybir.dt.float32r
    ALU, ACT, AX = mybir.AluOpType, mybir.ActivationFunctionType, mybir.AxisListType

    with ExitStack() as ctx:
        def sb(name, shape, dt=f32):
            return ctx.enter_context(nc.sbuf_tensor(name, shape, dt))

        def sem(name):
            return ctx.enter_context(nc.semaphore(name))

        w_raw = sb("w_raw", [P, SLOTS, W])
        w_hi = sb("w_hi", [P, SLOTS, W], f32r)
        w_lo = sb("w_lo", [P, SLOTS, W], f32r)
        xt_hi = sb("xt_hi", [P, TT, KT, P], f32r)
        xt_lo = sb("xt_lo", [P, TT, KT, P], f32r)
        x_tok = sb("x_tok", [P, TT, D])
        gain = sb("gain", [P, 2, D])
        mix = sb("mix", [P, 520])
        ex = sb("ex", [P, E_ALL])
        ex_hi = sb("ex_hi", [P, NSPLIT], f32r)
        ex_lo = sb("ex_lo", [P, NSPLIT], f32r)
        cst = sb("cst", [P, C_ALL])
        id_r = sb("id_r", [P, P], f32r)
        ssd_mask = sb("ssd_mask", [P, 512], f32r)
        att_mask = sb("att_mask", [P, P], f32r)
        big = sb("big", [P, 8, 260])
        xbc = sb("xbc", [P, 8, SEQ])
        u_raw = sb("u_raw", [P, 2, 260])
        uc = sb("uc", [P, 2, SEQ])
        gate_g = sb("gate_g", [P, 2, SEQ])
        qf = sb("qf", [P, AH, SEQ])
        kf = sb("kf", [P, AH, SEQ])
        v_tok = sb("v_tok", [P, TT, 256])
        z_tok = sb("z_tok", [P, TT, 512])
        sp = sb("sp", [P, 6, 258])
        cum = sb("cum", [ROWS, SEQ])
        cum_hi = sb("cum_hi", [ROWS, SEQ], f32r)
        cum_lo = sb("cum_lo", [ROWS, SEQ], f32r)
        sel = sb("sel", [ROWS, SH, P], f32r)
        expa = sb("expa", [ROWS, 1])
        c8 = sb("c8", [P, 2, 2])
        cum_tok = sb("cum_tok", [P, TT, 2, ROWS])
        ncum_tok = sb("ncum_tok", [P, TT, ROWS])
        ecum = sb("ecum", [P, SH])
        lru = sb("lru", [P, 4, 2, SEQ])
        xdt = sb("xdt", [P, TT, SH, HD])
        xdd = sb("xdd", [P, SH, HD])
        b_tok = sb("b_tok", [P, NG, P])
        cb = sb("cb", [P, NG, TT, P])
        state = sb("state", [P, SH * HD])
        y_tok = sb("y_tok", [P, TT, 512])
        probs = sb("probs", [P, 3, 512])
        nmax = sb("nmax", [P, 2, AH])
        rsum = sb("rsum", [P, 2, AH])
        nmean = sb("nmean", [P, TT])
        ssq = sb("ssq", [P, TT])
        rstd = sb("rstd", [P, TT])
        warm = sb("warm", [P, 2])
        msq = sb("msq", [P, TT * NG])
        ht_hi = sb("ht_hi", [P, 2, TT, P], f32r)
        ht_lo = sb("ht_lo", [P, 2, TT, P], f32r)
        hz_hi = sb("hz_hi", [P, 2, TT, P], f32r)
        hz_lo = sb("hz_lo", [P, 2, TT, P], f32r)
        ps = ctx.enter_context(nc.psum_tensor("ps", [P, 8, 512], f32))

        ident = cst[:, C_ID:C_ID + P]
        decay = big[:, :, :].rearrange("p a b -> p (a b)")[:, 0:SH * TT * P].rearrange(
            "p (h c l) -> p h c l", h=SH, c=TT)
        x_new = big[:, :, :].rearrange("p a b -> p (a b)")[:, 0:TT * D].rearrange("p (t d) -> p t d", t=TT)
        silu_g = probs[:, 0, :].rearrange("p (t f) -> p t f", t=TT)
        h_tok = probs[:, 1, :].rearrange("p (t f) -> p t f", t=TT)
        probs_t = xbc[:, 0:6, :].rearrange("p a b -> p (a b)").rearrange("p (a k) -> p a k", a=3)

        def block_of(h, q, k):
            return (0, h * P) if q == 0 else (1 + h // 2, (h % 2 * 2 + k) * P)
        y_off = xdd
        GU, HT = 4, 6

        x_loaded, cst_loaded = [sem(f"x_loaded{t}") for t in range(TT)], sem("cst_loaded")
        raw_in = [sem(f"raw_in{s}") for s in range(SLOTS)]
        hi_ready, lo_ready = sem("hi_ready"), sem("lo_ready")
        unit_done = sem("unit_done")
        ex_in, gain_in, mix_in = sem("ex_in"), sem("gain_in"), sem("mix_in")
        gain_used, mix_used = sem("gain_used"), sem("mix_used")
        exhi_ready, exlo_ready = sem("exhi_ready"), sem("exlo_ready")
        masks_ready, pads_ready = sem("masks_ready"), sem("pads_ready")
        x_ready = sem("x_ready")
        xt_turned, xthi_ready, xt_ready = sem("xt_turned"), sem("xthi_ready"), sem("xt_ready")
        gu_half, silu_ready, h_ready = sem("gu_half"), sem("silu_ready"), sem("h_ready")
        ht_turned, hthi_ready, ht_ready = sem("ht_turned"), sem("hthi_ready"), sem("ht_ready")
        acc_half = sem("acc_half")
        fd_done, abs_ready, exp_ready, cum_ready, cumhi_ready = (sem(n) for n in (
            "fd_done", "abs_ready", "exp_ready", "cum_ready", "cumhi_ready"))
        conv_first, conv_ready, xbc_ready = sem("conv_first"), sem("conv_ready"), sem("xbc_ready")
        v_out, z_out, g_out, q_out, k_out = (sem(n) for n in ("v_out", "z_out", "g_out", "q_out", "k_out"))
        cumsplit_ready, f_rows_ready, b_out, cb_out = (sem(n) for n in (
            "cumsplit_ready", "f_rows_ready", "b_out", "cb_out"))
        mean_ready, ssq_ready = sem("mean_ready"), sem("ssq_ready")
        cum_turned, cumtok_ready = sem("cum_turned"), sem("cumtok_ready")
        xs_turned, b_turned, cb_done = sem("xs_turned"), sem("b_turned"), sem("cb_done")
        gates_done, gates_ready, aa_ready = sem("gates_done"), sem("gates_ready"), sem("aa_ready")
        one_a2_ready, root_ready, ya_ready, yahi_ready, yalo_ready = (sem(n) for n in (
            "one_a2_ready", "root_ready", "ya_ready", "yahi_ready", "yalo_ready"))
        bc_done, decay_ready = sem("bc_done"), sem("decay_ready")
        xs_used, xdd_ready, m_ready = sem("xs_used"), sem("xdd_ready"), sem("m_ready")
        logits_done, nmax_ready, probs_raw, probs_ready = (sem(n) for n in (
            "logits_done", "nmax_ready", "probs_raw", "probs_ready"))
        ydiag_done, state_done, state_ready, yoff_done = (sem(n) for n in (
            "ydiag_done", "state_done", "state_ready", "yoff_done"))
        probs_turned, probst_ready, pv_done, ybhi_ready, yblo_ready = (sem(n) for n in (
            "probs_turned", "probst_ready", "pv_done", "ybhi_ready", "yblo_ready"))
        yz_ready, msq_ready, yn_ready, yc_turned, ychi_ready, yclo_ready = (sem(n) for n in (
            "yz_ready", "msq_ready", "yn_ready", "yc_turned", "ychi_ready", "yclo_ready"))
        var_ready, std_ready, ms_ready, rms_ready = sem("var_ready"), sem("std_ready"), sem("ms_ready"), sem("rms_ready")
        biased_ready, sig_ready = sem("biased_ready"), sem("sig_ready")
        dve_step, act_step, stored = sem("dve_step"), sem("act_step"), sem("stored")

        block = ctx.enter_context(nc.Block())

        @block.sync
        def _(sp_):
            def load(layer, n, slot):
                sp_.wait_ge(lo_ready, layer * UNITS + free_count(n))
                sp_.dma_start(w_raw[:, slot, :], w_stream[layer, n]).then_inc(raw_in[slot], 16)

            for t in range(TT):
                sp_.dma_start(x_tok[:, t, :], x_in_dram[:, t, :]).then_inc(x_loaded[t], 16)
            with sp_.Fori(0, DEPTH) as layer:
                for n in range(SLOTS):
                    load(layer, n, n)
                with sp_.Fori(1, UNITS // SLOTS) as g:
                    for s in range(SLOTS):
                        load(layer, g * SLOTS + s, s)
                for n in range(UNITS // SLOTS * SLOTS, UNITS):
                    load(layer, n, n % SLOTS)
            for t in range(TT):
                sp_.wait_ge(x_ready, 8 * DEPTH + t + 1)
                sp_.dma_start(out[:, t, :], x_tok[:, t, :]).then_inc(stored, 16)
            sp_.wait_ge(stored, 16 * TT)

        @block.gpsimd
        def _(pool):
            with pool.Fori(0, DEPTH) as layer:
                pool.wait_ge(x_ready, layer * 8 + 2)
                pool.dma_start(ex[:, :], extras[layer]).then_inc(ex_in, 16)
                pool.dma_start(mix[:, :], mix_rows[layer].partition_broadcast(P)).then_inc(mix_in, 16)
                for i in range(4):
                    pool.wait_ge(gain_used, layer * 4 + i + 1)
                    pool.dma_start(gain[:, :, :], norms[layer, i].partition_broadcast(P)).then_inc(gain_in, 16)

        @block.tensor
        def _(pe):
            mm = nc.tensor.matmul

            def unit_ready(layer, n):
                pe.wait_ge(lo_ready, layer * UNITS + n + 1 + SLOTS)

            def three(out_, a_hi, a_lo, b_hi, b_lo, start, stop):
                mm(out_, a_hi, b_hi, start=start, stop=False)
                mm(out_, a_hi, b_lo, start=False, stop=False)
                return mm(out_, a_lo, b_hi, start=False, stop=stop)

            def turn_x(layer, j, t):
                pe.wait_ge(x_ready, (layer * 4 + j) * 2 + t + 1)
                for k in range(KT):
                    last = nc.tensor.transpose(ps[:, 2 * t + k // 4, k % 4 * P:(k % 4 + 1) * P],
                                               x_tok[:, t, k * P:(k + 1) * P], ident)
                last.then_inc(xt_turned, 1)

            def xt_whole(layer, j, t):
                pe.wait_ge(xt_ready, (layer * 4 + j) * 2 + t + 1)

            def token_tile(slot, t, half, bank):
                hi = w_hi[:, slot, :].rearrange("p (k c) -> p k c", k=4)
                lo = w_lo[:, slot, :].rearrange("p (k c) -> p k c", k=4)
                for k in range(4):
                    kt = 4 * half + k
                    last = three(ps[:, bank, :], xt_hi[:, t, kt, :], xt_lo[:, t, kt, :], hi[:, k], lo[:, k],
                                 kt == 0, kt == KT - 1)
                return last

            def row_tile(slot, t, lhs, bank, first, last_unit):
                hi = w_hi[:, slot, :].rearrange("p (k h c) -> p k h c", k=2, h=2)
                lo = w_lo[:, slot, :].rearrange("p (k h c) -> p k h c", k=2, h=2)
                for k in range(2):
                    a_hi, a_lo = lhs(k, t)
                    for h in range(2):
                        mm(ps[:, bank + 2 * t + h, :], a_hi, hi[:, k, h], start=first and k == 0, stop=False)
                    for h in range(2):
                        mm(ps[:, bank + 2 * t + h, :], a_hi, lo[:, k, h], start=False, stop=False)
                    for h in range(2):
                        last = mm(ps[:, bank + 2 * t + h, :], a_lo, hi[:, k, h], start=False, stop=last_unit and k == 1)
                return last

            def row_unit(layer, n, slot, lhs, bank, first, last_unit, signal=None):
                unit_ready(layer, n)
                for t in range(TT):
                    last = row_tile(slot, t, lhs, bank, first, last_unit)
                    if t == 0 and signal is not None:
                        last.then_inc(signal, 1)
                last.then_inc(unit_done, 1)

            def channel_unit(layer, n, bank):
                unit_ready(layer, n)
                hi = w_hi[:, n % SLOTS, :].rearrange("p (k c) -> p k c", k=KT)
                lo = w_lo[:, n % SLOTS, :].rearrange("p (k c) -> p k c", k=KT)
                for m in range(2):
                    for k in range(KT):
                        c = slice(m * P, (m + 1) * P)
                        last = three(ps[:, bank, m * SEQ:(m + 1) * SEQ], hi[:, k, c], lo[:, k, c],
                                     xt_hi[:, :, k, :], xt_lo[:, :, k, :], k == 0, k == KT - 1)
                last.then_inc(unit_done, 1)

            def turn_h(chunk):
                pe.wait_ge(h_ready, chunk * 2 + 2)
                for k in range(2):
                    for t in range(TT):
                        last = nc.tensor.transpose(ps[:, HT, (k * TT + t) * P:(k * TT + t + 1) * P],
                                                   h_tok[:, t, k * P:(k + 1) * P], ident)
                last.then_inc(ht_turned, 1)

            def ht(k, t):
                return ht_hi[:, k, t, :], ht_lo[:, k, t, :]

            def hz(k, t):
                return hz_hi[:, k, t, :], hz_lo[:, k, t, :]

            def gate_up(layer, n, slots):
                unit_ready(layer, n)
                for t in range(TT):
                    last = token_tile(slots[0], t, 0, GU + t)
                last.then_inc(unit_done, 1)
                unit_ready(layer, n + 1)
                token_tile(slots[1], 0, 1, GU).then_inc(gu_half, 1)
                token_tile(slots[1], 1, 1, GU + 1).then_inc(unit_done, 1)

            def ffn(layer, f, base, j):
                chunk0 = (layer * 2 + f) * CHUNKS
                turn_x(layer, j, 0)
                unit_ready(layer, base)
                xt_whole(layer, j, 0)
                token_tile(0, 0, 0, GU)
                turn_x(layer, j, 1)
                unit_ready(layer, base + 1)
                token_tile(1, 0, 1, GU).then_inc(gu_half, 1)
                xt_whole(layer, j, 1)
                token_tile(0, 1, 0, GU + 1).then_inc(unit_done, 1)
                token_tile(1, 1, 1, GU + 1).then_inc(unit_done, 1)
                turn_h(chunk0)
                gate_up(layer, base + 2, (2, 0))
                pe.wait_ge(ht_ready, chunk0 + 1)
                row_unit(layer, base + 4, 1, ht, 0, True, False)
                turn_h(chunk0 + 1)
                with pe.Fori(2, CHUNKS - 1) as c:
                    gate_up(layer, c * 3 + (base - 1), (2, 0))
                    pe.wait_ge(ht_ready, chunk0 + c)
                    row_unit(layer, c * 3 + (base + 1), 1, ht, 0, False, False)
                    turn_h(chunk0 + c)
                gate_up(layer, base + 3 * CHUNKS - 4, (2, 0))
                pe.wait_ge(ht_ready, chunk0 + CHUNKS - 1)
                unit_ready(layer, base + 3 * CHUNKS - 2)
                row_tile(1, 0, ht, 0, False, False)
                turn_h(chunk0 + CHUNKS - 1)
                row_tile(1, 1, ht, 0, False, False).then_inc(unit_done, 1)
                pe.wait_ge(ht_ready, chunk0 + CHUNKS)
                row_unit(layer, base + FFN_UNITS - 1, 2, hz, 0, False, True, acc_half)

            def xt(kt0):
                return lambda k, t: (xt_hi[:, t, kt0 + k, :], xt_lo[:, t, kt0 + k, :])

            def v_tile(t):
                hi = w_hi[:, U_V % SLOTS, :].rearrange("p (k c) -> p k c", k=KT)
                lo = w_lo[:, U_V % SLOTS, :].rearrange("p (k c) -> p k c", k=KT)
                for k in range(KT):
                    last = three(ps[:, 7, t * 256:(t + 1) * 256], xt_hi[:, t, k, :], xt_lo[:, t, k, :],
                                 hi[:, k], lo[:, k], k == 0, k == KT - 1)
                return last

            pe.wait_ge(cst_loaded, 16)
            with pe.Fori(0, DEPTH) as layer:
                ffn(layer, 0, U_FFN1, 0)

                turn_x(layer, 1, 0)
                unit_ready(layer, U_V)
                xt_whole(layer, 1, 0)
                v_tile(0)
                unit_ready(layer, U_Z)
                token_tile(U_Z % SLOTS, 0, 0, 4)
                turn_x(layer, 1, 1)
                unit_ready(layer, U_Z + 1)
                token_tile((U_Z + 1) % SLOTS, 0, 1, 4)
                xt_whole(layer, 1, 1)
                v_tile(1).then_inc(unit_done, 1)
                token_tile(U_Z % SLOTS, 1, 0, 5).then_inc(unit_done, 1)
                token_tile((U_Z + 1) % SLOTS, 1, 1, 5).then_inc(unit_done, 1)
                pe.wait_ge(exlo_ready, layer + 1)
                for k in range(KT):
                    c = slice(k * ROWS, (k + 1) * ROWS)
                    last = three(ps[0:ROWS, 0, 0:SEQ], ex_hi[:, c], ex_lo[:, c], xt_hi[:, :, k, :], xt_lo[:, :, k, :],
                                 k == 0, k == KT - 1)
                last.then_inc(fd_done, 1)
                channel_unit(layer, U_XS, 1)
                channel_unit(layer, U_XS + 1, 6)
                pe.wait_ge(z_out, layer + 1)
                channel_unit(layer, U_B, 5)
                pe.wait_ge(conv_first, layer * 5 + 2)
                channel_unit(layer, U_C, 6)
                pe.wait_ge(cumsplit_ready, layer + 1)
                for b, bank in enumerate((2, 3, 1, 4)):
                    for i in range(2):
                        for first, part in ((True, cum_hi), (False, cum_lo)):
                            mm(ps[:, bank, i * SEQ:(i + 1) * SEQ], sel[:, 2 * b + i, :], part[:, :],
                               start=first and i == 0, stop=False, skip_group_check=True)
                    last = mm(ps[:, bank, :], id_r[:, :], ssd_mask[:, :], start=False, stop=True, skip_group_check=True)
                last.then_inc(bc_done, 1)
                for t in range(TT):
                    for i, rows in enumerate((cum[:, :], sp[0:ROWS, 5, 0:SEQ])):
                        c = (t * 2 + i) * ROWS
                        last = nc.tensor.transpose(ps[:, 0, c:c + ROWS], rows[:, t * P:(t + 1) * P],
                                                   cst[0:ROWS, C_ID:C_ID + ROWS])
                last.then_inc(cum_turned, 1)
                pe.wait_ge(v_out, layer + 1)
                channel_unit(layer, U_U, 7)
                pe.wait_ge(conv_first, layer * 5 + 4)
                pe.wait_ge(xbc_ready, layer * 4 + 2)
                for t in range(TT):
                    for m in range(4):
                        last = nc.tensor.transpose(ps[:, 5 + t, m * P:(m + 1) * P], xbc[:, m, t * P:(t + 1) * P], ident)
                last.then_inc(xs_turned, 1)
                pe.wait_ge(cumtok_ready, layer + 1)
                pe.wait_ge(xbc_ready, layer * 4 + 3)
                for g in range(NG):
                    last = nc.tensor.transpose(ps[:, 0, g * P:(g + 1) * P], xbc[:, 4 + g, 0:P], ident)
                last.then_inc(b_turned, 1)
                pe.wait_ge(conv_first, layer * 5 + 5)
                channel_unit(layer, U_G, 7)
                pe.wait_ge(decay_ready, layer * 16 + 8)
                pe.wait_ge(xbc_ready, layer * 4 + 4)
                for g in range(NG):
                    for c in range(TT):
                        s = slice(c * P, (c + 1) * P)
                        last = mm(ps[:, 2, (g * TT + c) * P:(g * TT + c + 1) * P], xbc[:, 4 + g, s], xbc[:, 6 + g, s],
                                  start=True, stop=True)
                last.then_inc(cb_done, 1)
                pe.wait_ge(b_out, layer + 1)
                pe.wait_ge(conv_ready, layer * 5 + 5)
                for bank, w in ((3, E_WA), (0, E_WX)):
                    for m in range(2):
                        last = mm(ps[:, bank, m * SEQ:(m + 1) * SEQ], ex[:, w + m * P:w + (m + 1) * P], uc[:, m, :],
                                  start=True, stop=True)
                last.then_inc(gates_done, 1)
                pe.wait_ge(xs_used, layer + 1)
                channel_unit(layer, U_Q, 5)
                channel_unit(layer, U_K, 6)
                pe.wait_ge(cb_out, layer + 1)
                pe.wait_ge(xdd_ready, layer + 1)
                for g in range(NG):
                    last = mm(ps[:, 2, g * 256:(g + 1) * 256], b_tok[:, g, :],
                              xdd[:, 4 * g:4 * g + 4, :].rearrange("p h d -> p (h d)"), start=True, stop=True)
                last.then_inc(state_done, 1)
                pe.wait_ge(gates_ready, layer + 1)
                pe.wait_ge(m_ready, layer * 4 + 4)
                for c in range(TT):
                    for h in range(SH):
                        last = mm(ps[:, c, h * HD:(h + 1) * HD], decay[:, h, c, :], xdt[:, c, h, :],
                                  start=True, stop=True)
                last.then_inc(ydiag_done, 1)
                pe.wait_ge(f_rows_ready, layer + 1)
                pe.wait_ge(q_out, layer + 1)
                pe.wait_ge(k_out, layer + 1)
                pe.wait_ge(g_out, layer + 1)
                for h in range(AH):
                    for q, k in ((0, 0), (1, 0), (1, 1)):
                        b, c = block_of(h, q, k)
                        last = mm(ps[:, 5 + b, c:c + P], qf[:, h, q * P:(q + 1) * P], kf[:, h, k * P:(k + 1) * P],
                                  start=True, stop=q != k)
                        if q == k:
                            last = mm(ps[:, 5 + b, c:c + P], id_r[:, :], att_mask[:, :], start=False, stop=True)
                last.then_inc(logits_done, 1)
                pe.wait_ge(state_ready, layer + 1)
                for g in range(NG):
                    last = mm(ps[:, 3, g * 256:(g + 1) * 256], xbc[:, 6 + g, P:2 * P], state[:, g * 256:(g + 1) * 256],
                              start=True, stop=True)
                last.then_inc(yoff_done, 1)
                pe.wait_ge(yz_ready, layer + 1)
                pe.wait_ge(yalo_ready, layer + 1)
                row_unit(layer, U_YA, U_YA % SLOTS, xt(0), 0, True, False)
                for t in range(TT):
                    pe.wait_ge(yn_ready, layer * 2 + t + 1)
                    if t > 0:
                        pe.wait_ge(yclo_ready, layer * 2 + t)
                    for m in range(4):
                        last = nc.tensor.transpose(ps[:, 4, m * P:(m + 1) * P], y_tok[:, t, m * P:(m + 1) * P], ident)
                    last.then_inc(yc_turned, 1)
                pe.wait_ge(probs_ready, layer + 1)
                for b in range(3):
                    for i in range(4):
                        last = nc.tensor.transpose(ps[:, 5 + b, i * P:(i + 1) * P], probs[:, b, i * P:(i + 1) * P], ident)
                last.then_inc(probs_turned, 1)
                pe.wait_ge(yclo_ready, layer * 2 + 2)
                row_unit(layer, U_YC, U_YC % SLOTS, xt(4), 0, False, False)
                row_unit(layer, U_YC + 1, (U_YC + 1) % SLOTS, xt(6), 0, False, False)
                pe.wait_ge(probst_ready, layer + 1)
                for h in range(AH):
                    rows = slice(h % 2 * HD, h % 2 * HD + HD)
                    v = [v_tok[:, t, h * HD:(h + 1) * HD] for t in range(TT)]
                    o = ps[rows, 4, h // 2 * SEQ:(h // 2 + 1) * SEQ]
                    for q, k in ((0, 0), (1, 0), (1, 1)):
                        b, c = block_of(h, q, k)
                        last = mm(o[:, q * P:(q + 1) * P], v[k], probs_t[:, b, c:c + P], start=k == 0, stop=k == q)
                last.then_inc(pv_done, 1)
                pe.wait_ge(yblo_ready, layer + 1)
                row_unit(layer, U_YB, U_YB % SLOTS, xt(2), 0, False, True, acc_half)

                ffn(layer, 1, U_FFN2, 2)
                row_unit(layer, U_PE, U_PE % SLOTS,
                         lambda k, t: tuple(e[:, E_PT - E_SPLIT + k * SEQ + t * P:E_PT - E_SPLIT + k * SEQ + (t + 1) * P]
                                            for e in (ex_hi, ex_lo)), 4, True, True)
                turn_x(layer, 3, 0)
                for i in range(3):
                    if i == 2:
                        turn_x(layer, 3, 1)
                    unit_ready(layer, U_GATE + i)
                    if i == 0:
                        xt_whole(layer, 3, 0)
                    row_tile((U_GATE + i) % SLOTS, 0, xt(2 * i), 0, i == 0, False)
                xt_whole(layer, 3, 1)
                for i in range(3):
                    row_tile((U_GATE + i) % SLOTS, 1, xt(2 * i), 0, i == 0, False).then_inc(unit_done, 1)
                row_unit(layer, U_GATE + 3, (U_GATE + 3) % SLOTS, xt(6), 0, False, True, acc_half)

        @block.scalar
        def _(act):
            fn = nc.scalar.activation
            flat2 = "p a b -> p (a b)"

            def make_hi(layer, n, slot, nth):
                act.wait_ge(raw_in[slot], (layer * SLOT_UNITS[slot] + nth + 1) * 16)
                act.wait_ge(unit_done, layer * UNITS + free_count(n))
                fn(w_hi[:, slot, :], w_raw[:, slot, :], ACT.Copy).then_inc(hi_ready, 1)

            def hi_of(layer, n):
                make_hi(layer, n, n % SLOTS, n // SLOTS)

            def square(layer, i, t):
                act.wait_ge(mean_ready, (layer * 3 + i) * 2 + t + 1)
                fn(ps[:, 2 * t:2 * t + 2, :].rearrange("p b c -> p (b c)"), x_new[:, t, :], ACT.Square,
                   bias=nmean[:, t:t + 1], accum_out=ssq[:, t:t + 1]).then_inc(ssq_ready, 1)

            def root(layer, i, t):
                act.wait_ge(var_ready, (layer * 3 + i) * 2 + t + 1)
                fn(rstd[:, t:t + 1], rstd[:, t:t + 1], ACT.Sqrt).then_inc(std_ready, 1)

            def xt_hi_of(layer, j, t):
                act.wait_ge(xt_turned, (layer * 4 + j) * 2 + t + 1)
                fn(xt_hi[:, t, :, :].rearrange("p k c -> p (k c)"),
                   ps[:, 2 * t:2 * t + 2, :].rearrange("p b c -> p (b c)"), ACT.Copy).then_inc(xthi_ready, 1)

            def norm_and_turn(layer, i, next_unit):
                fn(warm[:, 0:1], warm[:, 1:2], ACT.Sqrt)
                square(layer, i, 0)
                root(layer, i, 0)
                hi_of(layer, next_unit)
                square(layer, i, 1)
                xt_hi_of(layer, i + 1, 0)
                root(layer, i, 1)
                xt_hi_of(layer, i + 1, 1)

            def silu(done_first, done_second):
                act.wait_ge(gu_half, done_first)
                fn(silu_g[:, 0, :], ps[:, GU, 0:FC], ACT.Silu).then_inc(silu_ready, 1)
                act.wait_ge(unit_done, done_second)
                fn(silu_g[:, 1, :], ps[:, GU + 1, 0:FC], ACT.Silu).then_inc(silu_ready, 1)

            def ht_hi_of(chunk, dst):
                act.wait_ge(ht_turned, chunk + 1)
                fn(dst[:, :, :, :].rearrange("p k t c -> p (k t c)"), ps[:, HT, :], ACT.Copy).then_inc(hthi_ready, 1)

            def ffn(layer, f, base):
                chunk0 = (layer * 2 + f) * CHUNKS
                silu(chunk0 + 1, layer * UNITS + base + 2 + SLOTS)
                hi_of(layer, base + 3)
                ht_hi_of(chunk0, ht_hi)
                hi_of(layer, base + 4)
                with act.Fori(1, CHUNKS - 1) as c:
                    make_hi(layer, c * 3 + (base + 2), 2, c + base // 3)
                    silu(chunk0 + c + 1, layer * UNITS + c * 3 + base + 1 + SLOTS)
                    make_hi(layer, c * 3 + (base + 3), 0, c + (base // 3 + 1))
                    ht_hi_of(chunk0 + c, ht_hi)
                    make_hi(layer, c * 3 + (base + 4), 1, c + (base // 3 + 1))
                c = CHUNKS - 1
                hi_of(layer, base + 3 * c + 2)
                silu(chunk0 + c + 1, layer * UNITS + c * 3 + base + 1 + SLOTS)
                ht_hi_of(chunk0 + c, hz_hi)
                hi_of(layer, base + 3 * c + 3)
                hi_of(layer, base + 3 * c + 4)

            act.dma_start(cst[:, :], consts).then_inc(cst_loaded, 16)
            act.wait_ge(pads_ready, 2)
            with act.Fori(0, DEPTH) as layer:
                hi_of(layer, 0)
                xt_hi_of(layer, 0, 0)
                hi_of(layer, 1)
                xt_hi_of(layer, 0, 1)
                hi_of(layer, 2)
                act.wait_ge(ex_in, layer * 16 + 16)
                fn(ex_hi[:, :], ex[:, E_SPLIT:E_ALL], ACT.Copy).then_inc(exhi_ready, 1)
                ffn(layer, 0, U_FFN1)
                norm_and_turn(layer, 0, U_V + 2)

                def done(n):
                    act.wait_ge(unit_done, layer * UNITS + n + 1 + SLOTS)

                def conv_in(i, bank):
                    act.wait_ge(pads_ready, layer + 3)
                    fn(big[:, 2 * i:2 * i + 2, 3:3 + SEQ], ps[:, bank, :].rearrange("p (m s) -> p m s", m=2),
                       ACT.Copy)
                    for m in range(2 * i, 2 * i + 2):
                        last = fn(xbc[:, m, :], ps[:, bank, m % 2 * SEQ:(m % 2 + 1) * SEQ], ACT.Identity,
                                  bias=ex[:, E_CB + m:E_CB + m + 1], scale=ex[:, E_CW + 24 + m:E_CW + 25 + m])
                    last.then_inc(conv_first, 1)

                def conv_out(i):
                    act.wait_ge(conv_ready, layer * 5 + i + 1)
                    fn(xbc[:, 2 * i:2 * i + 2, :], xbc[:, 2 * i:2 * i + 2, :], ACT.Silu).then_inc(xbc_ready, 1)

                done(U_V)
                fn(v_tok[:, :, :].rearrange(flat2), ps[:, 7, :], ACT.Copy).then_inc(v_out, 1)
                hi_of(layer, U_V + 3)
                done(U_Z)
                hi_of(layer, U_Z + 3)
                done(U_Z + 1)
                fn(z_tok[:, :, :], ps[:, 4:6, :], ACT.Silu).then_inc(z_out, 1)
                hi_of(layer, U_Z + 4)
                act.wait_ge(abs_ready, layer + 1)
                fn(sp[:, 1, :], sp[:, 1, :], ACT.Exp, scale=-1.0).then_inc(act_step, 1)
                act.wait_ge(act_step, layer * ACT_STEPS + 1)
                fn(expa[:, :], ex[0:ROWS, E_ALOG:E_ALOG + 1], ACT.Exp).then_inc(exp_ready, 1)
                done(U_XS)
                conv_in(0, 1)
                hi_of(layer, U_XS + 3)
                done(U_XS + 1)
                conv_in(1, 6)
                hi_of(layer, U_XS + 4)
                act.wait_ge(cum_ready, layer + 1)
                fn(cum_hi[:, :], cum[:, :], ACT.Copy).then_inc(cumhi_ready, 1)
                done(U_B)
                conv_in(2, 5)
                hi_of(layer, U_B + 3)
                conv_out(0)
                conv_out(1)
                done(U_C)
                conv_in(3, 6)
                hi_of(layer, U_C + 3)
                conv_out(2)
                act.wait_ge(cum_turned, layer + 1)
                fn(cum_tok[:, :, :, :].rearrange("p a b c -> p (a b c)"), ps[:, 0, 0:TT * 2 * ROWS], ACT.Copy)
                fn(ncum_tok[:, :, :], ps[:, 0, 0:TT * 2 * ROWS].rearrange("p (a b c) -> p a b c", a=TT, b=2)[:, :, 0, :],
                   ACT.Copy, scale=-1.0).then_inc(act_step, 1)
                conv_out(3)
                fn(ecum[:, :], ps[:, 0, 2 * ROWS + AH:3 * ROWS], ACT.Exp).then_inc(cumtok_ready, 1)

                def decays(heads):
                    for h in heads:
                        for c in range(TT):
                            fn(decay[:, h, c, :], ps[:, (2, 3, 1, 4)[h // 2], (h % 2 * TT + c) * P:(h % 2 * TT + c + 1) * P],
                               ACT.Exp, bias=ncum_tok[:, c, AH + h:AH + h + 1]).then_inc(decay_ready, 1)

                act.wait_ge(act_step, layer * ACT_STEPS + 2)
                act.wait_ge(conv_ready, layer * 5 + 4)
                decays(range(0, 4))
                done(U_U)
                fn(u_raw[:, :, 3:3 + SEQ], ps[:, 7, :].rearrange("p (m s) -> p m s", m=2), ACT.Copy)
                for m in range(2):
                    last = fn(uc[:, m, :], ps[:, 7, m * SEQ:(m + 1) * SEQ], ACT.Identity,
                              bias=ex[:, E_UB + m:E_UB + m + 1], scale=ex[:, E_UW + 6 + m:E_UW + 7 + m])
                last.then_inc(conv_first, 1)
                hi_of(layer, U_U + 3)
                act.wait_ge(b_turned, layer + 1)
                fn(b_tok[:, :, :].rearrange(flat2), ps[:, 0, 0:256], ACT.Copy).then_inc(b_out, 1)
                decays(range(4, 8))
                fn(qf[HD:HD + ROWS, :, :], cum[:, :].unsqueeze(1).to_broadcast([ROWS, AH, SEQ]), ACT.Copy)
                fn(kf[96:96 + ROWS, :, :], cum[:, :].unsqueeze(1).to_broadcast([ROWS, AH, SEQ]), ACT.Copy,
                   scale=-1.0).then_inc(f_rows_ready, 1)
                done(U_G)
                fn(gate_g[:, :, :].rearrange(flat2), ps[:, 7, :], ACT.Gelu_apprx_tanh).then_inc(g_out, 1)
                act.wait_ge(cb_done, layer + 1)
                fn(cb[:, :, :, :].rearrange("p a b c -> p (a b c)"), ps[:, 2, :], ACT.Copy).then_inc(cb_out, 1)
                hi_of(layer, U_G + 3)
                act.wait_ge(gates_done, layer + 1)
                for i, (bank, b) in enumerate(((3, E_BA), (0, E_BX))):
                    for m in range(2):
                        last = fn(lru[:, i, m, :], ps[:, bank, m * SEQ:(m + 1) * SEQ], ACT.Sigmoid,
                                  bias=ex[:, b + m:b + m + 1])
                last.then_inc(gates_ready, 1)
                act.wait_ge(gates_ready, layer + 1)
                for m in range(2):
                    fn(lru[:, 2, m, :], lru[:, 0, m, :], ACT.Exp, scale=c8[:, 0, m:m + 1])
                for m in range(2):
                    last = fn(lru[:, 3, m, :], lru[:, 0, m, :], ACT.Tanh, scale=c8[:, 1, m:m + 1])
                last.then_inc(aa_ready, 1)

                def head_rows(dst, bank, scale, signal):
                    for r in range(2):
                        last = fn(dst[0:HD, r:AH:2, :], ps[r * HD:(r + 1) * HD, bank, :].rearrange("p (a s) -> p a s", a=2),
                                  ACT.Copy, scale=scale)
                    last.then_inc(signal, 1)

                done(U_Q)
                head_rows(qf, 5, HD ** -0.5, q_out)
                hi_of(layer, U_Q + 3)
                act.wait_ge(one_a2_ready, layer + 1)
                fn(lru[:, 3, :, :], lru[:, 3, :, :], ACT.Sqrt).then_inc(root_ready, 1)
                done(U_K)
                head_rows(kf, 6, 1.0, k_out)
                act.wait_ge(state_done, layer + 1)
                fn(state[:, :], ps[:, 2, :], ACT.Copy).then_inc(state_ready, 1)
                hi_of(layer, U_K + 3)

                def split_hi(kt0, n, src, signal):
                    fn(xt_hi[:, :, kt0:kt0 + n, :], src, ACT.Copy).then_inc(signal, 1)

                act.wait_ge(ya_ready, layer + 1)
                split_hi(0, 2, lru[:, 1, :, :].rearrange("p m (t c) -> p t m c", t=TT), yahi_ready)
                act.wait_ge(yz_ready, layer + 1)
                for t in range(TT):
                    for g in range(NG):
                        i = t * NG + g
                        fn(big[:, i, 0:256], y_tok[:, t, g * 256:(g + 1) * 256], ACT.Square,
                           accum_out=msq[:, i:i + 1]).then_inc(msq_ready, 1)
                act.wait_ge(ms_ready, layer + 1)
                fn(msq[:, :], msq[:, :], ACT.Sqrt).then_inc(rms_ready, 1)
                act.wait_ge(nmax_ready, layer + 1)
                for h in range(AH):
                    for q in range(2):
                        b, c = block_of(h, q, 0)
                        last = fn(probs[:, b, c:c + (q + 1) * P], ps[:, 5 + b, c:c + (q + 1) * P], ACT.Exp,
                                  bias=nmax[:, q, h:h + 1], accum_out=rsum[:, q, h:h + 1])
                last.then_inc(probs_raw, 1)
                for t in range(TT):
                    act.wait_ge(yc_turned, layer * 2 + t + 1)
                    fn(xt_hi[:, t, 4:8, :].rearrange("p k c -> p (k c)"), ps[:, 4, :], ACT.Copy).then_inc(ychi_ready, 1)
                hi_of(layer, U_YA + 3)
                act.wait_ge(probs_turned, layer + 1)
                fn(probs_t, ps[:, 5:8, :], ACT.Copy).then_inc(probst_ready, 1)
                hi_of(layer, U_YC + 3)
                hi_of(layer, U_YC + 4)
                act.wait_ge(pv_done, layer + 1)
                split_hi(2, 2, ps[:, 4, :].rearrange("p (m t c) -> p t m c", m=2, t=TT), ybhi_ready)
                norm_and_turn(layer, 1, U_YB + 3)
                ffn(layer, 1, U_FFN2)
                norm_and_turn(layer, 2, U_PE + 2)
                hi_of(layer, U_PE + 3)
                hi_of(layer, U_GATE + 3)
                fn(warm[:, 0:1], warm[:, 1:2], ACT.Sigmoid)
                for t in range(TT):
                    act.wait_ge(biased_ready, layer * 2 + t + 1)
                    fn(x_new[:, t, :], x_new[:, t, :], ACT.Sigmoid).then_inc(sig_ready, 1)

        @block.vector
        def _(dve):
            v = nc.vector

            def make_lo(layer, n, slot):
                dve.wait_ge(hi_ready, layer * UNITS + n + 1)
                v.tensor_tensor(w_lo[:, slot, :], w_raw[:, slot, :], w_hi[:, slot, :].bitcast(f32),
                                ALU.subtract).then_inc(lo_ready, 1)

            def lo_of(layer, n):
                make_lo(layer, n, n % SLOTS)

            def xt_lo_of(layer, j, t):
                dve.wait_ge(xthi_ready, (layer * 4 + j) * 2 + t + 1)
                v.tensor_tensor(xt_lo[:, t, :, :].rearrange("p k c -> p (k c)"),
                                ps[:, 2 * t:2 * t + 2, :].rearrange("p b c -> p (b c)"),
                                xt_hi[:, t, :, :].rearrange("p k c -> p (k c)").bitcast(f32),
                                ALU.subtract).then_inc(xt_ready, 1)

            def hidden(chunk):
                for t in range(TT):
                    dve.wait_ge(silu_ready, chunk * 2 + t + 1)
                    v.scalar_tensor_tensor(out=h_tok[:, t, :], in0=silu_g[:, t, :], scalar=0.5,
                                           in1=ps[:, GU + t, FC:2 * FC], op0=ALU.mult, op1=ALU.mult).then_inc(h_ready, 1)

            def ht_lo_of(chunk, dst, hi):
                dve.wait_ge(hthi_ready, chunk + 1)
                v.tensor_tensor(dst[:, :, :, :].rearrange("p k t c -> p (k t c)"), ps[:, HT, :],
                                hi[:, :, :, :].rearrange("p k t c -> p (k t c)").bitcast(f32),
                                ALU.subtract).then_inc(ht_ready, 1)

            def ffn(layer, f, base):
                chunk0 = (layer * 2 + f) * CHUNKS
                hidden(chunk0)
                lo_of(layer, base + 3)
                ht_lo_of(chunk0, ht_lo, ht_hi)
                lo_of(layer, base + 4)
                with dve.Fori(1, CHUNKS - 1) as c:
                    make_lo(layer, c * 3 + (base + 2), 2)
                    hidden(chunk0 + c)
                    make_lo(layer, c * 3 + (base + 3), 0)
                    ht_lo_of(chunk0 + c, ht_lo, ht_hi)
                    make_lo(layer, c * 3 + (base + 4), 1)
                c = CHUNKS - 1
                lo_of(layer, base + 3 * c + 2)
                hidden(chunk0 + c)
                ht_lo_of(chunk0 + c, hz_lo, hz_hi)
                lo_of(layer, base + 3 * c + 3)
                lo_of(layer, base + 3 * c + 4)

            v.memset(u_raw[:, :, 0:3], 0.0).then_inc(pads_ready, 1)
            v.memset(warm[:, :], 1.0).then_inc(pads_ready, 1)
            v.memset(sp[:, :, :], 0.0).then_inc(lo_ready, SLOTS)
            v.memset(msq[:, :], 0.0).then_inc(unit_done, SLOTS)
            v.memset(rstd[:, :], 0.0).then_inc(gain_used, 1)
            v.memset(qf[:, :, :], 0.0).then_inc(masks_ready, 1)
            v.memset(kf[:, :, :], 0.0).then_inc(masks_ready, 1)
            for t in range(TT):
                dve.wait_ge(x_loaded[t], 16)
                v.memset(ssq[:, t:t + 1], 0.0).then_inc(x_ready, 1)

            with dve.Fori(0, DEPTH) as layer:
                steps = [0]

                def step(ins):
                    steps[0] += 1
                    ins.then_inc(dve_step, 1)
                    dve.wait_ge(dve_step, layer * DVE_STEPS + steps[0])

                def done(n):
                    dve.wait_ge(unit_done, layer * UNITS + n + 1 + SLOTS)

                def norm_sums(i, t, last_unit):
                    if t == 0:
                        dve.wait_ge(acc_half, layer * 4 + i + 1)
                    else:
                        done(last_unit)
                    step(v.scalar_tensor_tensor(out=x_new[:, t, :], in0=x_tok[:, t, :], scalar=ALPHA,
                                                in1=ps[:, 2 * t:2 * t + 2, :].rearrange("p b c -> p (b c)"),
                                                op0=ALU.mult, op1=ALU.add, accum_out=nmean[:, t:t + 1]))
                    v.tensor_scalar(nmean[:, t:t + 1], nmean[:, t:t + 1], -1.0 / D, None, ALU.mult)\
                        .then_inc(mean_ready, 1)
                    dve.wait_ge(mean_ready, (layer * 3 + i) * 2 + t + 1)
                    v.scalar_tensor_tensor(out=x_tok[:, t, :], in0=x_new[:, t, :], scalar=nmean[:, t:t + 1],
                                           in1=gain[:, 0, :], op0=ALU.add, op1=ALU.mult)
                    dve.wait_ge(ssq_ready, (layer * 3 + i) * 2 + t + 1)
                    v.tensor_scalar(rstd[:, t:t + 1], ssq[:, t:t + 1], 1.0 / D, EPS, ALU.mult, ALU.add)\
                        .then_inc(var_ready, 1)

                def norm_scale(i, t):
                    dve.wait_ge(std_ready, (layer * 3 + i) * 2 + t + 1)
                    step(v.reciprocal(rstd[:, t:t + 1], rstd[:, t:t + 1]))
                    v.scalar_tensor_tensor(out=x_tok[:, t, :], in0=x_tok[:, t, :], scalar=rstd[:, t:t + 1],
                                           in1=gain[:, 1, :], op0=ALU.mult, op1=ALU.add).then_inc(x_ready, 1)

                def norm_and_turn(i, last_unit, next_unit):
                    dve.wait_ge(gain_in, (layer * 4 + i + 1) * 16)
                    norm_sums(i, 0, last_unit)
                    norm_scale(i, 0)
                    norm_sums(i, 1, last_unit)
                    xt_lo_of(layer, i + 1, 0)
                    norm_scale(i, 1)
                    lo_of(layer, next_unit)
                    dve.wait_ge(x_ready, (layer * 4 + i) * 2 + 4)
                    v.memset(nmean[:, 0:1], 0.0).then_inc(gain_used, 1)
                    xt_lo_of(layer, i + 1, 1)

                lo_of(layer, 0)
                xt_lo_of(layer, 0, 0)
                lo_of(layer, 1)
                xt_lo_of(layer, 0, 1)
                lo_of(layer, 2)
                dve.wait_ge(exhi_ready, layer + 1)
                v.tensor_tensor(ex_lo[:, :], ex[:, E_SPLIT:E_ALL], ex_hi[:, :].bitcast(f32),
                                ALU.subtract).then_inc(exlo_ready, 1)
                ffn(layer, 0, U_FFN1)
                norm_and_turn(0, U_FFN1 + FFN_UNITS - 1, U_V + 2)

                dve.wait_ge(cst_loaded, 16)
                heads = cst[0:ROWS, C_ID + AH:C_ID + ROWS]
                v.tensor_copy(id_r[:, :], ident)
                v.tensor_copy(ssd_mask[:, :].rearrange("p (a b) -> p a b", a=4),
                              cst[:, C_SSD:C_SSD + P].unsqueeze(1).to_broadcast([P, 4, P]))
                v.tensor_copy(att_mask[:, :], cst[:, C_ATT:C_ATT + P])
                v.tensor_copy(sel[:, :, :], heads.unsqueeze(2).to_broadcast([ROWS, SH, P]))
                dve.wait_ge(masks_ready, 2)
                for rows in (qf[96:96 + ROWS, :, :], kf[HD:HD + ROWS, :, :]):
                    v.tensor_copy(rows, cst[0:ROWS, C_ID:C_ID + AH].unsqueeze(2).to_broadcast([ROWS, AH, SEQ]))
                v.memset(big[:, :, 0:3], 0.0).then_inc(pads_ready, 1)
                for n in (U_V, U_Z, U_Z + 1):
                    lo_of(layer, n + 3)

                v.tensor_scalar(sp[:, 0, SEQ:SEQ + 2], ex[:, E_LAM:E_LAM + 2], -1.0, None, ALU.mult)
                dve.wait_ge(fd_done, layer + 1)
                step(v.tensor_scalar(sp[0:ROWS, 0, 0:SEQ], ps[0:ROWS, 0, 0:SEQ], ex[0:ROWS, E_BIAS:E_BIAS + 1],
                                     ex[0:ROWS, E_SIGN:E_SIGN + 1], ALU.add, ALU.mult))
                v.scalar_tensor_tensor(out=sp[:, 1, :], in0=sp[:, 0, :], scalar=-1.0, in1=sp[:, 0, :],
                                       op0=ALU.mult, op1=ALU.max).then_inc(abs_ready, 1)
                dve.wait_ge(exp_ready, layer + 1)
                step(v.tensor_scalar(sp[:, 2, :], sp[:, 1, :], 2.0, None, ALU.add))
                step(v.reciprocal(sp[:, 2, :], sp[:, 2, :]))
                step(v.tensor_tensor(sp[:, 1, :], sp[:, 1, :], sp[:, 2, :], ALU.mult))
                step(v.tensor_tensor(sp[:, 3, :], sp[:, 1, :], sp[:, 1, :], ALU.mult))
                step(v.tensor_scalar(sp[:, 4, :], sp[:, 3, :], 1.0 / 17, None, ALU.mult))
                for k in (15, 13, 11, 9, 7, 5, 3):
                    step(v.scalar_tensor_tensor(out=sp[:, 4, :], in0=sp[:, 4, :], scalar=1.0 / k, in1=sp[:, 3, :],
                                                op0=ALU.add, op1=ALU.mult))
                step(v.scalar_tensor_tensor(out=sp[:, 4, :], in0=sp[:, 4, :], scalar=1.0, in1=sp[:, 1, :],
                                            op0=ALU.add, op1=ALU.mult))
                step(v.tensor_scalar(sp[:, 4, :], sp[:, 4, :], 2.0, None, ALU.mult))
                step(v.scalar_tensor_tensor(out=sp[:, 5, :], in0=sp[:, 0, :], scalar=0.0, in1=sp[:, 4, :],
                                            op0=ALU.max, op1=ALU.add))
                v.tensor_scalar(c8[:, 0, :], sp[:, 5, SEQ:SEQ + 2], -8.0, None, ALU.mult)
                v.tensor_scalar(c8[:, 1, :], sp[:, 5, SEQ:SEQ + 2], 8.0, None, ALU.mult)
                step(v.tensor_scalar(sp[0:ROWS, 2, 0:SEQ], sp[0:ROWS, 5, 0:SEQ], expa[:, 0:1], -1.0,
                                     ALU.mult, ALU.mult))
                v.tensor_tensor_scan(cum[:, :], cst[0:ROWS, C_RESET:C_RESET + SEQ], sp[0:ROWS, 2, 0:SEQ], 0.0,
                                     ALU.mult, ALU.add).then_inc(cum_ready, 1)

                def conv(dst, src, tiles, taps, count):
                    for j in range(3):
                        for m in tiles:
                            ins = v.scalar_tensor_tensor(out=dst[:, m, :], in0=src[:, m, j:j + SEQ],
                                                         scalar=ex[:, taps + j * count + m:taps + j * count + m + 1],
                                                         in1=dst[:, m, :], op0=ALU.mult, op1=ALU.add)
                        if j < 2:
                            step(ins)
                    ins.then_inc(conv_ready, 1)

                for i in range(4):
                    dve.wait_ge(conv_first, layer * 5 + i + 1)
                    conv(xbc, big, (2 * i, 2 * i + 1), E_CW, 8)
                    if i == 1:
                        dve.wait_ge(cumhi_ready, layer + 1)
                        v.tensor_tensor(cum_lo[:, :], cum[:, :], cum_hi[:, :].bitcast(f32), ALU.subtract)\
                            .then_inc(cumsplit_ready, 1)
                    lo_of(layer, U_XS + i + 3)
                dve.wait_ge(conv_first, layer * 5 + 5)
                conv(uc, u_raw, (0, 1), E_UW, 2)
                dve.wait_ge(xs_turned, layer + 1)
                dve.wait_ge(cumtok_ready, layer + 1)
                dve.wait_ge(mix_in, layer * 16 + 16)
                for t in range(TT):
                    xs = ps[:, 5 + t, :].rearrange("p (h d) -> p h d", h=SH)
                    v.tensor_tensor(xdt[:, t, :, :], xs, cum_tok[:, t, 1, AH:ROWS].unsqueeze(2).to_broadcast([P, SH, HD]),
                                    ALU.mult)
                    ins = v.tensor_tensor(y_tok[:, t, :].rearrange("p (h d) -> p h d", h=SH), xs,
                                          mix[:, 512:520].unsqueeze(2).to_broadcast([P, SH, HD]), ALU.mult)
                ins.then_inc(xs_used, 1)
                lo_of(layer, U_U + 3)
                dve.wait_ge(decay_ready, (layer + 1) * 16)
                dve.wait_ge(xs_used, layer + 1)
                v.tensor_tensor(xdd[:, :, :], xdt[:, 0, :, :], decay[:, :, 0, P - 1:P].to_broadcast([P, SH, HD]),
                                ALU.mult).then_inc(xdd_ready, 1)
                dve.wait_ge(xdd_ready, layer + 1)
                dve.wait_ge(cb_out, layer + 1)
                for g in range(NG):
                    for c in range(TT):
                        d = decay[:, 4 * g:4 * g + 4, c, :]
                        v.tensor_tensor(d, d, cb[:, g, c, :].unsqueeze(1).to_broadcast([P, 4, P]),
                                        ALU.mult).then_inc(m_ready, 1)
                lo_of(layer, U_G + 3)
                dve.wait_ge(aa_ready, layer + 1)
                r, ig, a, th = (lru[:, i, :, :] for i in range(4))
                step(v.tensor_tensor(r, a, a, ALU.mult))
                v.scalar_tensor_tensor(out=th, in0=r, scalar=1.0, in1=th, op0=ALU.add, op1=ALU.mult)\
                    .then_inc(one_a2_ready, 1)
                step(v.tensor_tensor(ig, ig, uc[:, :, :], ALU.mult))
                dve.wait_ge(root_ready, layer + 1)
                step(v.tensor_tensor(ig, ig, th, ALU.mult))
                for m in range(2):
                    ins = v.tensor_tensor_scan(r[:, m, :], a[:, m, :], ig[:, m, :], 0.0, ALU.mult, ALU.add)
                step(ins)
                v.tensor_tensor(ig, r, gate_g[:, :, :], ALU.mult).then_inc(ya_ready, 1)
                lo_of(layer, U_Q + 3)
                dve.wait_ge(ydiag_done, layer + 1)
                step(v.tensor_tensor(y_tok[:, :, :], y_tok[:, :, :], ps[:, 0:2, :], ALU.add))
                dve.wait_ge(yoff_done, layer + 1)
                step(v.tensor_tensor(y_off[:, :, :], ps[:, 3, :].rearrange("p (h d) -> p h d", h=SH),
                                     ecum[:, :].unsqueeze(2).to_broadcast([P, SH, HD]), ALU.mult))
                step(v.tensor_tensor(y_tok[:, 1, :], y_tok[:, 1, :], y_off[:, :, :].rearrange("p h d -> p (h d)"), ALU.add))
                v.tensor_tensor(y_tok[:, :, :], y_tok[:, :, :], z_tok[:, :, :], ALU.mult).then_inc(yz_ready, 1)

                def split_lo(kt0, n, src, signal):
                    v.tensor_tensor(xt_lo[:, :, kt0:kt0 + n, :], src, xt_hi[:, :, kt0:kt0 + n, :].bitcast(f32),
                                    ALU.subtract).then_inc(signal, 1)

                dve.wait_ge(yahi_ready, layer + 1)
                split_lo(0, 2, ig.rearrange("p m (t c) -> p t m c", t=TT), yalo_ready)
                dve.wait_ge(logits_done, layer + 1)
                v.tensor_reduce(nmax[:, 0, :], ps[:, 5, :].rearrange("p (h k) -> p h k", h=AH), AX.X, ALU.max)
                step(v.tensor_reduce(nmax[:, 1, :], ps[:, 6:8, :].rearrange("p b (h k) -> p (b h) k", h=2), AX.X, ALU.max))
                v.tensor_scalar(nmax[:, :, :], nmax[:, :, :], -1.0, None, ALU.mult).then_inc(nmax_ready, 1)
                dve.wait_ge(msq_ready, layer * 4 + 4)
                v.tensor_scalar(msq[:, :], msq[:, :], 1.0 / 256, EPS, ALU.mult, ALU.add).then_inc(ms_ready, 1)
                dve.wait_ge(rms_ready, layer + 1)
                step(v.reciprocal(msq[:, :], msq[:, :]))
                for t in range(TT):
                    for g in range(NG):
                        i, c = t * NG + g, slice(g * 256, (g + 1) * 256)
                        ins = v.scalar_tensor_tensor(out=y_tok[:, t, c], in0=y_tok[:, t, c], scalar=msq[:, i:i + 1],
                                                     in1=mix[:, c], op0=ALU.mult, op1=ALU.mult)
                    ins.then_inc(yn_ready, 1)
                lo_of(layer, U_K + 3)
                dve.wait_ge(probs_raw, layer + 1)
                step(v.reciprocal(rsum[:, :, :], rsum[:, :, :]))
                p0 = probs[:, 0, :].rearrange("p (h k) -> p h k", h=AH)
                p1 = probs[:, 1:3, :].rearrange("p b (h k) -> p (b h) k", h=2)
                v.tensor_tensor(p0, p0, rsum[:, 0, :].unsqueeze(2).to_broadcast([P, AH, P]), ALU.mult)
                v.tensor_tensor(p1, p1, rsum[:, 1, :].unsqueeze(2).to_broadcast([P, AH, 2 * P]), ALU.mult)\
                    .then_inc(probs_ready, 1)
                for t in range(TT):
                    dve.wait_ge(ychi_ready, layer * 2 + t + 1)
                    v.tensor_tensor(xt_lo[:, t, 4:8, :].rearrange("p k c -> p (k c)"), ps[:, 4, :],
                                    xt_hi[:, t, 4:8, :].rearrange("p k c -> p (k c)").bitcast(f32),
                                    ALU.subtract).then_inc(yclo_ready, 1)
                for n in range(U_YA, U_YB):
                    lo_of(layer, n + 3)
                dve.wait_ge(ybhi_ready, layer + 1)
                split_lo(2, 2, ps[:, 4, :].rearrange("p (m t c) -> p t m c", m=2, t=TT), yblo_ready)
                norm_and_turn(1, U_YB, U_YB + 3)
                ffn(layer, 1, U_FFN2)
                norm_and_turn(2, U_FFN2 + FFN_UNITS - 1, U_PE + 2)
                lo_of(layer, U_PE + 3)
                lo_of(layer, U_GATE + 3)
                dve.wait_ge(gain_in, (layer * 4 + 4) * 16)

                def biased(t):
                    v.tensor_tensor(x_new[:, t, :], ps[:, 2 * t:2 * t + 2, :].rearrange("p b c -> p (b c)"),
                                    gain[:, 0, :], ALU.add).then_inc(biased_ready, 1)

                def gated(t):
                    dve.wait_ge(sig_ready, layer * 2 + t + 1)
                    step(v.tensor_tensor(x_new[:, t, :], x_new[:, t, :],
                                         ps[:, 4 + 2 * t:6 + 2 * t, :].rearrange("p b c -> p (b c)"), ALU.mult))
                    v.tensor_tensor(x_tok[:, t, :], x_tok[:, t, :], x_new[:, t, :], ALU.add).then_inc(x_ready, 1)

                dve.wait_ge(acc_half, layer * 4 + 4)
                biased(0)
                done(U_GATE + 3)
                biased(1)
                gated(0)
                gated(1)
                dve.wait_ge(x_ready, layer * 8 + 10)
                v.memset(nmean[:, 0:1], 0.0).then_inc(gain_used, 1)
                assert steps[0] == DVE_STEPS, steps[0]


def lay_out(i):
    import numpy as np
    f = np.float32
    ws = np.zeros((DEPTH, UNITS, P, W), f)

    def tiles(w):
        return w.reshape(w.shape[0] // P, P, w.shape[1]).transpose(1, 0, 2)

    def flat(a):
        return a.reshape(P, -1)

    for l in range(DEPTH):
        for base, name in ((U_FFN1, "ffn1"), (U_FFN2, "ffn2")):
            wg, wu = tiles(i[f"{name}_wg"][l]), tiles(i[f"{name}_wu"][l])
            wd = tiles(i[f"{name}_wd"][l])
            n = base
            for c in range(CHUNKS + 1):
                if c < CHUNKS:
                    cols = slice(c * FC, (c + 1) * FC)
                    for half in range(2):
                        k = slice(4 * half, 4 * half + 4)
                        ws[l, n] = flat(np.stack([wg[:, k, cols], wu[:, k, cols]], axis=2))
                        n += 1
                if c > 0:
                    ws[l, n] = flat(wd[:, 2 * (c - 1):2 * c, :])
                    n += 1
        wi = tiles(i["w_in"][l])
        for n, col in ((U_XS, 1796), (U_XS + 1, 2052), (U_B, 2308), (U_C, 2564), (U_Q, 512), (U_K, 768), (U_V, 1024),
                       (U_U, 0), (U_G, 256)):
            ws[l, n] = flat(wi[:, :, col:col + 256])
        for half in range(2):
            ws[l, U_Z + half] = flat(wi[:, 4 * half:4 * half + 4, 1284:1796])
        for name, units in (("w_out", (U_YA, U_YB, U_YC, U_YC + 1)), ("pe_gate_w", range(U_GATE, U_GATE + 4)),
                            ("pe_proj", (U_PE,))):
            w = tiles(i[name][l])
            for j, n in enumerate(units):
                ws[l, n] = flat(w[:, 2 * j:2 * j + 2, :])

    ex = np.zeros((DEPTH, P, E_ALL), f)
    for l in range(DEPTH):
        ex[l, :, E_CW:E_CW + 32] = i["ssd_conv_w"][l].reshape(32, P).T
        ex[l, :, E_CB:E_CB + 8] = i["ssd_conv_b"][l].reshape(8, P).T
        ex[l, :, E_UW:E_UW + 8] = i["lru_conv_w"][l].reshape(8, P).T
        for at, name in ((E_UB, "lru_conv_b"), (E_BA, "lru_ba"), (E_BX, "lru_bx"), (E_LAM, "lru_lambda")):
            ex[l, :, at:at + 2] = i[name][l].reshape(2, P).T
        ex[l, 0:AH, E_BIAS] = i["fox_bf"][l]
        ex[l, AH:ROWS, E_BIAS] = i["ssd_dt_bias"][l]
        ex[l, 0:AH, E_SIGN] = -1.0
        ex[l, AH:ROWS, E_SIGN] = 1.0
        ex[l, AH:ROWS, E_ALOG] = i["ssd_a_log"][l]
        for at, name in ((E_WA, "lru_wa"), (E_WX, "lru_wx")):
            for h in range(4):
                r, m = h % 2 * HD, h // 2
                ex[l, r:r + HD, at + m * P + r:at + m * P + r + HD] = i[name][l, h]
        wi = tiles(i["w_in"][l])
        fd = ex[l, :, E_FD:E_PT].reshape(P, KT, ROWS)
        ex[l, :, E_FD:E_PT] = flat(np.concatenate([wi[:, :, 1280:1284], wi[:, :, 2820:2828]], axis=2))
        ex[l, :, E_PT:E_ALL] = flat(i["p"][l, 0].T.reshape(PLE // P, P, SEQ).transpose(1, 0, 2))

    norms = np.zeros((DEPTH, 4, 2, D), f)
    for j in range(3):
        norms[:, j, 0] = i[f"ln{j + 1}_g"]
        norms[:, j, 1] = i[f"ln{j + 1}_b"]
    norms[:, 3, 0] = i["pe_gate_b"]
    mix_rows = np.concatenate([i["ssd_norm_g"], i["ssd_d"]], axis=1)

    cst = np.zeros((P, C_ALL), f)
    cst[:, C_ID:C_ID + P] = np.eye(P, dtype=f)
    cst[:, C_SSD:C_SSD + P] = -BIG * np.tril(np.ones((P, P), f), -1)
    cst[:, C_ATT:C_ATT + P] = -BIG * np.triu(np.ones((P, P), f), 1)
    cst[0:ROWS, C_RESET:C_RESET + SEQ] = 1.0
    cst[AH:ROWS, C_RESET + P] = 0.0
    x = i["x"][0].reshape(TT, P, D).transpose(1, 0, 2)
    return {"w_stream": ws, "extras": ex, "norms": norms, "mix_rows": mix_rows, "consts": cst, "x": x}


def kernel(**inputs):
    import numpy as _np
    import concourse.bacc as _bacc
    from concourse import mybir as _mybir
    from concourse.bass_utils import run_bass_kernel_spmd as _run

    nc = _bacc.Bacc("TRN2", target_bir_lowering=False, num_devices=1)
    arrays, args = {}, []
    for name, a in lay_out({k: _np.asarray(v) for k, v in inputs.items()}).items():
        a = _np.ascontiguousarray(a)
        arrays[f"in_{name}_dram"] = a
        args.append(nc.dram_tensor(f"in_{name}_dram", a.shape, _mybir.dt.from_np(a.dtype), kind="ExternalInput").ap())
    args.append(nc.dram_tensor("out_0_dram", (P, TT, D), _mybir.dt.float32, kind="ExternalOutput").ap())
    trunk(nc, *args)
    r = _run(nc, [arrays], core_ids=[0])
    got = r.results[0]["out_0_dram"]
    return got.transpose(1, 0, 2).reshape(1, SEQ, D)
```

```python
import concourse.bass as bass
from concourse import mybir
from contextlib import ExitStack

P = 128
DEPTH, SEQ, D = 2, 256, 1024
TT = SEQ // P
KT = D // P
F = 2816
FC = 256
CHUNKS = F // FC
HD = 64
AH, SH = 4, 8
NG = 2
ROWS = AH + SH
PLE = 256
ALPHA = (2.0 * DEPTH) ** 0.25
EPS = 1e-5
BIG = 1e30

W = 2048
SLOTS = 3
FFN_UNITS = 3 * CHUNKS
U_FFN1 = 0
U_V, U_Z = FFN_UNITS, FFN_UNITS + 1
U_XS, U_B, U_C = U_Z + 2, U_Z + 4, U_Z + 5
U_U, U_G, U_Q, U_K = U_C + 1, U_C + 2, U_C + 3, U_C + 4
U_YA, U_YC, U_YB = U_K + 1, U_K + 2, U_K + 4
U_FFN2 = U_YB + 1
U_PE = U_FFN2 + FFN_UNITS
U_GATE = U_PE + 1
UNITS = U_GATE + 4
SLOT_UNITS = [(UNITS - s + SLOTS - 1) // SLOTS for s in range(SLOTS)]
assert U_FFN1 % SLOTS == 0 and U_FFN2 % SLOTS == 0 and FFN_UNITS % SLOTS == 0 and UNITS % SLOTS == 2

E_CW, E_CB = 0, 32
E_UW, E_UB = 40, 48
E_BA, E_BX, E_LAM = 50, 52, 54
E_BIAS, E_SIGN, E_ALOG = 56, 57, 58
E_WA, E_WX = 60, 316
E_SPLIT = 572
E_FD = E_SPLIT
E_PT = E_FD + KT * ROWS
E_ALL = E_PT + (PLE // P) * SEQ
NSPLIT = E_ALL - E_SPLIT

C_ID, C_SSD, C_ATT, C_RESET = 0, P, 2 * P, 3 * P
C_ALL = C_RESET + SEQ

DVE_STEPS, ACT_STEPS = 52, 1


def free_count(n):
    return {0: 2, 1: 3, 2: 1}.get(n, n + 1) if isinstance(n, int) else n + 1


def trunk(nc, w_stream, extras, norms, mix_rows, consts, x_in_dram, out):
    f32, f32r = mybir.dt.float32, mybir.dt.float32r
    ALU, ACT, AX = mybir.AluOpType, mybir.ActivationFunctionType, mybir.AxisListType

    with ExitStack() as ctx:
        def sb(name, shape, dt=f32):
            return ctx.enter_context(nc.sbuf_tensor(name, shape, dt))

        def sem(name):
            return ctx.enter_context(nc.semaphore(name))

        w_raw = sb("w_raw", [P, SLOTS, W])
        w_hi = sb("w_hi", [P, SLOTS, W], f32r)
        w_lo = sb("w_lo", [P, SLOTS, W], f32r)
        xt_hi = sb("xt_hi", [P, TT, KT, P], f32r)
        xt_lo = sb("xt_lo", [P, TT, KT, P], f32r)
        x_tok = sb("x_tok", [P, TT, D])
        gain = sb("gain", [P, 2, D])
        mix = sb("mix", [P, 520])
        ex = sb("ex", [P, E_ALL])
        ex_hi = sb("ex_hi", [P, NSPLIT], f32r)
        ex_lo = sb("ex_lo", [P, NSPLIT], f32r)
        cst = sb("cst", [P, C_ALL])
        id_r = sb("id_r", [P, P], f32r)
        ssd_mask = sb("ssd_mask", [P, 512], f32r)
        att_mask = sb("att_mask", [P, P], f32r)
        big = sb("big", [P, 8, 260])
        xbc = sb("xbc", [P, 8, SEQ])
        u_raw = sb("u_raw", [P, 2, 260])
        uc = sb("uc", [P, 2, SEQ])
        gate_g = sb("gate_g", [P, 2, SEQ])
        qf = sb("qf", [P, AH, SEQ])
        kf = sb("kf", [P, AH, SEQ])
        v_tok = sb("v_tok", [P, TT, 256])
        z_tok = sb("z_tok", [P, TT, 512])
        sp = sb("sp", [P, 6, 258])
        cum = sb("cum", [ROWS, SEQ])
        cum_hi = sb("cum_hi", [ROWS, SEQ], f32r)
        cum_lo = sb("cum_lo", [ROWS, SEQ], f32r)
        sel = sb("sel", [ROWS, SH, P], f32r)
        expa = sb("expa", [ROWS, 1])
        c8 = sb("c8", [P, 2, 2])
        cum_tok = sb("cum_tok", [P, TT, 2, ROWS])
        ncum_tok = sb("ncum_tok", [P, TT, ROWS])
        ecum = sb("ecum", [P, SH])
        lru = sb("lru", [P, 4, 2, SEQ])
        xdt = sb("xdt", [P, TT, SH, HD])
        xdd = sb("xdd", [P, SH, HD])
        b_tok = sb("b_tok", [P, NG, P])
        cb = sb("cb", [P, NG, TT, P])
        state = sb("state", [P, SH * HD])
        y_tok = sb("y_tok", [P, TT, 512])
        probs = sb("probs", [P, 3, 512])
        nmax = sb("nmax", [P, 2, AH])
        rsum = sb("rsum", [P, 2, AH])
        nmean = sb("nmean", [P, TT])
        ssq = sb("ssq", [P, TT])
        rstd = sb("rstd", [P, TT])
        warm = sb("warm", [P, 2])
        landed = sb("landed", [P, 2 * TT])
        msq = sb("msq", [P, TT * NG])
        ht_hi = sb("ht_hi", [P, 2, TT, P], f32r)
        ht_lo = sb("ht_lo", [P, 2, TT, P], f32r)
        hz_hi = sb("hz_hi", [P, 2, TT, P], f32r)
        hz_lo = sb("hz_lo", [P, 2, TT, P], f32r)
        ps = ctx.enter_context(nc.psum_tensor("ps", [P, 8, 512], f32))

        ident = cst[:, C_ID:C_ID + P]
        decay = big[:, :, :].rearrange("p a b -> p (a b)")[:, 0:SH * TT * P].rearrange(
            "p (h c l) -> p h c l", h=SH, c=TT)
        x_new = big[:, :, :].rearrange("p a b -> p (a b)")[:, 0:TT * D].rearrange("p (t d) -> p t d", t=TT)
        silu_g = probs[:, 0, :].rearrange("p (t f) -> p t f", t=TT)
        h_tok = probs[:, 1, :].rearrange("p (t f) -> p t f", t=TT)
        probs_t = xbc[:, 0:6, :].rearrange("p a b -> p (a b)").rearrange("p (a k) -> p a k", a=3)

        def block_of(h, q, k):
            return (0, h * P) if q == 0 else (1 + h // 2, (h % 2 * 2 + k) * P)
        y_off = xdd
        GU, HT = 4, 6

        x_loaded, cst_loaded = [sem(f"x_loaded{t}") for t in range(TT)], sem("cst_loaded")
        id_loaded = sem("id_loaded")
        raw_in = [sem(f"raw_in{s}") for s in range(SLOTS)]
        hi_ready, lo_ready = sem("hi_ready"), sem("lo_ready")
        unit_done = sem("unit_done")
        ex_in, gain_in, mix_in = sem("ex_in"), sem("gain_in"), sem("mix_in")
        gain_used, mix_used = sem("gain_used"), sem("mix_used")
        exhi_ready, exlo_ready = sem("exhi_ready"), sem("exlo_ready")
        masks_ready, pads_ready = sem("masks_ready"), sem("pads_ready")
        x_half, x_ready = sem("x_half"), sem("x_ready")
        xt_turned, xthi_ready, xt_ready = sem("xt_turned"), sem("xthi_ready"), sem("xt_ready")
        gu_half, silu_ready, h_ready = sem("gu_half"), sem("silu_ready"), sem("h_ready")
        ht_turned, hthi_ready, ht_ready = sem("ht_turned"), sem("hthi_ready"), sem("ht_ready")
        hz_turned, hzhi_ready, hz_ready = sem("hz_turned"), sem("hzhi_ready"), sem("hz_ready")
        gate_half = sem("gate_half")
        acc_half = sem("acc_half")
        fd_done, abs_ready, exp_ready, cum_ready, cumhi_ready = (sem(n) for n in (
            "fd_done", "abs_ready", "exp_ready", "cum_ready", "cumhi_ready"))
        conv_first, conv_ready, xbc_ready = sem("conv_first"), sem("conv_ready"), sem("xbc_ready")
        v_out, z_out, g_out, q_out, k_out = (sem(n) for n in ("v_out", "z_out", "g_out", "q_out", "k_out"))
        cumsplit_ready, f_rows_ready, b_out, cb_out = (sem(n) for n in (
            "cumsplit_ready", "f_rows_ready", "b_out", "cb_out"))
        mean_ready, ssq_ready = sem("mean_ready"), sem("ssq_ready")
        cum_turned, cumtok_ready = sem("cum_turned"), sem("cumtok_ready")
        xs_turned, b_turned, cb_done = sem("xs_turned"), sem("b_turned"), sem("cb_done")
        gates_done, gates_ready, aa_ready = sem("gates_done"), sem("gates_ready"), sem("aa_ready")
        one_a2_ready, root_ready, ya_ready, yahi_ready, yalo_ready = (sem(n) for n in (
            "one_a2_ready", "root_ready", "ya_ready", "yahi_ready", "yalo_ready"))
        y_read = sem("y_read")
        bc_done, decay_ready = sem("bc_done"), sem("decay_ready")
        xs_used, xdd_ready, m_ready = sem("xs_used"), sem("xdd_ready"), sem("m_ready")
        logits_done, nmax_ready, probs_raw, probs_ready = (sem(n) for n in (
            "logits_done", "nmax_ready", "probs_raw", "probs_ready"))
        ydiag_done, state_done, state_ready, yoff_done = (sem(n) for n in (
            "ydiag_done", "state_done", "state_ready", "yoff_done"))
        probs_turned, probst_ready, pv_done, ybhi_ready, yblo_ready = (sem(n) for n in (
            "probs_turned", "probst_ready", "pv_done", "ybhi_ready", "yblo_ready"))
        yz_ready, msq_ready, yn_ready, yc_turned, ychi_ready, yclo_ready = (sem(n) for n in (
            "yz_ready", "msq_ready", "yn_ready", "yc_turned", "ychi_ready", "yclo_ready"))
        var_ready, std_ready, ms_ready, rms_ready = sem("var_ready"), sem("std_ready"), sem("ms_ready"), sem("rms_ready")
        biased_ready, sig_ready = sem("biased_ready"), sem("sig_ready")
        dve_step, act_step, stored = sem("dve_step"), sem("act_step"), sem("stored")

        block = ctx.enter_context(nc.Block())

        @block.sync
        def _(sp_):
            def load(layer, n, slot):
                sp_.wait_ge(lo_ready, layer * UNITS + free_count(n))
                sp_.dma_start(w_raw[:, slot, :], w_stream[layer, n]).then_inc(raw_in[slot], 16)

            sp_.dma_start(x_tok[:, 0, :], x_in_dram[:, 0, :]).then_inc(x_loaded[0], 16)
            with sp_.Fori(0, DEPTH) as layer:
                for n in range(SLOTS):
                    load(layer, n, n)
                with sp_.Fori(1, UNITS // SLOTS) as g:
                    for s in range(SLOTS):
                        load(layer, g * SLOTS + s, s)
                for n in range(UNITS // SLOTS * SLOTS, UNITS):
                    load(layer, n, n % SLOTS)
            for t in range(TT):
                for half, written in enumerate((x_half, x_ready)):
                    sp_.wait_ge(written, 8 * DEPTH + t + 1)
                    c = slice(half * (D // 2), (half + 1) * (D // 2))
                    sp_.dma_start(out[:, t, c], x_tok[:, t, c]).then_inc(stored, 16)
            sp_.wait_ge(stored, 16 * 2 * TT)

        @block.gpsimd
        def _(pool):
            for t in range(TT):
                if t == 1:
                    pool.wait_ge(raw_in[0], 16)
                    pool.dma_start(x_tok[:, 1, :], x_in_dram[:, 1, :]).then_inc(x_loaded[1], 16)
                pool.wait_ge(x_loaded[t], 16)
                nc.gpsimd.memset(landed[:, 2 * t:2 * t + 1], 0.0).then_inc(x_half, 1)
                nc.gpsimd.memset(landed[:, 2 * t + 1:2 * t + 2], 0.0).then_inc(x_ready, 1)
            pool.dma_start(cst[:, P:C_ALL], consts[:, P:C_ALL]).then_inc(cst_loaded, 16)
            with pool.Fori(0, DEPTH) as layer:
                pool.wait_ge(x_ready, layer * 8 + 2)
                pool.wait_ge(raw_in[1], (layer * SLOT_UNITS[1] + 2) * 16)
                pool.dma_start(ex[:, :], extras[layer]).then_inc(ex_in, 16)
                pool.dma_start(mix[:, :], mix_rows[layer].partition_broadcast(P)).then_inc(mix_in, 16)
                for i in range(4):
                    pool.wait_ge(gain_used, layer * 4 + i + 1)
                    pool.dma_start(gain[:, :, :], norms[layer, i].partition_broadcast(P)).then_inc(gain_in, 16)

        @block.tensor
        def _(pe):
            mm = nc.tensor.matmul

            def unit_ready(layer, n):
                pe.wait_ge(lo_ready, layer * UNITS + n + 1 + SLOTS)

            def hi_in(layer, n):
                pe.wait_ge(hi_ready, layer * UNITS + n + 1)

            def three(out_, a_hi, a_lo, b_hi, b_lo, start, stop):
                mm(out_, a_hi, b_hi, start=start, stop=False)
                mm(out_, a_hi, b_lo, start=False, stop=False)
                return mm(out_, a_lo, b_hi, start=False, stop=stop)

            def turn_x(layer, j, t):
                for half, written in enumerate((x_half, x_ready)):
                    pe.wait_ge(written, (layer * 4 + j) * 2 + t + 1)
                    for k in range(4):
                        c = (4 * half + k) * P
                        last = nc.tensor.transpose(ps[:, 2 * t + half, k * P:(k + 1) * P], x_tok[:, t, c:c + P], ident)
                    last.then_inc(xt_turned, 1)

            def xt_hi_in(layer, j, t, half):
                pe.wait_ge(xthi_ready, ((layer * 4 + j) * 2 + t) * 2 + half + 1)

            def xt_whole(layer, j, t):
                pe.wait_ge(xt_ready, (layer * 4 + j) * 2 + t + 1)

            HH, HL, LH = (0, 0), (0, 1), (1, 0)
            ALL = (HH, HL, LH)

            def token_tile(slot, t, half, bank, passes=ALL, more=False):
                w = [part[:, slot, :].rearrange("p (k c) -> p k c", k=4) for part in (w_hi, w_lo)]
                for p in passes:
                    for k in range(4):
                        kt = 4 * half + k
                        last = mm(ps[:, bank, :], (xt_hi, xt_lo)[p[0]][:, t, kt, :], w[p[1]][:, k],
                                  start=p == HH and kt == 0, stop=not more and p == passes[-1] and kt == KT - 1)
                return last

            def row_tile(slot, t, lhs, bank, first, last_unit, ks=(0, 1), hs=(0, 1), passes=ALL):
                w = [part[:, slot, :].rearrange("p (k h c) -> p k h c", k=2, h=2) for part in (w_hi, w_lo)]
                for p in passes:
                    for k in ks:
                        for h in hs:
                            last = mm(ps[:, bank + 2 * t + h, :], lhs(k, t)[p[0]], w[p[1]][:, k, h],
                                      start=first and p == HH and k == 0, stop=last_unit and p == passes[-1] and k == 1)
                return last

            def row_tile_early(layer, n, t, lhs, bank, first, last_unit):
                hi_in(layer, n)
                row_tile(n % SLOTS, t, lhs, bank, first, False, passes=(HH, LH))
                unit_ready(layer, n)
                return row_tile(n % SLOTS, t, lhs, bank, False, last_unit, passes=(HL,))

            def channel_unit(layer, n, bank):
                unit_ready(layer, n)
                hi = w_hi[:, n % SLOTS, :].rearrange("p (k c) -> p k c", k=KT)
                lo = w_lo[:, n % SLOTS, :].rearrange("p (k c) -> p k c", k=KT)
                for m in range(2):
                    for k in range(KT):
                        c = slice(m * P, (m + 1) * P)
                        last = three(ps[:, bank, m * SEQ:(m + 1) * SEQ], hi[:, k, c], lo[:, k, c],
                                     xt_hi[:, :, k, :], xt_lo[:, :, k, :], k == 0, k == KT - 1)
                last.then_inc(unit_done, 1)

            def turn_h_tile(chunk, t):
                pe.wait_ge(h_ready, chunk * 2 + t + 1)
                for k in range(2):
                    last = nc.tensor.transpose(ps[:, HT, (k * TT + t) * P:(k * TT + t + 1) * P],
                                               h_tok[:, t, k * P:(k + 1) * P], ident)
                return last

            def turn_h(chunk):
                turn_h_tile(chunk, 0)
                turn_h_tile(chunk, 1).then_inc(ht_turned, 1)

            def ht(k, t):
                return ht_hi[:, k, t, :], ht_lo[:, k, t, :]

            def hz(k, t):
                return hz_hi[:, k, t, :], hz_lo[:, k, t, :]

            def gate_up(layer, n, slots):
                unit_ready(layer, n)
                for t in range(TT):
                    last = token_tile(slots[0], t, 0, GU + t)
                last.then_inc(unit_done, 1)
                unit_ready(layer, n + 1)
                token_tile(slots[1], 0, 1, GU).then_inc(gu_half, 1)
                token_tile(slots[1], 1, 1, GU + 1).then_inc(unit_done, 1)

            def down(layer, n, first):
                unit_ready(layer, n)
                row_tile(1, 0, ht, 0, first, False)
                row_tile(1, 1, ht, 0, first, False).then_inc(unit_done, 1)

            def ffn(layer, f, base, j):
                chunk0, turned0 = (layer * 2 + f) * CHUNKS, (layer * 2 + f) * (CHUNKS - 1)
                hi_in(layer, base)
                xt_hi_in(layer, j, 0, 0)
                token_tile(0, 0, 0, GU, (HH,))
                unit_ready(layer, base)
                token_tile(0, 0, 0, GU, (HL,))
                hi_in(layer, base + 1)
                xt_hi_in(layer, j, 0, 1)
                token_tile(1, 0, 1, GU, (HH,), more=True)
                xt_whole(layer, j, 0)
                token_tile(0, 0, 0, GU, (LH,))
                token_tile(1, 0, 1, GU, (LH,), more=True)
                turn_x(layer, j, 1)
                xt_hi_in(layer, j, 1, 0)
                token_tile(0, 1, 0, GU + 1, (HH, HL))
                unit_ready(layer, base + 1)
                token_tile(1, 0, 1, GU, (HL,)).then_inc(gu_half, 1)
                xt_whole(layer, j, 1)
                token_tile(0, 1, 0, GU + 1, (LH,)).then_inc(unit_done, 1)
                token_tile(1, 1, 1, GU + 1).then_inc(unit_done, 1)
                unit_ready(layer, base + 2)
                pe.wait_ge(h_ready, chunk0 * 2 + 1)
                token_tile(2, 0, 0, GU)
                turn_h(chunk0)
                token_tile(2, 1, 0, GU + 1).then_inc(unit_done, 1)
                unit_ready(layer, base + 3)
                token_tile(0, 0, 1, GU).then_inc(gu_half, 1)
                token_tile(0, 1, 1, GU + 1).then_inc(unit_done, 1)
                pe.wait_ge(ht_ready, turned0 + 1)
                down(layer, base + 4, True)
                turn_h(chunk0 + 1)
                with pe.Fori(2, CHUNKS - 1) as c:
                    gate_up(layer, c * 3 + (base - 1), (2, 0))
                    pe.wait_ge(ht_ready, turned0 + c)
                    down(layer, c * 3 + (base + 1), False)
                    turn_h(chunk0 + c)
                n, chunk, hz0 = base + 3 * CHUNKS - 4, chunk0 + CHUNKS - 1, (layer * 2 + f) * TT
                unit_ready(layer, n)
                token_tile(2, 0, 0, GU)
                token_tile(2, 1, 0, GU + 1).then_inc(unit_done, 1)
                unit_ready(layer, n + 1)
                token_tile(0, 0, 1, GU).then_inc(gu_half, 1)
                pe.wait_ge(ht_ready, turned0 + CHUNKS - 1)
                unit_ready(layer, n + 2)
                for t in range(TT):
                    if t == 1:
                        token_tile(0, 1, 1, GU + 1).then_inc(unit_done, 1)
                    last = row_tile(1, t, ht, 0, False, False, ks=(0,))
                    turn_h_tile(chunk, t).then_inc(hz_turned, 1)
                    last = row_tile(1, t, ht, 0, False, False, ks=(1,))
                    if t == 1:
                        last.then_inc(unit_done, 1)
                    pe.wait_ge(hz_ready, hz0 + t + 1)
                    if t == 0:
                        row_tile_early(layer, n + 3, 0, hz, 0, False, True).then_inc(acc_half, 1)
                    else:
                        row_tile(2, 1, hz, 0, False, True, ks=(0,))
                        turn_x(layer, j + 1, 0)
                        row_tile(2, 1, hz, 0, False, True, ks=(1,)).then_inc(unit_done, 1)

            def xt(kt0):
                return lambda k, t: (xt_hi[:, t, kt0 + k, :], xt_lo[:, t, kt0 + k, :])

            def v_tile(t, passes=ALL):
                w = [part[:, U_V % SLOTS, :].rearrange("p (k c) -> p k c", k=KT) for part in (w_hi, w_lo)]
                for p in passes:
                    for k in range(KT):
                        last = mm(ps[:, 7, t * 256:(t + 1) * 256], (xt_hi, xt_lo)[p[0]][:, t, k, :], w[p[1]][:, k],
                                  start=p == HH and k == 0, stop=p == LH and k == KT - 1)
                return last

            pe.wait_ge(id_loaded, 16)
            with pe.Fori(0, DEPTH) as layer:
                turn_x(layer, 0, 0)
                ffn(layer, 0, U_FFN1, 0)

                z0, z1 = U_Z % SLOTS, (U_Z + 1) % SLOTS
                hi_in(layer, U_V)
                xt_hi_in(layer, 1, 0, 1)
                v_tile(0, (HH,))
                unit_ready(layer, U_V)
                v_tile(0, (HL,))
                hi_in(layer, U_Z)
                token_tile(z0, 0, 0, 4, (HH,))
                xt_whole(layer, 1, 0)
                v_tile(0, (LH,))
                token_tile(z0, 0, 0, 4, (LH,))
                hi_in(layer, U_Z + 1)
                token_tile(z1, 0, 1, 4, (HH, LH), more=True)
                turn_x(layer, 1, 1)
                unit_ready(layer, U_Z)
                token_tile(z0, 0, 0, 4, (HL,))
                xt_hi_in(layer, 1, 1, 1)
                v_tile(1, (HH, HL))
                xt_whole(layer, 1, 1)
                v_tile(1, (LH,)).then_inc(unit_done, 1)
                token_tile(z0, 1, 0, 5).then_inc(unit_done, 1)
                unit_ready(layer, U_Z + 1)
                token_tile(z1, 0, 1, 4, (HL,))
                token_tile(z1, 1, 1, 5).then_inc(unit_done, 1)
                pe.wait_ge(exlo_ready, layer + 1)
                for k in range(KT):
                    c = slice(k * ROWS, (k + 1) * ROWS)
                    last = three(ps[0:ROWS, 0, 0:SEQ], ex_hi[:, c], ex_lo[:, c], xt_hi[:, :, k, :], xt_lo[:, :, k, :],
                                 k == 0, k == KT - 1)
                last.then_inc(fd_done, 1)
                channel_unit(layer, U_XS, 1)
                channel_unit(layer, U_XS + 1, 6)
                pe.wait_ge(z_out, layer + 1)
                channel_unit(layer, U_B, 5)
                pe.wait_ge(conv_first, layer * 5 + 2)
                channel_unit(layer, U_C, 6)
                pe.wait_ge(cumsplit_ready, layer + 1)
                for b, bank in enumerate((2, 3, 1, 4)):
                    for i in range(2):
                        for first, part in ((True, cum_hi), (False, cum_lo)):
                            mm(ps[:, bank, i * SEQ:(i + 1) * SEQ], sel[:, 2 * b + i, :], part[:, :],
                               start=first and i == 0, stop=False, skip_group_check=True)
                    last = mm(ps[:, bank, :], id_r[:, :], ssd_mask[:, :], start=False, stop=True, skip_group_check=True)
                last.then_inc(bc_done, 1)
                for t in range(TT):
                    for i, rows in enumerate((cum[:, :], sp[0:ROWS, 5, 0:SEQ])):
                        c = (t * 2 + i) * ROWS
                        last = nc.tensor.transpose(ps[:, 0, c:c + ROWS], rows[:, t * P:(t + 1) * P],
                                                   cst[0:ROWS, C_ID:C_ID + ROWS])
                last.then_inc(cum_turned, 1)
                pe.wait_ge(v_out, layer + 1)
                channel_unit(layer, U_U, 7)
                pe.wait_ge(conv_first, layer * 5 + 4)
                pe.wait_ge(xbc_ready, layer * 4 + 2)
                for t in range(TT):
                    for m in range(4):
                        last = nc.tensor.transpose(ps[:, 5 + t, m * P:(m + 1) * P], xbc[:, m, t * P:(t + 1) * P], ident)
                last.then_inc(xs_turned, 1)
                pe.wait_ge(cumtok_ready, layer + 1)
                pe.wait_ge(xbc_ready, layer * 4 + 3)
                for g in range(NG):
                    last = nc.tensor.transpose(ps[:, 0, g * P:(g + 1) * P], xbc[:, 4 + g, 0:P], ident)
                last.then_inc(b_turned, 1)
                pe.wait_ge(conv_first, layer * 5 + 5)
                channel_unit(layer, U_G, 7)
                pe.wait_ge(decay_ready, layer * 16 + 8)
                pe.wait_ge(xbc_ready, layer * 4 + 4)
                for g in range(NG):
                    for c in range(TT):
                        s = slice(c * P, (c + 1) * P)
                        last = mm(ps[:, 2, (g * TT + c) * P:(g * TT + c + 1) * P], xbc[:, 4 + g, s], xbc[:, 6 + g, s],
                                  start=True, stop=True)
                last.then_inc(cb_done, 1)
                pe.wait_ge(b_out, layer + 1)
                pe.wait_ge(conv_ready, layer * 5 + 5)
                for bank, w in ((3, E_WA), (0, E_WX)):
                    for m in range(2):
                        last = mm(ps[:, bank, m * SEQ:(m + 1) * SEQ], ex[:, w + m * P:w + (m + 1) * P], uc[:, m, :],
                                  start=True, stop=True)
                last.then_inc(gates_done, 1)
                pe.wait_ge(xs_used, layer + 1)
                channel_unit(layer, U_Q, 5)
                channel_unit(layer, U_K, 6)
                pe.wait_ge(cb_out, layer + 1)
                pe.wait_ge(xdd_ready, layer + 1)
                for g in range(NG):
                    last = mm(ps[:, 2, g * 256:(g + 1) * 256], b_tok[:, g, :],
                              xdd[:, 4 * g:4 * g + 4, :].rearrange("p h d -> p (h d)"), start=True, stop=True)
                last.then_inc(state_done, 1)
                pe.wait_ge(gates_ready, layer + 1)
                pe.wait_ge(m_ready, layer * 4 + 4)
                for c in range(TT):
                    for h in range(SH):
                        last = mm(ps[:, c, h * HD:(h + 1) * HD], decay[:, h, c, :], xdt[:, c, h, :],
                                  start=True, stop=True)
                last.then_inc(ydiag_done, 1)
                pe.wait_ge(state_ready, layer + 1)
                for g in range(NG):
                    last = mm(ps[:, 3, g * 256:(g + 1) * 256], xbc[:, 6 + g, P:2 * P], state[:, g * 256:(g + 1) * 256],
                              start=True, stop=True)
                last.then_inc(yoff_done, 1)
                pe.wait_ge(f_rows_ready, layer + 1)
                pe.wait_ge(q_out, layer + 1)
                pe.wait_ge(k_out, layer + 1)
                pe.wait_ge(g_out, layer + 1)
                for h in range(AH):
                    for q, k in ((0, 0), (1, 0), (1, 1)):
                        b, c = block_of(h, q, k)
                        last = mm(ps[:, 5 + b, c:c + P], qf[:, h, q * P:(q + 1) * P], kf[:, h, k * P:(k + 1) * P],
                                  start=True, stop=q != k)
                        if q == k:
                            last = mm(ps[:, 5 + b, c:c + P], id_r[:, :], att_mask[:, :], start=False, stop=True)
                last.then_inc(logits_done, 1)
                def turn_yc(t):
                    pe.wait_ge(yn_ready, layer * 2 + t + 1)
                    if t > 0:
                        pe.wait_ge(yclo_ready, layer * 2 + t)
                    for m in range(4):
                        last = nc.tensor.transpose(ps[:, 4, m * P:(m + 1) * P], y_tok[:, t, m * P:(m + 1) * P], ident)
                    last.then_inc(yc_turned, 1)

                ya, yc, yc2, yb = (n % SLOTS for n in (U_YA, U_YC, U_YC + 1, U_YB))
                unit_ready(layer, U_YA)
                pe.wait_ge(y_read, layer + 1)
                pe.wait_ge(yahi_ready, layer + 1)
                row_tile(ya, 0, xt(0), 0, True, False, passes=(HH, HL))
                pe.wait_ge(yalo_ready, layer + 1)
                row_tile(ya, 0, xt(0), 0, False, False, passes=(LH,))
                row_tile(ya, 1, xt(0), 0, True, False, ks=(0,))
                turn_yc(0)
                row_tile(ya, 1, xt(0), 0, False, False, ks=(1,)).then_inc(unit_done, 1)
                turn_yc(1)
                row_tile_early(layer, U_YC, 0, xt(4), 0, False, False)
                hi_in(layer, U_YC + 1)
                row_tile(yc2, 0, xt(6), 0, False, False, passes=(HH, LH))
                pe.wait_ge(probs_ready, layer + 1)
                for b in range(3):
                    for i in range(4):
                        last = nc.tensor.transpose(ps[:, 5 + b, i * P:(i + 1) * P], probs[:, b, i * P:(i + 1) * P], ident)
                last.then_inc(probs_turned, 1)
                pe.wait_ge(yclo_ready, layer * 2 + 2)
                row_tile(yc, 1, xt(4), 0, False, False, ks=(0,))
                unit_ready(layer, U_YC + 1)
                row_tile(yc2, 0, xt(6), 0, False, False, passes=(HL,))
                pe.wait_ge(probst_ready, layer + 1)
                for h in range(AH):
                    rows = slice(h % 2 * HD, h % 2 * HD + HD)
                    v = [v_tok[:, t, h * HD:(h + 1) * HD] for t in range(TT)]
                    o = ps[rows, 4, h // 2 * SEQ:(h // 2 + 1) * SEQ]
                    for q, k in ((0, 0), (1, 0), (1, 1)):
                        b, c = block_of(h, q, k)
                        last = mm(o[:, q * P:(q + 1) * P], v[k], probs_t[:, b, c:c + P], start=k == 0, stop=k == q)
                last.then_inc(pv_done, 1)
                row_tile(yc, 1, xt(4), 0, False, False, ks=(1,)).then_inc(unit_done, 1)
                pe.wait_ge(yblo_ready, layer + 1)
                row_tile_early(layer, U_YB, 0, xt(2), 0, False, True).then_inc(acc_half, 1)
                row_tile(yc2, 1, xt(6), 0, False, False).then_inc(unit_done, 1)
                row_tile(yb, 1, xt(2), 0, False, True, ks=(0,))
                turn_x(layer, 2, 0)
                row_tile(yb, 1, xt(2), 0, False, True, ks=(1,)).then_inc(unit_done, 1)

                ffn(layer, 1, U_FFN2, 2)

                def pt(k, t):
                    c = E_PT - E_SPLIT + k * SEQ + t * P
                    return ex_hi[:, c:c + P], ex_lo[:, c:c + P]

                def gate(i, t):
                    return row_tile((U_GATE + i) % SLOTS, t, xt(2 * i), 0, i == 0, i == 3)

                unit_ready(layer, U_PE)
                row_tile(U_PE % SLOTS, 0, pt, 4, True, True)
                xt_whole(layer, 3, 0)
                hi_in(layer, U_GATE)
                row_tile(U_GATE % SLOTS, 0, xt(0), 0, True, False, passes=(HH, LH))
                row_tile(U_PE % SLOTS, 1, pt, 4, True, True, ks=(0,))
                turn_x(layer, 3, 1)
                row_tile(U_PE % SLOTS, 1, pt, 4, False, True, ks=(1,)).then_inc(unit_done, 1)
                unit_ready(layer, U_GATE)
                row_tile(U_GATE % SLOTS, 0, xt(0), 0, False, False, passes=(HL,))
                row_tile_early(layer, U_GATE + 1, 0, xt(2), 0, False, False)
                xt_whole(layer, 3, 1)
                gate(0, 1).then_inc(unit_done, 1)
                row_tile_early(layer, U_GATE + 2, 0, xt(4), 0, False, False)
                gate(1, 1).then_inc(unit_done, 1)
                row_tile_early(layer, U_GATE + 3, 0, xt(6), 0, False, True).then_inc(acc_half, 1)
                gate(2, 1).then_inc(unit_done, 1)
                row_tile((U_GATE + 3) % SLOTS, 1, xt(6), 0, False, True, hs=(0,)).then_inc(gate_half, 1)
                row_tile((U_GATE + 3) % SLOTS, 1, xt(6), 0, False, True, hs=(1,)).then_inc(unit_done, 1)

        @block.scalar
        def _(act):
            fn = nc.scalar.activation
            flat2 = "p a b -> p (a b)"

            def make_hi(layer, n, slot, nth):
                act.wait_ge(raw_in[slot], (layer * SLOT_UNITS[slot] + nth + 1) * 16)
                act.wait_ge(unit_done, layer * UNITS + free_count(n))
                fn(w_hi[:, slot, :], w_raw[:, slot, :], ACT.Copy).then_inc(hi_ready, 1)

            def hi_of(layer, n):
                make_hi(layer, n, n % SLOTS, n // SLOTS)

            def square(layer, i, t):
                act.wait_ge(mean_ready, (layer * 3 + i) * 2 + t + 1)
                fn(ps[:, 2 * t:2 * t + 2, :].rearrange("p b c -> p (b c)"), x_new[:, t, :], ACT.Square,
                   bias=nmean[:, t:t + 1], accum_out=ssq[:, t:t + 1]).then_inc(ssq_ready, 1)

            def root(layer, i, t):
                act.wait_ge(var_ready, (layer * 3 + i) * 2 + t + 1)
                fn(rstd[:, t:t + 1], rstd[:, t:t + 1], ACT.Sqrt).then_inc(std_ready, 1)

            def xt_hi_of(layer, j, t):
                for half in range(2):
                    act.wait_ge(xt_turned, ((layer * 4 + j) * 2 + t) * 2 + half + 1)
                    fn(xt_hi[:, t, 4 * half:4 * half + 4, :].rearrange("p k c -> p (k c)"),
                       ps[:, 2 * t + half, :], ACT.Copy).then_inc(xthi_ready, 1)

            def norm_and_turn(layer, i, n):
                hi_of(layer, n)
                xt_hi_of(layer, i + 1, 0)
                hi_of(layer, n + 1)
                square(layer, i, 1)
                root(layer, i, 1)
                hi_of(layer, n + 2)
                xt_hi_of(layer, i + 1, 1)

            def silu_tile(t):
                fn(silu_g[:, t, :], ps[:, GU + t, 0:FC], ACT.Silu).then_inc(silu_ready, 1)

            def silu(done_first, done_second):
                act.wait_ge(gu_half, done_first)
                silu_tile(0)
                act.wait_ge(unit_done, done_second)
                silu_tile(1)

            def ht_hi_of(turned):
                act.wait_ge(ht_turned, turned + 1)
                fn(ht_hi[:, :, :, :].rearrange("p k t c -> p (k t c)"), ps[:, HT, :], ACT.Copy).then_inc(hthi_ready, 1)

            def hz_hi_of(layer, f, t):
                act.wait_ge(hz_turned, (layer * 2 + f) * TT + t + 1)
                fn(hz_hi[:, :, t, :], ps[:, HT, :].rearrange("p (k t c) -> p k t c", k=2, t=TT)[:, :, t, :],
                   ACT.Copy).then_inc(hzhi_ready, 1)

            def ffn(layer, f, base):
                chunk0, turned0 = (layer * 2 + f) * CHUNKS, (layer * 2 + f) * (CHUNKS - 1)
                silu(chunk0 + 1, layer * UNITS + base + 2 + SLOTS)
                hi_of(layer, base + 3)
                ht_hi_of(turned0)
                hi_of(layer, base + 4)
                if f == 0:
                    act.wait_ge(ex_in, layer * 16 + 16)
                    fn(ex_hi[:, :], ex[:, E_SPLIT:E_ALL], ACT.Copy).then_inc(exhi_ready, 1)
                with act.Fori(1, CHUNKS - 1) as c:
                    make_hi(layer, c * 3 + (base + 2), 2, c + base // 3)
                    silu(chunk0 + c + 1, layer * UNITS + c * 3 + base + 1 + SLOTS)
                    make_hi(layer, c * 3 + (base + 3), 0, c + (base // 3 + 1))
                    ht_hi_of(turned0 + c)
                    make_hi(layer, c * 3 + (base + 4), 1, c + (base // 3 + 1))
                c = CHUNKS - 1
                hi_of(layer, base + 3 * c + 2)
                act.wait_ge(gu_half, chunk0 + c + 1)
                silu_tile(0)
                hz_hi_of(layer, f, 0)
                square(layer, 2 * f, 0)
                act.wait_ge(unit_done, layer * UNITS + base + c * 3 + 1 + SLOTS)
                silu_tile(1)
                root(layer, 2 * f, 0)
                hz_hi_of(layer, f, 1)

            act.dma_start(ident, consts[:, C_ID:C_ID + P]).then_inc(id_loaded, 16)
            act.wait_ge(pads_ready, 2)
            fn(warm[:, 0:1], warm[:, 1:2], ACT.Sigmoid)
            with act.Fori(0, DEPTH) as layer:
                xt_hi_of(layer, 0, 0)
                hi_of(layer, 0)
                hi_of(layer, 1)
                xt_hi_of(layer, 0, 1)
                hi_of(layer, 2)
                ffn(layer, 0, U_FFN1)
                norm_and_turn(layer, 0, U_V)

                def done(n):
                    act.wait_ge(unit_done, layer * UNITS + n + 1 + SLOTS)

                def conv_in(i, bank):
                    act.wait_ge(pads_ready, layer + 3)
                    fn(big[:, 2 * i:2 * i + 2, 3:3 + SEQ], ps[:, bank, :].rearrange("p (m s) -> p m s", m=2),
                       ACT.Copy)
                    for m in range(2 * i, 2 * i + 2):
                        last = fn(xbc[:, m, :], ps[:, bank, m % 2 * SEQ:(m % 2 + 1) * SEQ], ACT.Identity,
                                  bias=ex[:, E_CB + m:E_CB + m + 1], scale=ex[:, E_CW + 24 + m:E_CW + 25 + m])
                    last.then_inc(conv_first, 1)

                def conv_out(i):
                    act.wait_ge(conv_ready, layer * 5 + i + 1)
                    fn(xbc[:, 2 * i:2 * i + 2, :], xbc[:, 2 * i:2 * i + 2, :], ACT.Silu).then_inc(xbc_ready, 1)

                done(U_V)
                fn(v_tok[:, :, :].rearrange(flat2), ps[:, 7, :], ACT.Copy).then_inc(v_out, 1)
                hi_of(layer, U_V + 3)
                done(U_Z)
                hi_of(layer, U_Z + 3)
                done(U_Z + 1)
                fn(z_tok[:, :, :], ps[:, 4:6, :], ACT.Silu).then_inc(z_out, 1)
                hi_of(layer, U_Z + 4)
                act.wait_ge(abs_ready, layer + 1)
                fn(sp[:, 1, :], sp[:, 1, :], ACT.Exp, scale=-1.0).then_inc(act_step, 1)
                act.wait_ge(act_step, layer * ACT_STEPS + 1)
                fn(expa[:, :], ex[0:ROWS, E_ALOG:E_ALOG + 1], ACT.Exp).then_inc(exp_ready, 1)
                done(U_XS)
                conv_in(0, 1)
                hi_of(layer, U_XS + 3)
                done(U_XS + 1)
                conv_in(1, 6)
                hi_of(layer, U_XS + 4)
                act.wait_ge(cum_ready, layer + 1)
                fn(cum_hi[:, :], cum[:, :], ACT.Copy).then_inc(cumhi_ready, 1)
                done(U_B)
                conv_in(2, 5)
                hi_of(layer, U_B + 3)
                conv_out(0)
                conv_out(1)
                done(U_C)
                conv_in(3, 6)
                hi_of(layer, U_C + 3)
                conv_out(2)
                act.wait_ge(cum_turned, layer + 1)
                fn(cum_tok[:, :, :, :].rearrange("p a b c -> p (a b c)"), ps[:, 0, 0:TT * 2 * ROWS], ACT.Copy)
                fn(ncum_tok[:, :, :], ps[:, 0, 0:TT * 2 * ROWS].rearrange("p (a b c) -> p a b c", a=TT, b=2)[:, :, 0, :],
                   ACT.Copy, scale=-1.0).then_inc(cumtok_ready, 1)
                done(U_U)
                fn(u_raw[:, :, 3:3 + SEQ], ps[:, 7, :].rearrange("p (m s) -> p m s", m=2), ACT.Copy)
                for m in range(2):
                    last = fn(uc[:, m, :], ps[:, 7, m * SEQ:(m + 1) * SEQ], ACT.Identity,
                              bias=ex[:, E_UB + m:E_UB + m + 1], scale=ex[:, E_UW + 6 + m:E_UW + 7 + m])
                last.then_inc(conv_first, 1)
                conv_out(3)
                act.wait_ge(cumtok_ready, layer + 1)
                fn(ecum[:, :], cum_tok[:, 1, 0, AH:ROWS], ACT.Exp)

                def decays(heads):
                    for h in heads:
                        for c in range(TT):
                            fn(decay[:, h, c, :], ps[:, (2, 3, 1, 4)[h // 2], (h % 2 * TT + c) * P:(h % 2 * TT + c + 1) * P],
                               ACT.Exp, bias=ncum_tok[:, c, AH + h:AH + h + 1]).then_inc(decay_ready, 1)

                act.wait_ge(conv_ready, layer * 5 + 4)
                decays(range(0, 4))
                hi_of(layer, U_U + 3)
                act.wait_ge(b_turned, layer + 1)
                fn(b_tok[:, :, :].rearrange(flat2), ps[:, 0, 0:256], ACT.Copy).then_inc(b_out, 1)
                decays(range(4, 8))
                fn(qf[HD:HD + ROWS, :, :], cum[:, :].unsqueeze(1).to_broadcast([ROWS, AH, SEQ]), ACT.Copy)
                fn(kf[96:96 + ROWS, :, :], cum[:, :].unsqueeze(1).to_broadcast([ROWS, AH, SEQ]), ACT.Copy,
                   scale=-1.0).then_inc(f_rows_ready, 1)
                done(U_G)
                fn(gate_g[:, :, :].rearrange(flat2), ps[:, 7, :], ACT.Gelu_apprx_tanh).then_inc(g_out, 1)
                act.wait_ge(cb_done, layer + 1)
                fn(cb[:, :, :, :].rearrange("p a b c -> p (a b c)"), ps[:, 2, :], ACT.Copy).then_inc(cb_out, 1)
                hi_of(layer, U_G + 3)
                act.wait_ge(gates_done, layer + 1)
                for i, (bank, b) in enumerate(((3, E_BA), (0, E_BX))):
                    for m in range(2):
                        last = fn(lru[:, i, m, :], ps[:, bank, m * SEQ:(m + 1) * SEQ], ACT.Sigmoid,
                                  bias=ex[:, b + m:b + m + 1])
                last.then_inc(gates_ready, 1)
                act.wait_ge(gates_ready, layer + 1)
                for m in range(2):
                    fn(lru[:, 2, m, :], lru[:, 0, m, :], ACT.Exp, scale=c8[:, 0, m:m + 1])
                for m in range(2):
                    last = fn(lru[:, 3, m, :], lru[:, 0, m, :], ACT.Tanh, scale=c8[:, 1, m:m + 1])
                last.then_inc(aa_ready, 1)

                def head_rows(dst, bank, scale, signal):
                    for r in range(2):
                        last = fn(dst[0:HD, r:AH:2, :], ps[r * HD:(r + 1) * HD, bank, :].rearrange("p (a s) -> p a s", a=2),
                                  ACT.Copy, scale=scale)
                    last.then_inc(signal, 1)

                done(U_Q)
                head_rows(qf, 5, HD ** -0.5, q_out)
                done(U_K)
                head_rows(kf, 6, 1.0, k_out)
                act.wait_ge(state_done, layer + 1)
                fn(state[:, :], ps[:, 2, :], ACT.Copy).then_inc(state_ready, 1)
                act.wait_ge(one_a2_ready, layer + 1)
                fn(lru[:, 3, :, :], lru[:, 3, :, :], ACT.Sqrt).then_inc(root_ready, 1)
                hi_of(layer, U_Q + 3)
                hi_of(layer, U_K + 3)

                def split_hi(kt0, n, src, signal):
                    fn(xt_hi[:, :, kt0:kt0 + n, :], src, ACT.Copy).then_inc(signal, 1)

                act.wait_ge(ya_ready, layer + 1)
                split_hi(0, 2, lru[:, 1, :, :].rearrange("p m (t c) -> p t m c", t=TT), yahi_ready)
                act.wait_ge(yz_ready, layer + 1)
                for t in range(TT):
                    for g in range(NG):
                        i = t * NG + g
                        fn(big[:, i, 0:256], y_tok[:, t, g * 256:(g + 1) * 256], ACT.Square,
                           accum_out=msq[:, i:i + 1]).then_inc(msq_ready, 1)
                act.wait_ge(ms_ready, layer + 1)
                fn(msq[:, :], msq[:, :], ACT.Sqrt).then_inc(rms_ready, 1)

                def yc_hi(t):
                    act.wait_ge(yc_turned, layer * 2 + t + 1)
                    fn(xt_hi[:, t, 4:8, :].rearrange("p k c -> p (k c)"), ps[:, 4, :], ACT.Copy).then_inc(ychi_ready, 1)

                act.wait_ge(nmax_ready, layer + 1)
                for h in range(AH):
                    for q in range(2):
                        b, c = block_of(h, q, 0)
                        last = fn(probs[:, b, c:c + (q + 1) * P], ps[:, 5 + b, c:c + (q + 1) * P], ACT.Exp,
                                  bias=nmax[:, q, h:h + 1], accum_out=rsum[:, q, h:h + 1])
                    if h == 0:
                        yc_hi(0)
                last.then_inc(probs_raw, 1)
                yc_hi(1)
                hi_of(layer, U_YA + 3)
                act.wait_ge(probs_turned, layer + 1)
                fn(probs_t, ps[:, 5:8, :], ACT.Copy).then_inc(probst_ready, 1)
                act.wait_ge(pv_done, layer + 1)
                split_hi(2, 2, ps[:, 4, :].rearrange("p (m t c) -> p t m c", m=2, t=TT), ybhi_ready)
                fn(warm[:, 0:1], warm[:, 1:2], ACT.Sqrt)
                square(layer, 1, 0)
                root(layer, 1, 0)
                norm_and_turn(layer, 1, U_FFN2)
                ffn(layer, 1, U_FFN2)
                norm_and_turn(layer, 2, U_PE)
                hi_of(layer, U_PE + 3)
                hi_of(layer, U_GATE + 3)
                fn(warm[:, 0:1], warm[:, 1:2], ACT.Sigmoid)
                for t in range(TT):
                    for half in range(2):
                        act.wait_ge(biased_ready, (layer * 2 + t) * 2 + half + 1)
                        c = slice(half * 512, half * 512 + 512)
                        fn(x_new[:, t, c], x_new[:, t, c], ACT.Sigmoid).then_inc(sig_ready, 1)

        @block.vector
        def _(dve):
            v = nc.vector

            def make_lo(layer, n, slot):
                dve.wait_ge(hi_ready, layer * UNITS + n + 1)
                v.tensor_tensor(w_lo[:, slot, :], w_raw[:, slot, :], w_hi[:, slot, :].bitcast(f32),
                                ALU.subtract).then_inc(lo_ready, 1)

            def lo_of(layer, n):
                make_lo(layer, n, n % SLOTS)

            def xt_lo_of(layer, j, t):
                dve.wait_ge(xthi_ready, ((layer * 4 + j) * 2 + t + 1) * 2)
                v.tensor_tensor(xt_lo[:, t, :, :].rearrange("p k c -> p (k c)"),
                                ps[:, 2 * t:2 * t + 2, :].rearrange("p b c -> p (b c)"),
                                xt_hi[:, t, :, :].rearrange("p k c -> p (k c)").bitcast(f32),
                                ALU.subtract).then_inc(xt_ready, 1)

            def hidden_tile(chunk, t):
                dve.wait_ge(silu_ready, chunk * 2 + t + 1)
                v.scalar_tensor_tensor(out=h_tok[:, t, :], in0=silu_g[:, t, :], scalar=0.5,
                                       in1=ps[:, GU + t, FC:2 * FC], op0=ALU.mult, op1=ALU.mult).then_inc(h_ready, 1)

            def hidden(chunk):
                for t in range(TT):
                    hidden_tile(chunk, t)

            def ht_lo_of(turned):
                dve.wait_ge(hthi_ready, turned + 1)
                v.tensor_tensor(ht_lo[:, :, :, :].rearrange("p k t c -> p (k t c)"), ps[:, HT, :],
                                ht_hi[:, :, :, :].rearrange("p k t c -> p (k t c)").bitcast(f32),
                                ALU.subtract).then_inc(ht_ready, 1)

            def hz_lo_of(layer, f, t):
                dve.wait_ge(hzhi_ready, (layer * 2 + f) * TT + t + 1)
                v.tensor_tensor(hz_lo[:, :, t, :], ps[:, HT, :].rearrange("p (k t c) -> p k t c", k=2, t=TT)[:, :, t, :],
                                hz_hi[:, :, t, :].bitcast(f32), ALU.subtract).then_inc(hz_ready, 1)

            def ffn(layer, f, base):
                chunk0, turned0 = (layer * 2 + f) * CHUNKS, (layer * 2 + f) * (CHUNKS - 1)
                hidden(chunk0)
                lo_of(layer, base + 3)
                ht_lo_of(turned0)
                lo_of(layer, base + 4)
                if f == 0:
                    dve.wait_ge(exhi_ready, layer + 1)
                    v.tensor_tensor(ex_lo[:, :], ex[:, E_SPLIT:E_ALL], ex_hi[:, :].bitcast(f32),
                                    ALU.subtract).then_inc(exlo_ready, 1)
                with dve.Fori(1, CHUNKS - 1) as c:
                    make_lo(layer, c * 3 + (base + 2), 2)
                    hidden(chunk0 + c)
                    make_lo(layer, c * 3 + (base + 3), 0)
                    ht_lo_of(turned0 + c)
                    make_lo(layer, c * 3 + (base + 4), 1)

            v.memset(nmean[:, :], 0.0).then_inc(lo_ready, SLOTS)
            v.memset(u_raw[:, :, 0:3], 0.0).then_inc(pads_ready, 1)
            v.memset(warm[:, :], 1.0).then_inc(pads_ready, 1)
            v.memset(msq[:, :], 0.0).then_inc(unit_done, SLOTS)
            v.memset(rstd[:, :], 0.0).then_inc(gain_used, 1)
            v.memset(sp[:, :, :], 0.0).then_inc(masks_ready, 1)
            v.memset(qf[:, :, :], 0.0).then_inc(masks_ready, 1)
            v.memset(kf[:, :, :], 0.0).then_inc(masks_ready, 1)

            with dve.Fori(0, DEPTH) as layer:
                steps = [0]

                def step(ins):
                    steps[0] += 1
                    ins.then_inc(dve_step, 1)
                    dve.wait_ge(dve_step, layer * DVE_STEPS + steps[0])

                def done(n):
                    dve.wait_ge(unit_done, layer * UNITS + n + 1 + SLOTS)

                def norm_mean(i, t, last_unit):
                    if t == 0:
                        dve.wait_ge(acc_half, layer * 4 + i + 1)
                    else:
                        done(last_unit)
                    step(v.scalar_tensor_tensor(out=x_new[:, t, :], in0=x_tok[:, t, :], scalar=ALPHA,
                                                in1=ps[:, 2 * t:2 * t + 2, :].rearrange("p b c -> p (b c)"),
                                                op0=ALU.mult, op1=ALU.add, accum_out=nmean[:, t:t + 1]))
                    v.tensor_scalar(nmean[:, t:t + 1], nmean[:, t:t + 1], -1.0 / D, None, ALU.mult)\
                        .then_inc(mean_ready, 1)

                def norm_center(i, t):
                    dve.wait_ge(mean_ready, (layer * 3 + i) * 2 + t + 1)
                    v.scalar_tensor_tensor(out=x_tok[:, t, :], in0=x_new[:, t, :], scalar=nmean[:, t:t + 1],
                                           in1=gain[:, 0, :], op0=ALU.add, op1=ALU.mult)

                def norm_var(i, t):
                    dve.wait_ge(ssq_ready, (layer * 3 + i) * 2 + t + 1)
                    v.tensor_scalar(rstd[:, t:t + 1], ssq[:, t:t + 1], 1.0 / D, EPS, ALU.mult, ALU.add)\
                        .then_inc(var_ready, 1)

                def norm_scale(i, t):
                    dve.wait_ge(std_ready, (layer * 3 + i) * 2 + t + 1)
                    step(v.reciprocal(rstd[:, t:t + 1], rstd[:, t:t + 1]))
                    for half, signal in enumerate((x_half, x_ready)):
                        c = slice(half * 512, half * 512 + 512)
                        v.scalar_tensor_tensor(out=x_tok[:, t, c], in0=x_tok[:, t, c], scalar=rstd[:, t:t + 1],
                                               in1=gain[:, 1, c], op0=ALU.mult, op1=ALU.add).then_inc(signal, 1)

                def norm_and_turn(i, last_unit, n, f=None):
                    chunk = None if f is None else (layer * 2 + f + 1) * CHUNKS - 1
                    if f is not None:
                        hidden_tile(chunk, 0)
                        hz_lo_of(layer, f, 0)
                        lo_of(layer, n - 1)
                    dve.wait_ge(gain_in, (layer * 4 + i + 1) * 16)
                    norm_mean(i, 0, last_unit)
                    norm_center(i, 0)
                    norm_var(i, 0)
                    if f is not None:
                        hidden_tile(chunk, 1)
                        hz_lo_of(layer, f, 1)
                    norm_scale(i, 0)
                    lo_of(layer, n)
                    norm_mean(i, 1, last_unit)
                    xt_lo_of(layer, i + 1, 0)
                    norm_var(i, 1)
                    norm_center(i, 1)
                    norm_scale(i, 1)
                    lo_of(layer, n + 1)
                    dve.wait_ge(x_ready, (layer * 4 + i) * 2 + 4)
                    v.memset(nmean[:, 0:1], 0.0).then_inc(gain_used, 1)
                    if i < 2:
                        xt_lo_of(layer, i + 1, 1)
                    lo_of(layer, n + 2)
                    if i == 2:
                        xt_lo_of(layer, i + 1, 1)

                lo_of(layer, 0)
                xt_lo_of(layer, 0, 0)
                lo_of(layer, 1)
                xt_lo_of(layer, 0, 1)
                lo_of(layer, 2)
                ffn(layer, 0, U_FFN1)
                norm_and_turn(0, U_V - 1, U_V, 0)

                dve.wait_ge(cst_loaded, 16)
                heads = cst[0:ROWS, C_ID + AH:C_ID + ROWS]
                v.tensor_copy(id_r[:, :], ident)
                v.tensor_copy(ssd_mask[:, :].rearrange("p (a b) -> p a b", a=4),
                              cst[:, C_SSD:C_SSD + P].unsqueeze(1).to_broadcast([P, 4, P]))
                v.tensor_copy(att_mask[:, :], cst[:, C_ATT:C_ATT + P])
                v.tensor_copy(sel[:, :, :], heads.unsqueeze(2).to_broadcast([ROWS, SH, P]))
                dve.wait_ge(masks_ready, 3)
                for rows in (qf[96:96 + ROWS, :, :], kf[HD:HD + ROWS, :, :]):
                    v.tensor_copy(rows, cst[0:ROWS, C_ID:C_ID + AH].unsqueeze(2).to_broadcast([ROWS, AH, SEQ]))
                v.memset(big[:, :, 0:3], 0.0).then_inc(pads_ready, 1)
                for n in (U_V, U_Z, U_Z + 1):
                    lo_of(layer, n + 3)

                v.tensor_scalar(sp[:, 0, SEQ:SEQ + 2], ex[:, E_LAM:E_LAM + 2], -1.0, None, ALU.mult)
                dve.wait_ge(fd_done, layer + 1)
                step(v.tensor_scalar(sp[0:ROWS, 0, 0:SEQ], ps[0:ROWS, 0, 0:SEQ], ex[0:ROWS, E_BIAS:E_BIAS + 1],
                                     ex[0:ROWS, E_SIGN:E_SIGN + 1], ALU.add, ALU.mult))
                v.scalar_tensor_tensor(out=sp[:, 1, :], in0=sp[:, 0, :], scalar=-1.0, in1=sp[:, 0, :],
                                       op0=ALU.mult, op1=ALU.max).then_inc(abs_ready, 1)
                dve.wait_ge(exp_ready, layer + 1)
                step(v.tensor_scalar(sp[:, 2, :], sp[:, 1, :], 2.0, None, ALU.add))
                step(v.reciprocal(sp[:, 2, :], sp[:, 2, :]))
                step(v.tensor_tensor(sp[:, 1, :], sp[:, 1, :], sp[:, 2, :], ALU.mult))
                step(v.tensor_tensor(sp[:, 3, :], sp[:, 1, :], sp[:, 1, :], ALU.mult))
                step(v.tensor_scalar(sp[:, 4, :], sp[:, 3, :], 1.0 / 17, None, ALU.mult))
                for k in (15, 13, 11, 9, 7, 5, 3):
                    step(v.scalar_tensor_tensor(out=sp[:, 4, :], in0=sp[:, 4, :], scalar=1.0 / k, in1=sp[:, 3, :],
                                                op0=ALU.add, op1=ALU.mult))
                step(v.scalar_tensor_tensor(out=sp[:, 4, :], in0=sp[:, 4, :], scalar=1.0, in1=sp[:, 1, :],
                                            op0=ALU.add, op1=ALU.mult))
                step(v.tensor_scalar(sp[:, 4, :], sp[:, 4, :], 2.0, None, ALU.mult))
                step(v.scalar_tensor_tensor(out=sp[:, 5, :], in0=sp[:, 0, :], scalar=0.0, in1=sp[:, 4, :],
                                            op0=ALU.max, op1=ALU.add))
                v.tensor_scalar(c8[:, 0, :], sp[:, 5, SEQ:SEQ + 2], -8.0, None, ALU.mult)
                v.tensor_scalar(c8[:, 1, :], sp[:, 5, SEQ:SEQ + 2], 8.0, None, ALU.mult)
                lo_of(layer, U_XS + 3)
                step(v.tensor_scalar(sp[0:ROWS, 2, 0:SEQ], sp[0:ROWS, 5, 0:SEQ], expa[:, 0:1], -1.0,
                                     ALU.mult, ALU.mult))
                v.tensor_tensor_scan(cum[:, :], cst[0:ROWS, C_RESET:C_RESET + SEQ], sp[0:ROWS, 2, 0:SEQ], 0.0,
                                     ALU.mult, ALU.add).then_inc(cum_ready, 1)

                def conv(dst, src, tiles, taps, count):
                    for j in range(3):
                        for m in tiles:
                            ins = v.scalar_tensor_tensor(out=dst[:, m, :], in0=src[:, m, j:j + SEQ],
                                                         scalar=ex[:, taps + j * count + m:taps + j * count + m + 1],
                                                         in1=dst[:, m, :], op0=ALU.mult, op1=ALU.add)
                        if j < 2:
                            step(ins)
                    ins.then_inc(conv_ready, 1)

                for i in range(4):
                    if i == 1:
                        dve.wait_ge(cumhi_ready, layer + 1)
                        v.tensor_tensor(cum_lo[:, :], cum[:, :], cum_hi[:, :].bitcast(f32), ALU.subtract)\
                            .then_inc(cumsplit_ready, 1)
                    dve.wait_ge(conv_first, layer * 5 + i + 1)
                    conv(xbc, big, (2 * i, 2 * i + 1), E_CW, 8)
                    if i > 0:
                        lo_of(layer, U_XS + i + 3)
                dve.wait_ge(conv_first, layer * 5 + 5)
                conv(uc, u_raw, (0, 1), E_UW, 2)
                dve.wait_ge(xs_turned, layer + 1)
                dve.wait_ge(cumtok_ready, layer + 1)
                dve.wait_ge(mix_in, layer * 16 + 16)
                for t in range(TT):
                    xs = ps[:, 5 + t, :].rearrange("p (h d) -> p h d", h=SH)
                    v.tensor_tensor(xdt[:, t, :, :], xs, cum_tok[:, t, 1, AH:ROWS].unsqueeze(2).to_broadcast([P, SH, HD]),
                                    ALU.mult)
                    ins = v.tensor_tensor(y_tok[:, t, :].rearrange("p (h d) -> p h d", h=SH), xs,
                                          mix[:, 512:520].unsqueeze(2).to_broadcast([P, SH, HD]), ALU.mult)
                ins.then_inc(xs_used, 1)
                lo_of(layer, U_U + 3)
                dve.wait_ge(decay_ready, (layer + 1) * 16)
                dve.wait_ge(xs_used, layer + 1)
                v.tensor_tensor(xdd[:, :, :], xdt[:, 0, :, :], decay[:, :, 0, P - 1:P].to_broadcast([P, SH, HD]),
                                ALU.mult).then_inc(xdd_ready, 1)
                dve.wait_ge(xdd_ready, layer + 1)
                dve.wait_ge(cb_out, layer + 1)
                for g in range(NG):
                    for c in range(TT):
                        d = decay[:, 4 * g:4 * g + 4, c, :]
                        v.tensor_tensor(d, d, cb[:, g, c, :].unsqueeze(1).to_broadcast([P, 4, P]),
                                        ALU.mult).then_inc(m_ready, 1)
                lo_of(layer, U_G + 3)
                dve.wait_ge(aa_ready, layer + 1)
                r, ig, a, th = (lru[:, i, :, :] for i in range(4))
                step(v.tensor_tensor(r, a, a, ALU.mult))
                v.scalar_tensor_tensor(out=th, in0=r, scalar=1.0, in1=th, op0=ALU.add, op1=ALU.mult)\
                    .then_inc(one_a2_ready, 1)
                step(v.tensor_tensor(ig, ig, uc[:, :, :], ALU.mult))
                dve.wait_ge(ydiag_done, layer + 1)
                step(v.tensor_tensor(y_tok[:, :, :], y_tok[:, :, :], ps[:, 0:2, :], ALU.add))
                dve.wait_ge(yoff_done, layer + 1)
                v.tensor_tensor(y_off[:, :, :], ps[:, 3, :].rearrange("p (h d) -> p h d", h=SH),
                                ecum[:, :].unsqueeze(2).to_broadcast([P, SH, HD]), ALU.mult).then_inc(y_read, 1)
                dve.wait_ge(root_ready, layer + 1)
                step(v.tensor_tensor(ig, ig, th, ALU.mult))
                for m in range(2):
                    ins = v.tensor_tensor_scan(r[:, m, :], a[:, m, :], ig[:, m, :], 0.0, ALU.mult, ALU.add)
                step(ins)
                v.tensor_tensor(ig, r, gate_g[:, :, :], ALU.mult).then_inc(ya_ready, 1)

                def split_lo(kt0, n, src, signal):
                    v.tensor_tensor(xt_lo[:, :, kt0:kt0 + n, :], src, xt_hi[:, :, kt0:kt0 + n, :].bitcast(f32),
                                    ALU.subtract).then_inc(signal, 1)

                dve.wait_ge(y_read, layer + 1)
                step(v.tensor_tensor(y_tok[:, 1, :], y_tok[:, 1, :], y_off[:, :, :].rearrange("p h d -> p (h d)"), ALU.add))
                v.tensor_tensor(y_tok[:, :, :], y_tok[:, :, :], z_tok[:, :, :], ALU.mult).then_inc(yz_ready, 1)
                dve.wait_ge(yahi_ready, layer + 1)
                split_lo(0, 2, ig.rearrange("p m (t c) -> p t m c", t=TT), yalo_ready)
                dve.wait_ge(logits_done, layer + 1)
                v.tensor_reduce(nmax[:, 0, :], ps[:, 5, :].rearrange("p (h k) -> p h k", h=AH), AX.X, ALU.max)
                step(v.tensor_reduce(nmax[:, 1, :], ps[:, 6:8, :].rearrange("p b (h k) -> p (b h) k", h=2), AX.X, ALU.max))
                v.tensor_scalar(nmax[:, :, :], nmax[:, :, :], -1.0, None, ALU.mult).then_inc(nmax_ready, 1)
                dve.wait_ge(msq_ready, layer * 4 + 4)
                v.tensor_scalar(msq[:, :], msq[:, :], 1.0 / 256, EPS, ALU.mult, ALU.add).then_inc(ms_ready, 1)
                dve.wait_ge(rms_ready, layer + 1)
                step(v.reciprocal(msq[:, :], msq[:, :]))
                for t in range(TT):
                    for g in range(NG):
                        i, c = t * NG + g, slice(g * 256, (g + 1) * 256)
                        ins = v.scalar_tensor_tensor(out=y_tok[:, t, c], in0=y_tok[:, t, c], scalar=msq[:, i:i + 1],
                                                     in1=mix[:, c], op0=ALU.mult, op1=ALU.mult)
                    ins.then_inc(yn_ready, 1)

                def yc_lo(t):
                    dve.wait_ge(ychi_ready, layer * 2 + t + 1)
                    v.tensor_tensor(xt_lo[:, t, 4:8, :].rearrange("p k c -> p (k c)"), ps[:, 4, :],
                                    xt_hi[:, t, 4:8, :].rearrange("p k c -> p (k c)").bitcast(f32),
                                    ALU.subtract).then_inc(yclo_ready, 1)

                yc_lo(0)
                lo_of(layer, U_Q + 3)
                dve.wait_ge(probs_raw, layer + 1)
                step(v.reciprocal(rsum[:, :, :], rsum[:, :, :]))
                p0 = probs[:, 0, :].rearrange("p (h k) -> p h k", h=AH)
                p1 = probs[:, 1:3, :].rearrange("p b (h k) -> p (b h) k", h=2)
                v.tensor_tensor(p0, p0, rsum[:, 0, :].unsqueeze(2).to_broadcast([P, AH, P]), ALU.mult)
                v.tensor_tensor(p1, p1, rsum[:, 1, :].unsqueeze(2).to_broadcast([P, AH, 2 * P]), ALU.mult)\
                    .then_inc(probs_ready, 1)
                yc_lo(1)
                lo_of(layer, U_K + 3)
                lo_of(layer, U_YA + 3)
                dve.wait_ge(ybhi_ready, layer + 1)
                split_lo(2, 2, ps[:, 4, :].rearrange("p (m t c) -> p t m c", m=2, t=TT), yblo_ready)
                norm_and_turn(1, U_YB, U_FFN2)
                ffn(layer, 1, U_FFN2)
                norm_and_turn(2, U_PE - 1, U_PE, 1)
                lo_of(layer, U_PE + 3)
                lo_of(layer, U_GATE + 3)
                dve.wait_ge(gain_in, (layer * 4 + 4) * 16)

                halves = [(half, slice(half * 512, half * 512 + 512)) for half in range(2)]

                def biased(t):
                    for half, c in halves:
                        if t == 1:
                            if half == 0:
                                dve.wait_ge(gate_half, layer + 1)
                            else:
                                done(U_GATE + 3)
                        v.tensor_tensor(x_new[:, t, c], ps[:, 2 * t + half, :], gain[:, 0, c], ALU.add)\
                            .then_inc(biased_ready, 1)

                def gated(t):
                    for half, c in halves:
                        dve.wait_ge(sig_ready, (layer * 2 + t) * 2 + half + 1)
                        step(v.tensor_tensor(x_new[:, t, c], x_new[:, t, c], ps[:, 4 + 2 * t + half, :], ALU.mult))
                        v.tensor_tensor(x_tok[:, t, c], x_tok[:, t, c], x_new[:, t, c], ALU.add)\
                            .then_inc((x_half, x_ready)[half], 1)

                dve.wait_ge(acc_half, layer * 4 + 4)
                biased(0)
                gated(0)
                biased(1)
                gated(1)
                dve.wait_ge(x_ready, layer * 8 + 10)
                v.memset(nmean[:, 0:1], 0.0).then_inc(gain_used, 1)
                assert steps[0] == DVE_STEPS, steps[0]


def lay_out(i):
    import numpy as np
    f = np.float32
    ws = np.zeros((DEPTH, UNITS, P, W), f)

    def tiles(w):
        return w.reshape(w.shape[0] // P, P, w.shape[1]).transpose(1, 0, 2)

    def flat(a):
        return a.reshape(P, -1)

    for l in range(DEPTH):
        for base, name in ((U_FFN1, "ffn1"), (U_FFN2, "ffn2")):
            wg, wu = tiles(i[f"{name}_wg"][l]), tiles(i[f"{name}_wu"][l])
            wd = tiles(i[f"{name}_wd"][l])
            n = base
            for c in range(CHUNKS + 1):
                if c < CHUNKS:
                    cols = slice(c * FC, (c + 1) * FC)
                    for half in range(2):
                        k = slice(4 * half, 4 * half + 4)
                        ws[l, n] = flat(np.stack([wg[:, k, cols], wu[:, k, cols]], axis=2))
                        n += 1
                if c > 0:
                    ws[l, n] = flat(wd[:, 2 * (c - 1):2 * c, :])
                    n += 1
        wi = tiles(i["w_in"][l])
        for n, col in ((U_XS, 1796), (U_XS + 1, 2052), (U_B, 2308), (U_C, 2564), (U_Q, 512), (U_K, 768), (U_V, 1024),
                       (U_U, 0), (U_G, 256)):
            ws[l, n] = flat(wi[:, :, col:col + 256])
        for half in range(2):
            ws[l, U_Z + half] = flat(wi[:, 4 * half:4 * half + 4, 1284:1796])
        for name, units in (("w_out", (U_YA, U_YB, U_YC, U_YC + 1)), ("pe_gate_w", range(U_GATE, U_GATE + 4)),
                            ("pe_proj", (U_PE,))):
            w = tiles(i[name][l])
            for j, n in enumerate(units):
                ws[l, n] = flat(w[:, 2 * j:2 * j + 2, :])

    ex = np.zeros((DEPTH, P, E_ALL), f)
    for l in range(DEPTH):
        ex[l, :, E_CW:E_CW + 32] = i["ssd_conv_w"][l].reshape(32, P).T
        ex[l, :, E_CB:E_CB + 8] = i["ssd_conv_b"][l].reshape(8, P).T
        ex[l, :, E_UW:E_UW + 8] = i["lru_conv_w"][l].reshape(8, P).T
        for at, name in ((E_UB, "lru_conv_b"), (E_BA, "lru_ba"), (E_BX, "lru_bx"), (E_LAM, "lru_lambda")):
            ex[l, :, at:at + 2] = i[name][l].reshape(2, P).T
        ex[l, 0:AH, E_BIAS] = i["fox_bf"][l]
        ex[l, AH:ROWS, E_BIAS] = i["ssd_dt_bias"][l]
        ex[l, 0:AH, E_SIGN] = -1.0
        ex[l, AH:ROWS, E_SIGN] = 1.0
        ex[l, AH:ROWS, E_ALOG] = i["ssd_a_log"][l]
        for at, name in ((E_WA, "lru_wa"), (E_WX, "lru_wx")):
            for h in range(4):
                r, m = h % 2 * HD, h // 2
                ex[l, r:r + HD, at + m * P + r:at + m * P + r + HD] = i[name][l, h]
        wi = tiles(i["w_in"][l])
        fd = ex[l, :, E_FD:E_PT].reshape(P, KT, ROWS)
        ex[l, :, E_FD:E_PT] = flat(np.concatenate([wi[:, :, 1280:1284], wi[:, :, 2820:2828]], axis=2))
        ex[l, :, E_PT:E_ALL] = flat(i["p"][l, 0].T.reshape(PLE // P, P, SEQ).transpose(1, 0, 2))

    norms = np.zeros((DEPTH, 4, 2, D), f)
    for j in range(3):
        norms[:, j, 0] = i[f"ln{j + 1}_g"]
        norms[:, j, 1] = i[f"ln{j + 1}_b"]
    norms[:, 3, 0] = i["pe_gate_b"]
    mix_rows = np.concatenate([i["ssd_norm_g"], i["ssd_d"]], axis=1)

    cst = np.zeros((P, C_ALL), f)
    cst[:, C_ID:C_ID + P] = np.eye(P, dtype=f)
    cst[:, C_SSD:C_SSD + P] = -BIG * np.tril(np.ones((P, P), f), -1)
    cst[:, C_ATT:C_ATT + P] = -BIG * np.triu(np.ones((P, P), f), 1)
    cst[0:ROWS, C_RESET:C_RESET + SEQ] = 1.0
    cst[AH:ROWS, C_RESET + P] = 0.0
    x = i["x"][0].reshape(TT, P, D).transpose(1, 0, 2)
    return {"w_stream": ws, "extras": ex, "norms": norms, "mix_rows": mix_rows, "consts": cst, "x": x}


def kernel(**inputs):
    import numpy as _np
    import concourse.bacc as _bacc
    from concourse import mybir as _mybir
    from concourse.bass_utils import run_bass_kernel_spmd as _run

    nc = _bacc.Bacc("TRN2", target_bir_lowering=False, num_devices=1)
    arrays, args = {}, []
    for name, a in lay_out({k: _np.asarray(v) for k, v in inputs.items()}).items():
        a = _np.ascontiguousarray(a)
        arrays[f"in_{name}_dram"] = a
        args.append(nc.dram_tensor(f"in_{name}_dram", a.shape, _mybir.dt.from_np(a.dtype), kind="ExternalInput").ap())
    args.append(nc.dram_tensor("out_0_dram", (P, TT, D), _mybir.dt.float32, kind="ExternalOutput").ap())
    trunk(nc, *args)
    r = _run(nc, [arrays], core_ids=[0])
    got = r.results[0]["out_0_dram"]
    return got.transpose(1, 0, 2).reshape(1, SEQ, D)
```
